# Optimizing a Trainium2 kernel written in Bass

```python
import functools
import jax
import jax.numpy as jnp
from jax import lax
import numpy as np

D_MODEL = 1024
BATCH = 1
SEQ = 128
DEPTH = 2
DEC_BATCH = 1
DEC_SEQ = 128
PAST_LEN = 128

GRID_W = 64
ROPE_BASE = 10000.0
NORM_EPS = 1e-6
QBLK = 128

GLA_HEADS = 4
GLA_DK = 32
GLA_DV = 64
GLA_GATE_RANK = 16
GLA_GATE_NORM = 16.0
GLA_CHUNK = 64

MLA_HEADS = 4
MLA_Q_RANK = 256
MLA_KV_RANK = 128
MLA_NOPE = 64
MLA_ROPE = 32
MLA_DV = 64

RET_HEADS = 4
RET_DK = 64
RET_DV = 64
RET_CHUNK = 64

GQA_HEADS = 4
GQA_KV_HEADS = 2
GQA_HD = 64
WINDOW = 128
WBLK = 128

MIX_W = GLA_HEADS * GLA_DV + MLA_HEADS * MLA_DV + RET_HEADS * RET_DV + GQA_HEADS * GQA_HD
IN_SPLITS = (
    GLA_HEADS * GLA_DK, GLA_HEADS * GLA_DK, GLA_HEADS * GLA_DV, GLA_HEADS * GLA_DV, GLA_GATE_RANK, GLA_GATE_RANK,
    MLA_Q_RANK, MLA_KV_RANK, MLA_ROPE,
    RET_HEADS * RET_DK, RET_HEADS * RET_DK, RET_HEADS * RET_DV, RET_HEADS * RET_DV,
    GQA_HEADS * GQA_HD, GQA_KV_HEADS * GQA_HD, GQA_KV_HEADS * GQA_HD,
)
IN_WIDTH = sum(IN_SPLITS)

D_FF = 2816
N_EXPERTS = 8
TOP_K = 2
D_FF_EXPERT = 3584
N_DENSE = (DEPTH + 1) // 2
N_MOE = DEPTH // 2

kernel_name = 'hybrid_prefix_diffusion_step'

def rmsnorm(x, g):
    xf = x.astype(jnp.float32)
    y = xf * lax.rsqrt(jnp.mean(xf * xf, axis=-1, keepdims=True) + NORM_EPS)
    return (y * g.astype(jnp.float32)).astype(x.dtype)

def head_rms(x):
    xf = x.astype(jnp.float32)
    return xf * lax.rsqrt(jnp.mean(xf * xf, axis=-1, keepdims=True) + NORM_EPS)

def split_heads(x, n):
    b, t, _ = x.shape
    return x.reshape(b, t, n, -1).transpose(0, 2, 1, 3)

def merge_heads(x):
    b, n, t, d = x.shape
    return x.transpose(0, 2, 1, 3).reshape(b, t, n * d)

def axial_rope(x):
    t, dr = x.shape[-2], x.shape[-1]
    n_rows = t // GRID_W
    rows = jnp.repeat(jnp.arange(n_rows, dtype=jnp.float32), GRID_W)
    cols = (jnp.arange(t) % GRID_W).astype(jnp.float32)
    quarter = dr // 4
    inv = jnp.power(ROPE_BASE, -jnp.arange(quarter, dtype=jnp.float32) / quarter)
    ang = jnp.concatenate([rows[:, None] * inv, cols[:, None] * inv], axis=-1)
    cos, sin = jnp.cos(ang), jnp.sin(ang)
    xf = x.astype(jnp.float32)
    x1, x2 = xf[..., : dr // 2], xf[..., dr // 2:]
    return jnp.concatenate([x1 * cos - x2 * sin, x1 * sin + x2 * cos], axis=-1).astype(x.dtype)

def softmax_with_sink(s, sink):
    if sink is None:
        return jax.nn.softmax(s, axis=-1)
    sk = sink.astype(jnp.float32).reshape((1,) + sink.shape + (1,) * (s.ndim - 3))
    m = jnp.maximum(jnp.max(s, axis=-1, keepdims=True), sk)
    p = jnp.exp(s - m)
    return p / (jnp.sum(p, axis=-1, keepdims=True) + jnp.exp(sk - m))

def dense_attention(q, k, v, sink):
    b, hk, g, tq, d = q.shape
    scale = d ** -0.5
    nq = tq // QBLK
    qb = jnp.moveaxis(q.reshape(b, hk, g, nq, QBLK, d), 3, 0)

    def one_block(q_blk):
        s = jnp.einsum('bkgqd,bktd->bkgqt', q_blk, k, preferred_element_type=jnp.float32) * scale
        p = softmax_with_sink(s, sink).astype(v.dtype)
        return jnp.einsum('bkgqt,bktv->bkgqv', p, v)

    o = lax.map(one_block, qb)
    return jnp.moveaxis(o, 0, 3).reshape(b, hk, g, tq, v.shape[-1])

def window_attention(q, k, v, kc, vc, sink):
    b, hk, g, t, d = q.shape
    scale = d ** -0.5
    nb = t // WBLK
    qb = q.reshape(b, hk, g, nb, WBLK, d)

    def band(x):
        xp = jnp.pad(x, ((0, 0), (0, 0), (WBLK, WBLK), (0, 0))).reshape(b, hk, nb + 2, WBLK, x.shape[-1])
        return jnp.concatenate([xp[:, :, :-2], xp[:, :, 1:-1], xp[:, :, 2:]], axis=3)

    kb, vb = band(k), band(v)
    s_loc = jnp.einsum('bkgnqd,bknjd->bkgnqj', qb, kb, preferred_element_type=jnp.float32) * scale
    qpos = jnp.arange(nb)[:, None, None] * WBLK + jnp.arange(WBLK)[None, :, None]
    kpos = (jnp.arange(nb)[:, None, None] - 1) * WBLK + jnp.arange(3 * WBLK)[None, None, :]
    valid = (jnp.abs(qpos - kpos) <= WINDOW) & (kpos >= 0) & (kpos < t)
    s_loc = jnp.where(valid, s_loc, -jnp.inf)
    s_ctx = jnp.einsum('bkgnqd,bkld->bkgnql', qb, kc, preferred_element_type=jnp.float32) * scale
    p = softmax_with_sink(jnp.concatenate([s_loc, s_ctx], axis=-1), sink).astype(v.dtype)
    o = (jnp.einsum('bkgnqj,bknjv->bkgnqv', p[..., : 3 * WBLK], vb)
         + jnp.einsum('bkgnql,bklv->bkgnqv', p[..., 3 * WBLK:], vc))
    return o.reshape(b, hk, g, t, v.shape[-1])

def chunked_recurrence(q, k, v, log_a, s0, chunk):
    b, h, t, dk = q.shape
    dv = v.shape[-1]
    n = t // chunk
    f32 = jnp.float32
    qc = q.astype(f32).reshape(b, h, n, chunk, dk)
    kc = k.astype(f32).reshape(b, h, n, chunk, dk)
    vc = v.astype(f32).reshape(b, h, n, chunk, dv)
    bc = jnp.cumsum(log_a.astype(f32).reshape(b, h, n, chunk, -1), axis=3)
    b_last = bc[:, :, :, -1:, :]
    causal = jnp.tril(jnp.ones((chunk, chunk), dtype=bool))
    diff = bc[:, :, :, :, None, :] - bc[:, :, :, None, :, :]
    dec = jnp.exp(jnp.where(causal[:, :, None], diff, -jnp.inf))
    if log_a.shape[-1] == 1:
        att = jnp.einsum('bhnid,bhnjd->bhnij', qc, kc) * dec[..., 0]
    else:
        att = jnp.einsum('bhnid,bhnjd,bhnijd->bhnij', qc, kc, dec)
    o_intra = jnp.einsum('bhnij,bhnjv->bhniv', att, vc)
    q_in = qc * jnp.exp(bc)
    kv_chunk = jnp.einsum('bhnjd,bhnjv->bhndv', kc * jnp.exp(b_last - bc), vc)
    a_chunk = jnp.exp(b_last[:, :, :, 0, :])

    def step(s, inp):
        q_n, kv_n, a_n = inp
        o_n = jnp.einsum('bhid,bhdv->bhiv', q_n, s)
        return a_n[..., None] * s + kv_n, o_n

    xs = (jnp.moveaxis(q_in, 2, 0), jnp.moveaxis(kv_chunk, 2, 0), jnp.moveaxis(a_chunk, 2, 0))
    s_t, o_inter = lax.scan(step, s0.astype(f32), xs)
    o = o_intra + jnp.moveaxis(o_inter, 0, 2)
    return o.reshape(b, h, t, dv), s_t

def bidir_recurrence(q, k, v, la_f, la_b, s0_f, s0_b, chunk):
    o_f, s_f = chunked_recurrence(q, k, v, la_f, s0_f, chunk)
    flip = lambda a: jnp.flip(a, axis=2)
    o_b, s_b = chunked_recurrence(flip(q), flip(k), flip(v), flip(la_b), s0_b, chunk)
    return o_f + flip(o_b), s_f, s_b

def mla_keys(ckv, krope, w_kv_up):
    kv = split_heads(ckv @ w_kv_up, MLA_HEADS)
    b, h, t, _ = kv.shape
    k = jnp.concatenate([kv[..., :MLA_NOPE], jnp.broadcast_to(krope[:, None], (b, h, t, MLA_ROPE))], axis=-1)
    return k, kv[..., MLA_NOPE:]

def token_mixer(h, lp, ctx):
    latent = ctx is not None
    b, t, _ = h.shape
    f32 = jnp.float32
    pts = []
    acc = 0
    for s in IN_SPLITS[:-1]:
        acc += s
        pts.append(acc)
    (gq, gk, gv, gog, glr_f, glr_b, mcq, mckv, mkr,
     rq, rk, rv, rg, aq, ak, av) = jnp.split(h @ lp['w_in'], pts, axis=-1)

    la_gla = [split_heads(jax.nn.log_sigmoid((lr @ lp['gla_gate_w'][d] + lp['gla_gate_b'][d]).astype(f32))
                          / GLA_GATE_NORM, GLA_HEADS) for d, lr in enumerate((glr_f, glr_b))]
    s0 = ctx['gla'] if latent else jnp.zeros((b, 2, GLA_HEADS, GLA_DK, GLA_DV), f32)
    o, sg_f, sg_b = bidir_recurrence(split_heads(gq, GLA_HEADS), split_heads(gk, GLA_HEADS) * GLA_DK ** -0.5,
                                     split_heads(gv, GLA_HEADS), la_gla[0], la_gla[1], s0[:, 0], s0[:, 1], GLA_CHUNK)
    o_gla = merge_heads(head_rms(o)).astype(h.dtype) * jax.nn.silu(gog)

    qh = split_heads(rmsnorm(mcq, lp['mla_q_norm_g']) @ lp['mla_w_q_up'], MLA_HEADS)
    q_nope, q_rope = qh[..., :MLA_NOPE], qh[..., MLA_NOPE:]
    ckv = rmsnorm(mckv, lp['mla_kv_norm_g'])
    krope = mkr
    if latent:
        q_rope, krope = axial_rope(q_rope), axial_rope(krope)
    q_m = jnp.concatenate([q_nope, q_rope], axis=-1)
    k_m, v_m = mla_keys(ckv, krope, lp['mla_w_kv_up'])
    if latent:
        k_c, v_c = mla_keys(ctx['ckv'], ctx['krope'], lp['mla_w_kv_up'])
        k_m = jnp.concatenate([k_m, k_c], axis=2)
        v_m = jnp.concatenate([v_m, v_c], axis=2)
    o_mla = merge_heads(dense_attention(q_m[:, :, None], k_m, v_m, None)[:, :, 0])

    rqh, rkh = split_heads(rq, RET_HEADS), split_heads(rk, RET_HEADS)
    if latent:
        rqh, rkh = axial_rope(rqh), axial_rope(rkh)
    lg = jax.nn.log_sigmoid(lp['ret_decay'].astype(f32))
    la_ret = [jnp.broadcast_to(lg[d][None, :, None, None], (b, RET_HEADS, t, 1)) for d in range(2)]
    s0 = ctx['ret'] if latent else jnp.zeros((b, 2, RET_HEADS, RET_DK, RET_DV), f32)
    o, sr_f, sr_b = bidir_recurrence(rqh, rkh * RET_DK ** -0.5, split_heads(rv, RET_HEADS),
                                     la_ret[0], la_ret[1], s0[:, 0], s0[:, 1], RET_CHUNK)
    o_ret = merge_heads(head_rms(o)).astype(h.dtype) * jax.nn.silu(rg)

    qa, ka, va = split_heads(aq, GQA_HEADS), split_heads(ak, GQA_KV_HEADS), split_heads(av, GQA_KV_HEADS)
    if latent:
        qa, ka = axial_rope(qa), axial_rope(ka)
    grp = GQA_HEADS // GQA_KV_HEADS
    qa = qa.reshape(b, GQA_KV_HEADS, grp, t, GQA_HD)
    sink = lp['gqa_sink'].reshape(GQA_KV_HEADS, grp)
    if latent:
        o = window_attention(qa, ka, va, ctx['gk'], ctx['gv'], sink)
    else:
        o = dense_attention(qa, ka, va, sink)
    o_gqa = merge_heads(o.reshape(b, GQA_HEADS, t, GQA_HD))

    out = jnp.concatenate([o_gla, o_mla, o_ret, o_gqa], axis=-1) @ lp['w_out']
    if latent:
        return out, None
    new_ctx = {'gla': jnp.stack([sg_f, sg_b], axis=1), 'ret': jnp.stack([sr_f, sr_b], axis=1),
               'ckv': ckv, 'krope': krope, 'gk': ka, 'gv': va}
    return out, new_ctx

def swiglu(h, wg, wu, wd):
    return (jax.nn.silu(h @ wg) * (h @ wu)) @ wd

def moe_swiglu(h, router, wg, wu, wd):
    logits = (h @ router).astype(jnp.float32)
    top_v, top_i = lax.top_k(logits, TOP_K)
    w = jax.nn.softmax(top_v, axis=-1)
    gate = jnp.sum(jax.nn.one_hot(top_i, N_EXPERTS, dtype=jnp.float32) * w[..., None], axis=-2).astype(h.dtype)
    y = jnp.zeros_like(h)
    for e in range(N_EXPERTS):
        y = y + gate[..., e:e + 1] * swiglu(h, wg[e], wu[e], wd[e])
    return y

def modulation(cond, w_mod, b_mod):
    m = (jax.nn.silu(cond) @ w_mod + b_mod).reshape(-1, 1, 6 * D_MODEL)
    return jnp.split(m, 6, axis=-1)

def trunk_layer(x, mod, g1, g2, lp, ffn, ctx):
    sh1, sc1, gt1, sh2, sc2, gt2 = mod
    mix, new_ctx = token_mixer(rmsnorm(x, g1) * (1 + sc1) + sh1, lp, ctx)
    x = x + gt1 * mix
    x = x + gt2 * ffn(rmsnorm(x, g2) * (1 + sc2) + sh2)
    return x, new_ctx

def setup_inputs(seed: int = 0) -> dict:
    key = jax.random.key(seed)
    keys = iter(jax.random.split(key, 48))
    f32 = jnp.float32
    D = D_MODEL

    def nrm(shape, scale=1.0):
        return jax.random.normal(next(keys), shape, f32) * scale

    def gain(shape):
        return 1.0 + nrm(shape, 0.02)

    ret_base = jnp.log(jnp.exp2(5.0 + jnp.arange(RET_HEADS, dtype=f32)) - 1.0)
    return {
        'x_prompt': nrm((BATCH, SEQ, D)),
        'x_sample': nrm((DEC_BATCH, DEC_SEQ, D)),
        'state_gla': nrm((DEC_BATCH, DEPTH, 2, GLA_HEADS, GLA_DK, GLA_DV), 0.5),
        'state_ret': nrm((DEC_BATCH, DEPTH, 2, RET_HEADS, RET_DK, RET_DV), 0.5),
        'cache_mla_ckv': nrm((DEC_BATCH, DEPTH, PAST_LEN, MLA_KV_RANK)),
        'cache_mla_krope': nrm((DEC_BATCH, DEPTH, PAST_LEN, MLA_ROPE)),
        'cache_gqa_k': nrm((DEC_BATCH, DEPTH, GQA_KV_HEADS, PAST_LEN, GQA_HD)),
        'cache_gqa_v': nrm((DEC_BATCH, DEPTH, GQA_KV_HEADS, PAST_LEN, GQA_HD)),
        'c': nrm((DEC_BATCH, D)),
        'c_ctx': nrm((D,)),
        'norm1_g': gain((DEPTH, D)),
        'norm2_g': gain((DEPTH, D)),
        'final_norm_g': gain((D,)),
        'w_mod': nrm((DEPTH, D, 6 * D), 0.5 * D ** -0.5),
        'b_mod': nrm((DEPTH, 6 * D), 0.01),
        'w_in': nrm((DEPTH, D, IN_WIDTH), D ** -0.5),
        'w_out': nrm((DEPTH, MIX_W, D), MIX_W ** -0.5),
        'gla_gate_w': nrm((DEPTH, 2, GLA_GATE_RANK, GLA_HEADS * GLA_DK), GLA_GATE_RANK ** -0.5),
        'gla_gate_b': nrm((DEPTH, 2, GLA_HEADS * GLA_DK), 0.1),
        'mla_q_norm_g': gain((DEPTH, MLA_Q_RANK)),
        'mla_w_q_up': nrm((DEPTH, MLA_Q_RANK, MLA_HEADS * (MLA_NOPE + MLA_ROPE)), MLA_Q_RANK ** -0.5),
        'mla_kv_norm_g': gain((DEPTH, MLA_KV_RANK)),
        'mla_w_kv_up': nrm((DEPTH, MLA_KV_RANK, MLA_HEADS * (MLA_NOPE + MLA_DV)), MLA_KV_RANK ** -0.5),
        'ret_decay': ret_base + nrm((DEPTH, 2, RET_HEADS), 0.1),
        'gqa_sink': nrm((DEPTH, GQA_HEADS), 0.5),
        'ffn_w_gate': nrm((N_DENSE, D, D_FF), D ** -0.5),
        'ffn_w_up': nrm((N_DENSE, D, D_FF), D ** -0.5),
        'ffn_w_down': nrm((N_DENSE, D_FF, D), D_FF ** -0.5),
        'moe_router': nrm((N_MOE, D, N_EXPERTS), D ** -0.5),
        'moe_w_gate': nrm((N_MOE, N_EXPERTS, D, D_FF_EXPERT), D ** -0.5),
        'moe_w_up': nrm((N_MOE, N_EXPERTS, D, D_FF_EXPERT), D ** -0.5),
        'moe_w_down': nrm((N_MOE, N_EXPERTS, D_FF_EXPERT, D), D_FF_EXPERT ** -0.5),
    }

def reference(x_prompt, x_sample, state_gla, state_ret, cache_mla_ckv, cache_mla_krope, cache_gqa_k, cache_gqa_v,
              c, c_ctx, norm1_g, norm2_g, final_norm_g, w_mod, b_mod, w_in, w_out, gla_gate_w, gla_gate_b,
              mla_q_norm_g, mla_w_q_up, mla_kv_norm_g, mla_w_kv_up, ret_decay, gqa_sink,
              ffn_w_gate, ffn_w_up, ffn_w_down, moe_router, moe_w_gate, moe_w_up, moe_w_down):
    xp, xs = x_prompt, x_sample
    gla_l, ret_l, ckv_l, kr_l, gk_l, gv_l = [], [], [], [], [], []
    for l in range(DEPTH):
        lp = {'w_in': w_in[l], 'w_out': w_out[l], 'gla_gate_w': gla_gate_w[l], 'gla_gate_b': gla_gate_b[l],
              'mla_q_norm_g': mla_q_norm_g[l], 'mla_w_q_up': mla_w_q_up[l], 'mla_kv_norm_g': mla_kv_norm_g[l],
              'mla_w_kv_up': mla_w_kv_up[l], 'ret_decay': ret_decay[l], 'gqa_sink': gqa_sink[l]}
        j = l // 2
        if l % 2 == 0:
            ffn = functools.partial(swiglu, wg=ffn_w_gate[j], wu=ffn_w_up[j], wd=ffn_w_down[j])
        else:
            ffn = functools.partial(moe_swiglu, router=moe_router[j], wg=moe_w_gate[j], wu=moe_w_up[j],
                                    wd=moe_w_down[j])
        xp, ctx = trunk_layer(xp, modulation(c_ctx, w_mod[l], b_mod[l]), norm1_g[l], norm2_g[l], lp, ffn, None)
        gla_l.append(ctx['gla'].astype(x_prompt.dtype))
        ret_l.append(ctx['ret'].astype(x_prompt.dtype))
        ckv_l.append(ctx['ckv'])
        kr_l.append(ctx['krope'])
        gk_l.append(ctx['gk'])
        gv_l.append(ctx['gv'])
        cache = {'gla': state_gla[:, l], 'ret': state_ret[:, l], 'ckv': cache_mla_ckv[:, l],
                 'krope': cache_mla_krope[:, l], 'gk': cache_gqa_k[:, l], 'gv': cache_gqa_v[:, l]}
        xs, _ = trunk_layer(xs, modulation(c, w_mod[l], b_mod[l]), norm1_g[l], norm2_g[l], lp, ffn, cache)
    y_prompt = rmsnorm(xp, final_norm_g)
    y_sample = rmsnorm(xs, final_norm_g)
    new_state_gla = jnp.stack(gla_l, axis=1)
    new_state_ret = jnp.stack(ret_l, axis=1)
    new_cache_mla_ckv = jnp.stack(ckv_l, axis=1)
    new_cache_mla_krope = jnp.stack(kr_l, axis=1)
    new_cache_gqa_k = jnp.stack(gk_l, axis=1)
    new_cache_gqa_v = jnp.stack(gv_l, axis=1)
    return (y_prompt, y_sample, new_state_gla, new_state_ret, new_cache_mla_ckv, new_cache_mla_krope,
            new_cache_gqa_k, new_cache_gqa_v)


_drawn_inputs = setup_inputs


def setup_inputs(seed=0):
    import zlib

    import numpy as np

    out = dict(_drawn_inputs(seed))
    spreads = {}
    factors = {'cache_mla_ckv': 2.941,
     'cache_mla_krope': 3.61,
     'cache_gqa_k': 3.265,
     'cache_gqa_v': 3.22,
     'norm2_g': 3.79,
     'final_norm_g': 8.271,
     'mla_q_norm_g': 6.403,
     'mla_kv_norm_g': 2.886,
     'gqa_sink': 64.0}
    for name, (base, spread) in spreads.items():
        noise = np.random.default_rng([zlib.crc32(name.encode()), seed]).standard_normal(out[name].shape)
        drawn = base * np.exp(spread * noise) if base else spread * noise
        out[name] = jnp.asarray(drawn.astype(out[name].dtype))
    for name, factor in factors.items():
        out[name] = (out[name] * factor).astype(out[name].dtype)
    return out
```

```python
from contextlib import ExitStack

import numpy as np

import concourse.bass as bass
from concourse import mybir

F32 = mybir.dt.float32
U32 = mybir.dt.uint32
I32 = mybir.dt.int32
ALU = mybir.AluOpType
ACT = mybir.ActivationFunctionType
AX = mybir.AxisListType.X

P = 128
NS = 2
EPS = 1e-6
GRID_W, ROPE_BASE = 64, 10000.0
GLA_GATE_NORM = 16.0
LEVELS = 7

WIDTHS = [("gq", 128), ("gk", 128), ("gv", 256), ("gog", 256), ("glr", 32), ("mcq", 256), ("mckv", 128),
          ("mkr", 32), ("rq", 256), ("rk", 256), ("rv", 256), ("rg", 256), ("aq", 256), ("ak", 128), ("av", 128)]
COL = {}
_at = 0
for _name, _w in WIDTHS:
    COL[_name] = (_at, _at + _w)
    _at += _w
IN_WIDTH = _at

CONSTS = [("ident", P), ("scan", 4 * P), ("dist", 2 * P), ("pos", 4), ("cos64", 32), ("sin64", 32), ("cos32", 16),
          ("sin32", 16), ("iota", P), ("masks", LEVELS * P), ("sum_qf", LEVELS * P), ("sum_qb", LEVELS * P),
          ("sum_kf", LEVELS * P), ("sum_kb", LEVELS * P)]
CCOL = {}
_at = 0
for _name, _w in CONSTS:
    CCOL[_name] = (_at, _at + _w)
    _at += _w
N_CONST = _at

PAGE = 2048
SLOTS = 9
FF = 2
MOE_SLOTS = 14
TILES = 3
CAP = 32 * TILES


def constant_table():
    t = np.arange(P)
    out = np.zeros((P, N_CONST), np.float32)

    def put(name, a):
        lo, hi = CCOL[name]
        out[:, lo:hi] = np.asarray(a, np.float32).reshape(P, hi - lo)

    put("ident", np.eye(P))
    masks, sums = [], {"sum_qf": [], "sum_qb": [], "sum_kf": [], "sum_kb": []}
    u, i = t[:, None], t[None, :]
    for level in range(LEVELS):
        half = 64 >> level
        block = t // (2 * half)
        second = (t % (2 * half)) >= half
        masks.append((block[:, None] == block[None, :]) & (second[:, None] != second[None, :]))
        m, s2 = (block * 2 * half + half)[None, :], second[None, :]
        sums["sum_qf"].append(s2 & (u >= m) & (u <= i))
        sums["sum_qb"].append(~s2 & (u >= i) & (u < m))
        sums["sum_kf"].append(~s2 & (u > i) & (u < m))
        sums["sum_kb"].append(s2 & (u >= m) & (u < i))
    put("masks", np.stack(masks, 1))
    for name, a in sums.items():
        put(name, np.stack(a, 1) / GLA_GATE_NORM)
    put("scan", np.stack([u > i, u < i, u <= i, u >= i], 1) / GLA_GATE_NORM)
    put("dist", np.stack([np.maximum(i - u, 0), np.maximum(u - i, 0)], 1))
    put("pos", np.stack([P - 1 - t, t, t + 1, P - t], 1))
    rows, cols = (t // GRID_W).astype(np.float32), (t % GRID_W).astype(np.float32)
    for d in (64, 32):
        quarter = d // 4
        inv = np.power(np.float32(ROPE_BASE), -np.arange(quarter, dtype=np.float32) / np.float32(quarter))
        ang = np.concatenate([rows[:, None] * inv, cols[:, None] * inv], axis=1).astype(np.float32)
        put(f"cos{d}", np.cos(ang))
        put(f"sin{d}", np.sin(ang))
    put("iota", np.tile(t, (P, 1)))
    return out


def hybrid_step(nc, io):
    D = io["x_prompt"].shape[-1]
    L = io["w_in"].shape[0]
    KT = D // P
    D_FF = io["ffn_w_gate"].shape[-1]
    E, D_FFE = io["moe_w_gate"].shape[1], io["moe_w_gate"].shape[-1]
    H = 4
    HALF = D // 2
    IN_PAGES = -(-IN_WIDTH // 256)
    DENSE_UNITS = D_FF // (FF * P)
    SPILL_UNITS = D_FFE // (FF * P)
    DENSE_BLOCKS, SPILL_BLOCKS = DENSE_UNITS * FF, SPILL_UNITS * FF
    UNITS = D_FFE // 512
    MOE_PAGES = 6 * UNITS
    MOE_TILES = UNITS * TILES
    assert MOE_PAGES % MOE_SLOTS == 0 and MOE_TILES % 3 == 0

    pages = []
    for layer in range(L):
        for third in range(3):
            pages.append(("mod_bias", layer, third, 0))
            pages += [("mod", layer, third, kt) for kt in range(KT)]
        pages += [("w_in", layer, c, 0) for c in range(IN_PAGES)]
        pages += [("w_out", layer, c, 0) for c in range(KT // 2)]
        if layer % 2 == 0:
            for u in range(DENSE_UNITS):
                pages += [("gate", layer, u, 0), ("up", layer, u, 0), ("down", layer, u, 0)]
    n_pages = len(pages)
    page_at = {key: n for n, key in enumerate(pages)}
    loads_before_moe = [len(range(s, n_pages, SLOTS)) if s < SLOTS else 0 for s in range(MOE_SLOTS)]
    LOADS = MOE_PAGES // MOE_SLOTS

    with ExitStack() as ctx:
        def sb(name, shape, dt=F32):
            return ctx.enter_context(nc.sbuf_tensor(name, shape, dt))

        def sem(name):
            return ctx.enter_context(nc.semaphore(name))

        arena = sb("arena", [P, SLOTS * PAGE + N_CONST + NS * IN_WIDTH + 2 * NS * D])
        at_const = SLOTS * PAGE
        at_proj = at_const + N_CONST
        at_gates = at_proj + NS * IN_WIDTH
        ring = arena[:, 0:at_const].rearrange("p (s n) -> p s n", s=SLOTS)
        const = arena[:, at_const:at_proj]
        proj = arena[:, at_proj:at_gates].rearrange("p (s n) -> p s n", s=NS)
        gates = arena[:, at_gates:].rearrange("p (g s n) -> p g s n", g=2, s=NS)
        at_tables = at_const + CCOL["masks"][0]
        moe_at = [PAGE * k for k in range(SLOTS)] + [at_tables, at_tables + PAGE, at_proj, at_proj + PAGE, at_gates]
        assert len(moe_at) == MOE_SLOTS and 2 * PAGE <= N_CONST - CCOL["masks"][0] and 2 * PAGE + D <= NS * IN_WIDTH
        final_g = arena[:, at_proj + 2 * PAGE:at_proj + 2 * PAGE + D]
        x = sb("x", [P, NS, D])
        hT = sb("hT", [P, KT, NS * P])
        row = sb("row", [P, NS, D])
        mixed = sb("mixed", [P, D])
        scratch = sb("scratch", [P, 5504])
        mod_T = sb("mod_T", [P, 4, KT, NS])
        scale_A = sb("scale_A", [P, 2, KT, NS])
        cond = sb("cond", [P, NS, KT])
        cond_raw = sb("cond_raw", [P, NS, KT])
        ones2 = sb("ones2", [1, 2])
        pick = sb("pick", [P, NS, P])
        stat = sb("stat", [P, 64])
        half_neg = sb("half_neg", [P, 4])
        gT = sb("gT", [P, 2, KT])
        q_g = sb("q_g", [P, 2])
        kv_g = sb("kv_g", [P, P])
        w_q_up = sb("w_q_up", [P, 2, 384])
        w_kv_up = sb("w_kv_up", [P, 512])
        w_lr = sb("w_lr", [33, 256])
        lrT = sb("lrT", [33, P])
        decay = sb("decay", [P, 2 * H])
        lg = sb("lg", [P, 2 * H])
        lg_abs = sb("lg_abs", [P, 2 * H])
        ret_pow = sb("ret_pow", [P, 4, H])
        ret_D = sb("ret_D", [P, H, P])
        sink = sb("sink", [P, H])
        ctx_ckv = sb("ctx_ckv", [P, P])
        ctx_kr = sb("ctx_kr", [P, 32])
        ctx_k = sb("ctx_k", [P, 2, 64])
        ctx_v = sb("ctx_v", [P, 2, 64])
        s0_gla = sb("s0_gla", [P, 2, 256])
        s0_ret = sb("s0_ret", [64, 2, H, 64])
        router = sb("router", [P, KT, E])
        moe_w = sb("moe_w", [P, NS, E + 1])
        moe_m = sb("moe_m", [P, NS, E + 1])
        moe_pos = sb("moe_pos", [P, NS, E + 1])
        moe_spill = sb("moe_spill", [P, NS, E])
        moe_count = sb("moe_count", [1, E], I32)
        route_i = sb("route_i", [P, NS, 8], U32)
        ps = ctx.enter_context(nc.psum_tensor("ps", [P, 8, 512], F32))

        def take(at, *shape):
            n = int(np.prod(shape))
            v = scratch[:, at:at + n]
            if len(shape) == 2:
                v = v.rearrange("p (a b) -> p a b", a=shape[0])
            if len(shape) == 3:
                v = v.rearrange("p (a b c) -> p a b c", a=shape[0], b=shape[1])
            return v

        g_x = take(0, 16, P)
        g_d = take(2048, 2, P)
        g_qT, g_kT = take(2304, 4, P), take(2816, 4, P)
        g_sT = take(3328, 2, P)
        g_att = take(3584, H, P)
        g_la = take(4608, 256)
        g_abs = take(4864, 256)
        r_qT, r_kT, r_att = take(0, H, P), take(512, H, P), take(1024, H, P)
        r_kd = take(1536, 2, 256)
        o_sum = take(2560, 256)
        o_tmp = take(2816, 256)
        o_sq = take(3072, 256)
        o_gate = take(3328, 256)
        rope_t = [row[:, 0, 256 * k:256 * k + 256] for k in range(4)]
        mod_row = row[:, 0, 0:512]
        g_st = row[:, 1, 0:512].rearrange("p (d n) -> p d n", d=2)
        r_st = row[:, 1, 512:1024].rearrange("p (a n) -> p a n", a=2 * H)
        a_q, a_k, a_v = take(0, H, 96), take(384, 2, H, 96), take(1152, 2, H, 64)
        a_qT, a_kT = take(1664, H, P), take(2176, 2, H, P)
        a_p, a_pT = take(3200, H, 256), take(4224, 2, H, P)
        m_q, m_ckv = take(4224, 256), take(5376, P)
        m_qT = take(4608, 4, P)
        f_sg, f_hid = take(0, 2, 256), take(512, 4, 256)
        t_logit, t_top, t_idx = take(4096, NS, 8), take(4112, NS, 8), take(4128, NS, 8)
        t_w, t_count = take(4144, NS, 8), take(4160, 8)
        f_y = take(0, NS, D)
        e_h = take(2048, KT, CAP)
        e_sg = take(2048 + KT * CAP, 3, P)
        e_hid = take(2048 + KT * CAP + 384, 2, TILES, P)
        e_hidT = take(2048 + KT * CAP + 384 + 768, 4, CAP)
        e_y = take(2048 + KT * CAP + 384 + 768 + 384, D)
        sel = mixed[:, 0:NS * P].rearrange("p (s n) -> p s n", s=NS)[:, :, 0:CAP]
        sel_w = mixed[:, 256:256 + NS * P].rearrange("p (s n) -> p s n", s=NS)[:, :, 0:CAP]
        sel_wT = mixed[:, 512:512 + NS * P].rearrange("p (s n) -> p s n", s=NS)
        s_sg, s_hid = e_h.rearrange("p k n -> p (k n)")[:, 0:256], e_hid.rearrange("p a b c -> p (a b c)")[:, 0:256]

        def c(name):
            lo, hi = CCOL[name]
            return const[:, lo:hi]

        def pj(s, name):
            lo, hi = COL[name]
            return proj[:, s, lo:hi]

        def heads(v, n):
            return v.rearrange("p (h d) -> p h d", h=n)

        ident = c("ident")
        masks = c("masks").rearrange("p (l t) -> p l t", l=LEVELS)
        sum_qf, sum_qb, sum_kf, sum_kb = (c(f"sum_{k}").rearrange("p (l t) -> p l t", l=LEVELS)
                                          for k in ("qf", "qb", "kf", "kb"))
        scan = c("scan").rearrange("p (l t) -> p l t", l=4)
        dist = c("dist").rearrange("p (l t) -> p l t", l=2)

        def last(v, n):
            return v.unsqueeze(2).to_broadcast([v.shape[0], v.shape[1], n])

        def mid(v, n):
            return v.unsqueeze(1).to_broadcast([v.shape[0], n, v.shape[1]])

        loaded = [sem(f"page_loaded_{i}") for i in range(MOE_SLOTS)]
        const_in, x_in, params_in, final_g_in = sem("const_in"), sem("x_in"), sem("params_in"), sem("final_g_in")
        const_set = sem("const_set")
        cond_ready = sem("cond_ready")
        mod_bias_used, mod_used, w_in_used, w_out_used = (sem("mod_bias_used"), sem("mod_used"), sem("w_in_used"),
                                                          sem("w_out_used"))
        mod_rows_act, mod_rows_dve, mod_turned, mod_kept = (sem("mod_rows_act"), sem("mod_rows_dve"), sem("mod_turned"),
                                                            sem("mod_kept"))
        ret_lg_abs, ret_exp, ret_lg, ret_dist, ret_ready = (sem("ret_lg_abs"), sem("ret_exp"), sem("ret_lg"), sem("ret_dist"),
                                                   sem("ret_ready"))
        ret_D_ready = sem("ret_D_ready")
        sq_ready, var_ready, rstd_ready, xn_ready, xT_done, h_ready, h_ready_act = (
            sem("sq_ready"), sem("var_ready"), sem("rstd_ready"), sem("xn_ready"), sem("xT_done"), sem("h_ready"),
            sem("h_ready_act"))
        proj_done, proj_act, proj_dve = sem("proj_done"), sem("proj_act"), sem("proj_dve")
        roped = sem("roped")
        lr_turned, lr_kept, lr_done, lr_abs, lr_soft, la_ready = (sem("lr_turned"), sem("lr_kept"), sem("lr_done"),
                                                                  sem("lr_abs"), sem("lr_soft"), sem("la_ready"))
        sums_done, decays_ready, decayed = sem("sums_done"), sem("decays_ready"), sem("decayed")
        g_turned, g_q_kept, g_k_kept, g_att_done, g_att_kept = (sem("g_turned"), sem("g_q_kept"), sem("g_k_kept"),
                                                                sem("g_att_done"), sem("g_att_kept"))
        ext_turned, ext_kept = sem("ext_turned"), sem("ext_kept")
        g_out_done, g_state_kept = sem("g_out_done"), sem("g_state_kept")
        o_kept, o_sq_ready, o_gate_exp, o_var, o_rstd, o_mixed = (sem("o_kept"), sem("o_sq_ready"), sem("o_gate_exp"),
                                                                  sem("o_var"), sem("o_rstd"), sem("o_mixed"))
        r_turned, r_q_kept, r_k_kept, r_scores, r_att_kept, r_out_done, r_state_kept = (
            sem("r_turned"), sem("r_q_kept"), sem("r_k_kept"), sem("r_scores"), sem("r_att_kept"), sem("r_out_done"),
            sem("r_state_kept"))
        m_sq, m_var, m_rstd, m_normed, m_turned, m_kept, m_up_done, m_q_kept, m_k_kept = (
            sem("m_sq"), sem("m_var"), sem("m_rstd"), sem("m_normed"), sem("m_turned"), sem("m_kept"),
            sem("m_up_done"), sem("m_q_kept"), sem("m_k_kept"))
        a_turned, a_q_kept, a_k_kept, a_scores, a_shift, a_probs, a_p_turned, a_p0_kept, a_p1_kept, a_out, a_mixed = (
            sem("a_turned"), sem("a_q_kept"), sem("a_k_kept"), sem("a_scores"), sem("a_shift"), sem("a_probs"),
            sem("a_p_turned"), sem("a_p0_kept"), sem("a_p1_kept"), sem("a_out"), sem("a_mixed"))
        mix_turned, mix_kept, mix_kept_act, x_mixed = sem("mix_turned"), sem("mix_kept"), sem("mix_kept_act"), sem("x_mixed")
        logits_done, route_top, route_exp, route_ready = (sem("logits_done"), sem("route_top"), sem("route_exp"),
                                                          sem("route_ready"))
        gu_done, silu_ready, hid_ready, down_done, y_kept = (sem("gu_done"), sem("silu_ready"), sem("hid_ready"),
                                                             sem("down_done"), sem("y_kept"))
        h_back, h_rows_act, h_rows_dve, places_done = (sem("h_back"), sem("h_rows_act"), sem("h_rows_dve"),
                                                       sem("places_done"))
        sel_ready, sel_w_ready, sel_w_turned, sel_wT_ready, gather_done, gathered_act, gathered_dve = (
            sem("sel_ready"), sem("sel_w_ready"), sem("sel_w_turned"), sem("sel_wT_ready"), sem("gather_done"),
            sem("gathered_act"), sem("gathered_dve"))
        hid_turned, hidT_ready, y_copied_act, y_copied_dve, scatter_done, y_added = (
            sem("hid_turned"), sem("hidT_ready"), sem("y_copied_act"), sem("y_copied_dve"), sem("scatter_done"),
            sem("y_added"))
        spill_loaded = [sem("spill_loaded_0"), sem("spill_loaded_1")]
        spill_gu, spill_silu, spill_hid, spill_down, spill_y = (sem("spill_gu"), sem("spill_silu"), sem("spill_hid"),
                                                                sem("spill_down"), sem("spill_y"))
        stored = sem("stored")
        final_ready, finished = sem("final_ready"), sem("finished")
        dve_step, act_step, pool_step = sem("dve_step"), sem("act_step"), sem("pool_step")
        stores_per_layer = 2 * H + 1 + 4
        N_PARAMS = 15 + 2 * H + 1

        def slot_of(key):
            return page_at[key] % SLOTS

        def page(key):
            return ring[:, slot_of(key), :]

        def wait_page(eng, key):
            n = page_at[key]
            eng.wait_ge(loaded[n % SLOTS], 16 * (n // SLOTS + 1))

        block = ctx.enter_context(nc.Block())

        @block.sync
        def _(sp):
            def source(key):
                kind, layer, i, kt = key
                if kind == "mod_bias":
                    return io["b_mod"][layer:layer + 1, i * PAGE:(i + 1) * PAGE]
                if kind == "mod":
                    return io["w_mod"][layer, kt * P:(kt + 1) * P, i * PAGE:(i + 1) * PAGE]
                if kind == "w_in":
                    w = min(256, IN_WIDTH - 256 * i)
                    return io["w_in"][layer].rearrange("(k p) n -> p k n", p=P)[:, :, 256 * i:256 * i + w]
                if kind == "w_out":
                    return io["w_out"][layer].rearrange("(k p) n -> p k n", p=P)[:, 2 * i:2 * i + 2, :]
                if kind == "down":
                    return io["ffn_w_down"][layer // 2].rearrange("(b p) n -> p b n", p=P)[:, FF * i:FF * i + FF, :]
                w = io["ffn_w_gate" if kind == "gate" else "ffn_w_up"]
                return w[layer // 2].rearrange("(k p) n -> p k n", p=P)[:, :, 256 * i:256 * i + 256]

            def target(key):
                kind, _, i, _ = key
                if kind == "mod_bias":
                    return page(key)[0:1, :]
                if kind == "mod":
                    return page(key)
                if kind in ("w_out", "down"):
                    return page(key).rearrange("p (b n) -> p b n", b=2)
                w = min(256, IN_WIDTH - 256 * i) if kind == "w_in" else 256
                return page(key).rearrange("p (k n) -> p k n", k=KT)[:, :, 0:w]

            def wait_used(key):
                kind, layer, i, kt = key
                if kind == "mod_bias":
                    sp.wait_ge(mod_bias_used, 3 * layer + i + 1)
                elif kind == "mod":
                    sp.wait_ge(mod_used, KT * (3 * layer + i) + kt + 1)
                elif kind == "w_in":
                    sp.wait_ge(w_in_used, IN_PAGES * layer + i + 1)
                elif kind == "w_out":
                    sp.wait_ge(w_out_used, (KT // 2) * layer + i + 1)
                elif kind == "down":
                    sp.wait_ge(down_done, FF * (i + 1))
                else:
                    sp.wait_ge(gu_done, FF * (i + 1))

            for n, key in enumerate(pages):
                if n >= SLOTS:
                    wait_used(pages[n - SLOTS])
                sp.dma_start(target(key), source(key)).then_inc(loaded[n % SLOTS], 16)

            gate_v = io["moe_w_gate"][0].rearrange("e (k p) n -> e p k n", p=P)
            up_v = io["moe_w_up"][0].rearrange("e (k p) n -> e p k n", p=P)
            down_v = io["moe_w_down"][0].rearrange("e (b p) n -> e p b n", p=P)

            def expert_source(e, kind, i):
                if kind == "down":
                    return down_v[bass.ds(e, 1), :, FF * i:FF * i + FF, :].rearrange("e p b n -> p (e b) n")
                w = gate_v if kind == "gate" else up_v
                return w[bass.ds(e, 1), :, :, 256 * i:256 * i + 256].rearrange("e p k n -> p (e k) n")

            def load_expert_page(e, j):
                u, k = j // 6, j % 6
                kind, i = (("gate", "up", "gate", "up", "down", "down")[k], 2 * u + (0, 0, 1, 1, 0, 1)[k])
                at = moe_at[j % MOE_SLOTS]
                dst = arena[:, at:at + PAGE].rearrange("p (b n) -> p b n", b=2 if kind == "down" else KT)
                sp.dma_start(dst, expert_source(e, kind, i)).then_inc(loaded[j % MOE_SLOTS], 16)

            def wait_expert_page_used(e, j):
                u = j // 6
                if j % 6 >= 4:
                    sp.wait_ge(down_done, e * UNITS + (DENSE_BLOCKS + u + 1))
                else:
                    sp.wait_ge(gu_done, e * MOE_TILES + (DENSE_BLOCKS + TILES * (u + 1)))

            for j in range(MOE_SLOTS):
                if j < SLOTS:
                    wait_used([pages[n] for n in range(j, n_pages, SLOTS)][-1])
                elif j == SLOTS:
                    sp.wait_ge(x_mixed, 2 * L - 1)
                load_expert_page(0, j)
            with sp.Fori(0, E - 1) as e:
                for j in range(MOE_SLOTS, MOE_PAGES):
                    wait_expert_page_used(e, j - MOE_SLOTS)
                    load_expert_page(e, j)
                for j in range(MOE_SLOTS):
                    wait_expert_page_used(e, MOE_PAGES - MOE_SLOTS + j)
                    load_expert_page(e + 1, j)
            for j in range(MOE_SLOTS, MOE_PAGES):
                wait_expert_page_used(E - 1, j - MOE_SLOTS)
                load_expert_page(E - 1, j)
            sp.wait_ge(gu_done, DENSE_BLOCKS + E * MOE_TILES)
            sp.wait_ge(down_done, DENSE_BLOCKS + E * UNITS)
            sp.wait_ge(y_added, 2 * E + 3)
            with sp.Fori(0, E) as e:
                count = sp.value_load(moe_count[0:1, bass.ds(e, 1)], min_val=0, max_val=NS * P)
                with sp.If(count > CAP):
                    for u in range(SPILL_UNITS):
                        sp.wait_ge(spill_down, e * SPILL_BLOCKS + max(1, 1 + FF * (u - 1)))
                        for k, kind in enumerate(("gate", "up", "down")):
                            at = PAGE * (3 * (u % 2) + k)
                            dst = arena[:, at:at + PAGE].rearrange("p (b n) -> p b n", b=2 if kind == "down" else KT)
                            sp.dma_start(dst, expert_source(e, kind, u)).then_inc(spill_loaded[u % 2], 16)
                with sp.Else():
                    sp.wait_ge(spill_down, e * SPILL_BLOCKS + 1)
                    for half in range(2):
                        sp.sem_inc(spill_loaded[half], 16 * 3 * SPILL_UNITS // 2)
            for s, name in enumerate(("y_prompt", "y_sample")):
                sp.wait_ge(final_ready, s + 1)
                sp.dma_start(io[name][0], row[:, s, :]).then_inc(finished, 16)
            sp.wait_ge(finished, 32)

        @block.gpsimd
        def _(pool):
            g = nc.gpsimd
            steps = [0]

            def link(ins):
                steps[0] += 1
                ins.then_inc(pool_step, 1)
                pool.wait_ge(pool_step, steps[0])

            pool.dma_start(const[:], io["constants"]).then_inc(const_in, 16)
            with nc.allow_non_contiguous_dma(reason="vectors of one number per partition"):
                pool.dma_start(cond_raw[:, 0, :], io["c_ctx"].rearrange("(k p) -> p k", p=P)).then_inc(x_in, 16)
                pool.dma_start(cond_raw[:, 1, :], io["c"][0].rearrange("(k p) -> p k", p=P)).then_inc(x_in, 16)
            pool.dma_start(x[:, 0, :], io["x_prompt"][0]).then_inc(x_in, 16)
            pool.dma_start(x[:, 1, :], io["x_sample"][0]).then_inc(x_in, 16)
            for k, (dst, value) in enumerate([(s0_gla[:], 0.0), (w_lr[:], 0.0), (lrT[32:33, :], 1.0),
                                              (half_neg[:], -0.5), (ones2[:], 1.0)]):
                g.memset(dst, value).then_inc(const_set, 1)
                pool.wait_ge(const_set, k + 1)

            def load_params(layer):
                def ld(dst, src):
                    pool.dma_start(dst, src).then_inc(params_in, 16)
                with nc.allow_non_contiguous_dma(reason="vectors of one number per partition"):
                    ld(gT[:, 0, :], io["norm1_g"][layer].rearrange("(k p) -> p k", p=P))
                    ld(gT[:, 1, :], io["norm2_g"][layer].rearrange("(k p) -> p k", p=P))
                    ld(q_g[:], io["mla_q_norm_g"][layer].rearrange("(k p) -> p k", p=P))
                ld(kv_g[:], io["mla_kv_norm_g"][layer:layer + 1, :].to_broadcast([P, P]))
                ld(w_q_up[:], io["mla_w_q_up"][layer].rearrange("(k p) n -> p k n", p=P))
                ld(w_kv_up[:], io["mla_w_kv_up"][layer])
                ld(w_lr[0:16, 0:128], io["gla_gate_w"][layer, 0])
                ld(w_lr[16:32, 128:256], io["gla_gate_w"][layer, 1])
                ld(w_lr[32:33, :], io["gla_gate_b"][layer:layer + 1].rearrange("l d n -> l (d n)"))
                ld(decay[:], io["ret_decay"][layer:layer + 1].rearrange("l d h -> l (d h)").to_broadcast([P, 2 * H]))
                ld(sink[:], io["gqa_sink"][layer:layer + 1, :].to_broadcast([P, H]))
                ld(ctx_ckv[:], io["cache_mla_ckv"][0, layer])
                ld(ctx_kr[:], io["cache_mla_krope"][0, layer])
                ld(ctx_k[:], io["cache_gqa_k"][0, layer].rearrange("h t d -> t h d"))
                ld(ctx_v[:], io["cache_gqa_v"][0, layer].rearrange("h t d -> t h d"))
                for d in range(2):
                    for h in range(H):
                        ld(s0_gla[32 * h:32 * h + 32, d, 64 * h:64 * h + 64], io["state_gla"][0, layer, d, h])
                ld(s0_ret[:].rearrange("k d h v -> k (d h) v"), io["state_ret"][0, layer].rearrange("d h k v -> k (d h) v"))

            def rope(v, n, d):
                x1, x2 = v[:, :, 0:d // 2], v[:, :, d // 2:d]
                cos, sin = mid(c(f"cos{d}"), n), mid(c(f"sin{d}"), n)
                ta, tb, tc, td = (r[:, 0:n * d // 2].rearrange("p (h d) -> p h d", h=n) for r in rope_t)
                link(g.tensor_tensor(ta, x1, cos, ALU.mult))
                link(g.tensor_tensor(tb, x2, sin, ALU.mult))
                link(g.tensor_tensor(tc, x1, sin, ALU.mult))
                link(g.tensor_tensor(td, x2, cos, ALU.mult))
                link(g.tensor_tensor(x1, ta, tb, ALU.subtract))
                return g.tensor_tensor(x2, tc, td, ALU.add)

            load_params(0)
            pool.dma_start(router[:], io["moe_router"][0].rearrange("(k p) e -> p k e", p=P)).then_inc(params_in, 16)

            for layer in range(L):
                if layer:
                    pool.wait_ge(x_mixed, 2 * layer - 1)
                    pool.wait_ge(stored, 16 * stores_per_layer * layer)
                    load_params(layer)
                def rstd(m):
                    for s in range(NS):
                        pool.wait_ge(var_ready, NS * m + s + 1)
                        g.tensor_tensor(stat[:, 4 + s:5 + s], stat[:, 2 + s:3 + s], half_neg[:, 0:1],
                                        ALU.pow).then_inc(rstd_ready, 1)
                rstd(2 * layer)
                pool.wait_ge(proj_act, (IN_PAGES + 1) // 2 * (layer + 1))
                pool.wait_ge(proj_dve, IN_PAGES // 2 * (layer + 1))

                def store(dst, src):
                    pool.dma_start(dst, src).then_inc(stored, 16)
                store(io["new_cache_mla_krope"][0, layer], pj(0, "mkr"))
                store(io["new_cache_gqa_k"][0, layer].rearrange("h t d -> t h d"), heads(pj(0, "ak"), 2))
                store(io["new_cache_gqa_v"][0, layer].rearrange("h t d -> t h d"), heads(pj(0, "av"), 2))
                rope(proj[:, 1, COL["rq"][0]:COL["rk"][1]].rearrange("p (h d) -> p h d", h=8), 8, 64).then_inc(roped, 1)
                pool.wait_ge(roped, 3 * layer + 1)
                rope(proj[:, 1, COL["aq"][0]:COL["ak"][1]].rearrange("p (h d) -> p h d", h=6), 6, 64).then_inc(roped, 1)
                pool.wait_ge(roped, 3 * layer + 2)
                rope(heads(pj(1, "mkr"), 1), 1, 32).then_inc(roped, 1)
                for s in range(NS):
                    n = NS * layer + s

                    def o_power(k):
                        pool.wait_ge(o_var, k + 1)
                        g.tensor_tensor(stat[:, 12:16], stat[:, 8:12], half_neg[:], ALU.pow).then_inc(o_rstd, 1)
                    if s == 0:
                        pool.wait_ge(g_state_kept, layer + 1)
                        for d in range(2):
                            for h in range(H):
                                store(io["new_state_gla"][0, layer, d, h],
                                      g_st[32 * h:32 * h + 32, d, 64 * h:64 * h + 64])
                    o_power(2 * n)
                    if s == 0:
                        pool.wait_ge(r_state_kept, layer + 1)
                        store(io["new_state_ret"][0, layer].rearrange("d h k v -> k (d h) v"), r_st[0:64, :, :])
                    o_power(2 * n + 1)
                    pool.wait_ge(m_var, n + 1)
                    g.tensor_tensor(stat[:, 20:22], stat[:, 18:20], half_neg[:, 0:2], ALU.pow).then_inc(m_rstd, 1)
                    if s == 0:
                        pool.wait_ge(m_normed, n + 1)
                        store(io["new_cache_mla_ckv"][0, layer], m_ckv)
                rstd(2 * layer + 1)
            pool.wait_ge(x_mixed, 2 * L - 1)
            pool.dma_start(final_g, io["final_norm_g"].rearrange("(a d) -> a d", a=1).to_broadcast([P, D]))\
                .then_inc(final_g_in, 16)
            rstd(2 * L)
            pool.wait_ge(stored, 16 * stores_per_layer * L)

        @block.tensor
        def _(pe):
            mm, turn = nc.tensor.matmul, nc.tensor.transpose

            def modulation(layer):
                for third in range(3):
                    if layer or third:
                        pe.wait_ge(mod_kept, 3 * layer + third)
                    if layer and not third:
                        pe.wait_ge(x_mixed, 2 * layer)
                    key = ("mod_bias", layer, third, 0)
                    wait_page(pe, key)
                    for q in range(4):
                        ins = mm(ps[32 * q:32 * q + 2, q, :], ones2[:], page(key)[0:1, 512 * q:512 * q + 512],
                                 start=True, stop=False)
                    ins.then_inc(mod_bias_used, 1)
                    for kt in range(KT):
                        key = ("mod", layer, third, kt)
                        wait_page(pe, key)
                        for q in range(4):
                            ins = mm(ps[32 * q:32 * q + 2, q, :], cond[:, :, kt], page(key)[:, 512 * q:512 * q + 512],
                                     start=False, stop=(kt == KT - 1))
                        ins.then_inc(mod_used, 1)
                    pe.wait_ge(mod_rows_act, 3 * layer + third + 1)
                    pe.wait_ge(mod_rows_dve, 3 * layer + third + 1)
                    for part in range(2):
                        for half in range(2):
                            q = 2 * part + half
                            rows = mod_row[32 * q:32 * q + 2, :]
                            if 2 * third + part in (2, 5):
                                for s in range(NS):
                                    ins = mm(ps[:, 4 + 2 * s + half, :], pick[32 * q:32 * q + 2, s, :], rows,
                                             start=True, stop=True)
                            else:
                                for j in range(4):
                                    ins = turn(ps[:, q, 2 * j:2 * j + 2], rows[:, P * j:P * j + P],
                                               ident[32 * q:32 * q + 2, 32 * q:32 * q + 2])
                        ins.then_inc(mod_turned, 1)

            def norm_turn(m):
                for s in range(NS):
                    pe.wait_ge(xn_ready, NS * m + s + 1)
                    for kt in range(KT):
                        ins = turn(ps[:, 2 * s + kt // 4, P * (kt % 4):P * (kt % 4) + P], row[:, s, P * kt:P * kt + P], ident)
                    ins.then_inc(xT_done, 1)

            def project(layer):
                pe.wait_ge(h_ready, 2 * layer + 1)
                pe.wait_ge(h_ready_act, 2 * layer + 1)
                for i in range(IN_PAGES):
                    key = ("w_in", layer, i, 0)
                    wait_page(pe, key)
                    w = min(256, IN_WIDTH - 256 * i)
                    b = page(key).rearrange("p (k n) -> p k n", k=KT)
                    if i >= 4:
                        if i % 2 == 0:
                            pe.wait_ge(proj_act, (IN_PAGES + 1) // 2 * layer + (i - 4) // 2 + 1)
                        else:
                            pe.wait_ge(proj_dve, IN_PAGES // 2 * layer + (i - 4) // 2 + 1)
                    for s in range(NS):
                        for kt in range(KT):
                            ins = mm(ps[:, 4 + i % 4, 256 * s:256 * s + w], hT[:, kt, P * s:P * s + P], b[:, kt, 0:w],
                                     start=(kt == 0), stop=(kt == KT - 1))
                    ins.then_inc(w_in_used, 1)

            def gla(layer, s):
                n = NS * layer + s
                turn(ps[0:32, 0, 0:P], pj(s, "glr"), ident).then_inc(lr_turned, 1)
                pe.wait_ge(lr_kept, n + 1)
                mm(ps[:, 1, 0:256], lrT[:], w_lr[:], start=True, stop=True).then_inc(lr_done, 1)
                pe.wait_ge(la_ready, n + 1)
                la_f, la_b = g_la[:, 0:P], g_la[:, P:2 * P]
                for level in range(LEVELS):
                    b, o = 2 + level // 4, P * (level % 4)
                    for to, fwd, bwd in ((b, sum_qf, sum_qb), (b + 2, sum_kf, sum_kb)):
                        mm(ps[:, to, o:o + P], fwd[:, level, :], la_f, start=True, stop=False)
                        mm(ps[:, to, o:o + P], bwd[:, level, :], la_b, start=False, stop=True)
                mm(ps[:, 3, 3 * P:], scan[:, 2 * s, :], la_f, start=True, stop=True)
                mm(ps[:, 5, 3 * P:], scan[:, 2 * s + 1, :], la_b, start=True, stop=True).then_inc(sums_done, 1)
                pe.wait_ge(decayed, n + 1)
                for r in range(2):
                    for j in range(4):
                        level = 4 * r + j
                        q_l = g_x[:, level, :] if level < LEVELS else g_d[:, 0, :]
                        k_l = g_x[:, 8 + level, :] if level < LEVELS else g_d[:, 1, :]
                        turn(ps[:, 0, P * j:P * j + P], q_l, ident)
                        ins = turn(ps[:, 1, P * j:P * j + P], k_l, ident)
                    ins.then_inc(g_turned, 1)
                    pe.wait_ge(g_q_kept, 2 * n + r + 1)
                    pe.wait_ge(g_k_kept, 2 * n + r + 1)
                    if r == 1:
                        pe.wait_ge(g_att_kept, 2 * n + 1)
                    for h in range(H):
                        for j in range(4):
                            ins = mm(ps[:, 2 + h, P * j:P * j + P], g_kT[32 * h:32 * h + 32, j, :],
                                     g_qT[32 * h:32 * h + 32, j, :], start=True, stop=True, tile_position=(32 * h, 0))
                    ins.then_inc(g_att_done, 1)
                gv = pj(s, "gv")
                if s == 1:
                    for d in range(2):
                        ins = turn(ps[:, 0, P * d:P * d + P], g_x[:, 7 + 8 * d, :], ident)
                    ins.then_inc(ext_turned, 1)
                else:
                    for d in range(2):
                        mm(ps[:, 7, 256 * d:256 * d + 256], g_x[:, 7 + 8 * d, :], gv, start=True, stop=True)
                pe.wait_ge(g_att_kept, 2 * n + 2)
                for h in range(H):
                    ins = mm(ps[:, 6, 64 * h:64 * h + 64], g_att[:, h, :], gv[:, 64 * h:64 * h + 64],
                             start=(s == 0 or h == 0), stop=(s == 0), skip_group_check=True)
                if s == 1:
                    pe.wait_ge(ext_kept, layer + 1)
                    for d in range(2):
                        ins = mm(ps[:, 6, 0:256], g_sT[:, d, :], s0_gla[:, d, :], start=False, stop=(d == 1),
                                 skip_group_check=True)
                ins.then_inc(g_out_done, 1)

            def retention(layer, s):
                n = NS * layer + s
                pe.wait_ge(o_mixed, 2 * n + 1)
                if s == 1:
                    pe.wait_ge(roped, 3 * layer + 1)
                for h in range(H):
                    turn(ps[0:64, 0, P * h:P * h + P], pj(s, "rq")[:, 64 * h:64 * h + 64], ident)
                    ins = turn(ps[0:64, 1, P * h:P * h + P], pj(s, "rk")[:, 64 * h:64 * h + 64], ident)
                ins.then_inc(r_turned, 1)
                pe.wait_ge(r_q_kept, n + 1)
                pe.wait_ge(r_k_kept, n + 1)
                for h in range(H):
                    ins = mm(ps[:, 2, P * h:P * h + P], r_kT[0:64, h, :], r_qT[0:64, h, :], start=True, stop=True)
                ins.then_inc(r_scores, 1)
                rv = pj(s, "rv")
                pe.wait_ge(r_att_kept, n + 1)
                for h in range(H):
                    mm(ps[:, 6, 64 * h:64 * h + 64], r_att[:, h, :], rv[:, 64 * h:64 * h + 64], start=True, stop=True)
                for d in range(2):
                    for h in range(H):
                        o = 256 * d + 64 * h
                        if s == 1:
                            ins = mm(ps[:, 3, o:o + 64], r_qT[0:64, h, :], s0_ret[:, d, h, :], start=True, stop=True)
                        else:
                            ins = mm(ps[0:64, 3, o:o + 64], r_kd[:, d, 64 * h:64 * h + 64], rv[:, 64 * h:64 * h + 64],
                                     start=True, stop=True)
                ins.then_inc(r_out_done, 1)

            def mla_up(layer, s):
                n = NS * layer + s
                pe.wait_ge(o_mixed, 2 * n + 2)
                pe.wait_ge(m_normed, n + 1)
                turn(ps[:, 0, 0:P], m_q[:, 0:P], ident)
                turn(ps[:, 0, P:2 * P], m_q[:, P:2 * P], ident)
                ins = turn(ps[:, 0, 2 * P:3 * P], m_ckv, ident)
                if s == 1:
                    ins = turn(ps[:, 0, 3 * P:], ctx_ckv[:], ident)
                ins.then_inc(m_turned, 1)
                pe.wait_ge(m_kept, n + 1)
                for k in range(2):
                    mm(ps[:, 1, 0:384], m_qT[:, k, :], w_q_up[:, k, :], start=(k == 0), stop=(k == 1))
                ins = mm(ps[:, 2, :], m_qT[:, 2, :], w_kv_up[:], start=True, stop=True)
                if s == 1:
                    ins = mm(ps[:, 3, :], m_qT[:, 3, :], w_kv_up[:], start=True, stop=True)
                ins.then_inc(m_up_done, 1)

            def attention(layer, s, kind):
                n = NS * layer + s
                a = 2 * n + kind
                nk = 1 + s
                if kind == 0:
                    pe.wait_ge(m_q_kept, n + 1)
                    pe.wait_ge(m_k_kept, n + 1)
                    dk, q = 96, a_q
                    k, nh = [a_k[:, t] for t in range(nk)], H
                    v = [a_v[:, t] for t in range(nk)]
                else:
                    pe.wait_ge(a_mixed, 2 * n + 1)
                    if s == 1:
                        pe.wait_ge(roped, 3 * layer + 2)
                    dk, q = 64, heads(pj(s, "aq"), H)
                    k, nh = [heads(pj(s, "ak"), 2), ctx_k[:]][:nk], 2
                    v = [heads(pj(s, "av"), 2), ctx_v[:]][:nk]
                for h in range(H):
                    ins = turn(ps[0:dk, 0, P * h:P * h + P], q[:, h, :], ident)
                for t in range(nk):
                    for h in range(nh):
                        ins = turn(ps[0:dk, 1 + t, P * h:P * h + P], k[t][:, h, :], ident)
                ins.then_inc(a_turned, 1)
                pe.wait_ge(a_q_kept, a + 1)
                pe.wait_ge(a_k_kept, a + 1)
                for h in range(H):
                    for t in range(nk):
                        o = 256 * (h % 2) + P * t
                        ins = mm(ps[:, 3 + h // 2, o:o + P], a_qT[0:dk, h, :], a_kT[0:dk, t, h * nh // H, :],
                                 start=True, stop=True)
                ins.then_inc(a_scores, 1)
                pe.wait_ge(a_probs, a + 1)
                for t in range(nk):
                    for h in range(H):
                        ins = turn(ps[:, 5 + t, P * h:P * h + P], a_p[:, h, P * t:P * t + P], ident)
                ins.then_inc(a_p_turned, 1)
                pe.wait_ge(a_p0_kept, a + 1)
                if s == 1:
                    pe.wait_ge(a_p1_kept, 2 * layer + kind + 1)
                for h in range(H):
                    for t in range(nk):
                        ins = mm(ps[:, 7, 64 * h:64 * h + 64], a_pT[:, t, h, :], v[t][:, h * nh // H, :],
                                 start=(t == 0), stop=(t == nk - 1))
                ins.then_inc(a_out, 1)

            def out_project(layer):
                for i in range(KT // 2):
                    key = ("w_out", layer, i, 0)
                    wait_page(pe, key)
                    b = page(key).rearrange("p (k n) -> p k n", k=2)
                    for s in range(NS):
                        for half in range(2):
                            for k in range(2):
                                kt = 2 * i + k
                                ins = mm(ps[:, 4 + 2 * s + half, :], hT[:, kt, P * s:P * s + P],
                                         b[:, k, HALF * half:HALF * half + HALF], start=(kt == 0), stop=(kt == KT - 1))
                    ins.then_inc(w_out_used, 1)

            def gate_up(gp, up, k, bank, done):
                for w, o in ((gp, 0), (up, 256)):
                    wv = w.rearrange("p (k n) -> p k n", k=KT)
                    for kt in range(KT):
                        ins = mm(ps[:, bank, o:o + 256], wv[:, kt, P * k:P * k + P], hT[:, kt, :],
                                 start=(kt == 0), stop=(kt == KT - 1))
                ins.then_inc(done, 1)

            def down(dp, k, hid, blk, n_blocks, done):
                dv = dp.rearrange("p (b n) -> p b n", b=2)
                for s in range(NS):
                    for half in range(2):
                        ins = mm(ps[:, 2 * s + half, :], hid[:, P * s:P * s + P],
                                 dv[:, k, HALF * half:HALF * half + HALF], start=(blk == 0), stop=(blk == n_blocks - 1))
                ins.then_inc(done, 1)

            def dense(layer):
                pe.wait_ge(h_ready, 2 * layer + 2)
                pe.wait_ge(h_ready_act, 2 * layer + 2)
                for blk in range(DENSE_BLOCKS + 1):
                    if blk < DENSE_BLOCKS:
                        u, k = blk // FF, blk % FF
                        if k == 0:
                            wait_page(pe, ("gate", layer, u, 0))
                            wait_page(pe, ("up", layer, u, 0))
                        if blk >= 4:
                            pe.wait_ge(hid_ready, blk - 3)
                        gate_up(page(("gate", layer, u, 0)), page(("up", layer, u, 0)), k, 4 + blk % 4, gu_done)
                    if blk:
                        u, k = (blk - 1) // FF, (blk - 1) % FF
                        if k == 0:
                            wait_page(pe, ("down", layer, u, 0))
                        pe.wait_ge(hid_ready, blk)
                        down(page(("down", layer, u, 0)), k, f_hid[:, (blk - 1) % 4], blk - 1, DENSE_BLOCKS, down_done)

            def route():
                pe.wait_ge(params_in, 16 * (N_PARAMS * L + 1))
                pe.wait_ge(h_ready, 2 * L)
                pe.wait_ge(h_ready_act, 2 * L)
                for s in range(NS):
                    for kt in range(KT):
                        ins = mm(ps[:, 4, E * s:E * s + E], hT[:, kt, P * s:P * s + P], router[:, kt, :],
                                 start=(kt == 0), stop=(kt == KT - 1))
                ins.then_inc(logits_done, 1)
                for s in range(NS):
                    for kt in range(KT):
                        ins = turn(ps[:, 2 * s + kt // 4, P * (kt % 4):P * (kt % 4) + P], hT[:, kt, P * s:P * s + P], ident)
                ins.then_inc(h_back, 1)
                pe.wait_ge(route_ready, 1)
                after, before = scan[:, 0, :], scan[:, 1, :]
                m0, m1 = moe_m[:, 0, 0:E], moe_m[:, 1, 0:E]
                for o, terms in ((0, [(before, m0)]), (E, [(before, m1), (after, m0), (before, m0)]),
                                 (2 * E, [(after, m0), (before, m0), (after, m1), (before, m1)])):
                    for k, (tri, m) in enumerate(terms):
                        ins = mm(ps[:, 5, o:o + E], tri, m, start=(k == 0), stop=(k == len(terms) - 1))
                ins.then_inc(places_done, 1)
                pe.wait_ge(h_rows_act, 1)
                pe.wait_ge(h_rows_dve, 1)
                pe.wait_ge(sel_ready, 1)
                gather()

            def gather():
                for kt in range(KT):
                    for s in range(NS):
                        ins = mm(ps[:, 2 + kt // 4, P * (kt % 4):P * (kt % 4) + CAP], row[:, s, P * kt:P * kt + P],
                                 sel[:, s, :], start=(s == 0), stop=(s == NS - 1))
                ins.then_inc(gather_done, 1)

            def scatter(s):
                for half in range(2):
                    ins = mm(ps[:, 2 + half, :], sel_wT[0:CAP, s, :], e_y[0:CAP, HALF * half:HALF * half + HALF],
                             start=True, stop=True)
                ins.then_inc(scatter_done, 1)

            def experts():
                def wait_expert_page(e, j):
                    pe.wait_ge(loaded[j % MOE_SLOTS],
                               e * (16 * LOADS) + 16 * (loads_before_moe[j % MOE_SLOTS] + j // MOE_SLOTS + 1))

                def gate_up_pair(j, k, g):
                    a, b = moe_at[j % MOE_SLOTS], moe_at[(j + 1) % MOE_SLOTS]
                    off = 256 * k + P * (g % 2)
                    return arena[:, a:a + 2 * (b - a)].rearrange("p (two n) -> p two n", two=2)[:, :, off:off + P]

                def tile_gate_up(e, u, t):
                    i = TILES * u + t
                    pe.wait_ge(hid_ready, e * MOE_TILES + (DENSE_BLOCKS + i - 2))
                    for kt in range(KT):
                        for g in range(4):
                            ins = mm(ps[32 * g:32 * g + 32, 4 + i % 3, 0:256], e_h[:, kt, 32 * t:32 * t + 32],
                                     gate_up_pair(6 * u + 2 * (g // 2), kt, g), start=(kt == 0), stop=(kt == KT - 1))
                    ins.then_inc(gu_done, 1)

                def turn_hidden(e, u):
                    pe.wait_ge(hid_ready, e * MOE_TILES + (DENSE_BLOCKS + TILES * (u + 1)))
                    for t in range(TILES):
                        ins = turn(ps[:, 7, P * t:P * t + P], e_hid[:, u % 2, t, :], ident)
                    ins.then_inc(hid_turned, 1)

                def unit_down(e, u):
                    pe.wait_ge(hidT_ready, e * UNITS + (u + 1))
                    wait_expert_page(e, 6 * u + 4)
                    wait_expert_page(e, 6 * u + 5)
                    for g in range(4):
                        at = moe_at[(6 * u + 4 + g // 2) % MOE_SLOTS] + D * (g % 2)
                        for half in range(2):
                            ins = mm(ps[0:CAP, half, :], e_hidT[:, g, :], arena[:, at + HALF * half:at + HALF * half + HALF],
                                     start=(u == 0 and g == 0), stop=(u == UNITS - 1 and g == 3))
                    ins.then_inc(down_done, 1)

                with pe.Fori(0, E) as e:
                    pe.wait_ge(gathered_act, e + 1)
                    pe.wait_ge(gathered_dve, e + 1)
                    for u in range(UNITS):
                        for j in range(4):
                            wait_expert_page(e, 6 * u + j)
                        tile_gate_up(e, u, 0)
                        if u:
                            turn_hidden(e, u - 1)
                        else:
                            pe.wait_ge(y_copied_act, e + 1)
                            pe.wait_ge(y_copied_dve, e + 1)
                            scatter(0)
                        tile_gate_up(e, u, 1)
                        if u:
                            unit_down(e, u - 1)
                        else:
                            pe.wait_ge(y_added, e * 2 + 2)
                            scatter(1)
                        for t in range(2, TILES):
                            tile_gate_up(e, u, t)
                        if u == 3:
                            pe.wait_ge(sel_w_ready, e + 1)
                            pe.wait_ge(y_added, e * 2 + 3)
                            for s in range(NS):
                                ins = turn(ps[0:CAP, 2, P * s:P * s + P], sel_w[:, s, :], ident)
                            ins.then_inc(sel_w_turned, 1)
                    pe.wait_ge(sel_ready, e + 2)
                    pe.wait_ge(sel_wT_ready, e + 2)
                    gather()
                    turn_hidden(e, UNITS - 1)
                    unit_down(e, UNITS - 1)
                pe.wait_ge(y_copied_act, E + 1)
                pe.wait_ge(y_copied_dve, E + 1)
                pe.wait_ge(gathered_act, E + 1)
                pe.wait_ge(gathered_dve, E + 1)
                scatter(0)
                pe.wait_ge(y_added, 2 * E + 2)
                scatter(1)

            def spill():
                pe.wait_ge(y_added, 2 * E + 3)
                pe.sem_inc(spill_down, 1)
                pe.sem_inc(spill_gu, 1)
                with pe.Fori(0, E) as e:
                    count = pe.value_load(moe_count[0:1, bass.ds(e, 1)], min_val=0, max_val=NS * P)
                    with pe.If(count > CAP):
                        for blk in range(SPILL_BLOCKS):
                            u, k = blk // FF, blk % FF
                            at = PAGE * 3 * (u % 2)
                            if k == 0:
                                pe.wait_ge(spill_loaded[u % 2], e * (24 * SPILL_UNITS) + 48 * (u // 2 + 1))
                            if blk == 0:
                                pe.wait_ge(spill_y, e * 2 + 1)
                            gate_up(arena[:, at:at + PAGE], arena[:, at + PAGE:at + 2 * PAGE], k, 4 + blk % 2, spill_gu)
                            pe.wait_ge(spill_hid, e * SPILL_BLOCKS + (blk + 2))
                            down(arena[:, at + 2 * PAGE:at + 3 * PAGE], k, s_hid, blk, SPILL_BLOCKS, spill_down)
                    with pe.Else():
                        pe.wait_ge(spill_down, e * SPILL_BLOCKS + 1)
                        pe.sem_inc(spill_gu, SPILL_BLOCKS)
                        pe.sem_inc(spill_down, SPILL_BLOCKS)

            pe.wait_ge(const_in, 16)
            pe.wait_ge(const_set, 5)
            pe.wait_ge(cond_ready, 9)
            for layer in range(L):
                modulation(layer)
                norm_turn(2 * layer)
                project(layer)
                pe.wait_ge(params_in, 16 * (N_PARAMS * (layer + 1) + 1))
                pe.wait_ge(proj_act, (IN_PAGES + 1) // 2 * (layer + 1))
                pe.wait_ge(proj_dve, IN_PAGES // 2 * (layer + 1))
                for s in range(NS):
                    n = NS * layer + s
                    gla(layer, s)
                    retention(layer, s)
                    mla_up(layer, s)
                    attention(layer, s, 0)
                    attention(layer, s, 1)
                    pe.wait_ge(a_mixed, 2 * n + 2)
                    for kt in range(KT):
                        ins = turn(ps[:, kt // 4, P * (kt % 4):P * (kt % 4) + P], mixed[:, P * kt:P * kt + P], ident)
                    ins.then_inc(mix_turned, 1)
                    pe.wait_ge(mix_kept, n + 1)
                    pe.wait_ge(mix_kept_act, n + 1)
                out_project(layer)
                norm_turn(2 * layer + 1)
                if layer % 2 == 0:
                    dense(layer)
                else:
                    route()
                    experts()
                    spill()

        @block.scalar
        def _(act):
            a_ = nc.scalar
            steps = [0]

            def link(ins):
                steps[0] += 1
                ins.then_inc(act_step, 1)
                act.wait_ge(act_step, steps[0])

            def keep_hidden_turned(act, a_, n):
                act.wait_ge(hid_turned, n)
                a_.copy(e_hidT.rearrange("p g (t n) -> p t g n", t=TILES),
                        ps[:, 7, 0:TILES * P].rearrange("p (t g n) -> p t g n", t=TILES, g=4)).then_inc(hidT_ready, 1)

            def norm_squares(m):
                for s in range(NS):
                    if m:
                        act.wait_ge(x_mixed, m)
                    a_.activation(row[:, s, :], x[:, s, :], ACT.Square, accum_out=stat[:, s:s + 1]).then_inc(sq_ready, 1)

            def norm_spread(m):
                act.wait_ge(xT_done, NS * m + 2)
                w = m % 2
                for kt in range(KT):
                    ins = a_.activation(hT[:, kt, P:2 * P], ps[:, 2 + kt // 4, P * (kt % 4):P * (kt % 4) + P], ACT.Identity,
                                        bias=mod_T[:, 2 * w, kt, 1:2], scale=scale_A[:, w, kt, 1:2])
                ins.then_inc(h_ready_act, 1)

            def o_post(k, gate, s):
                act.wait_ge(o_kept, k + 1)
                a_.activation(o_sq, o_sum, ACT.Square).then_inc(o_sq_ready, 1)
                a_.activation(o_gate, pj(s, gate), ACT.Exp, scale=-1.0).then_inc(o_gate_exp, 1)

            act.wait_ge(x_in, 64)
            a_.activation(cond[:], cond_raw[:], ACT.Silu).then_inc(cond_ready, 1)
            for layer in range(L):
                for third in range(3):
                    i = 3 * layer + third
                    act.wait_ge(mod_used, KT * (i + 1))
                    act.wait_ge(mod_bias_used, i + 1)
                    if i:
                        act.wait_ge(mod_kept, i)
                    a_.copy(mod_row[0:2], ps[0:2, 0, :])
                    a_.copy(mod_row[32:34], ps[32:34, 1, :]).then_inc(mod_rows_act, 1)
                act.wait_ge(mod_kept, 3 * (layer + 1))
                act.wait_ge(params_in, 16 * (N_PARAMS * (layer + 1) + 1))
                link(a_.activation(lg_abs[:], decay[:], ACT.Abs))
                link(a_.activation(lg_abs[:], lg_abs[:], ACT.Exp, scale=-1.0))
                a_.activation(lg_abs[:], lg_abs[:], ACT.Ln, bias=1.0).then_inc(ret_exp, 1)
                act.wait_ge(ret_lg, layer + 1)
                for k in range(4):
                    a_.activation(ret_pow[:, k, :], lg[:, H * (k % 2):H * (k % 2) + H], ACT.Exp,
                                  scale=c("pos")[:, k:k + 1]).then_inc(ret_ready, 1)
                act.wait_ge(ret_dist, layer + 1)
                a_.activation(ret_D[:], ret_D[:], ACT.Exp).then_inc(ret_ready, 1)
                norm_squares(2 * layer)
                norm_spread(2 * layer)
                for i in range(0, IN_PAGES, 2):
                    w = min(256, IN_WIDTH - 256 * i)
                    act.wait_ge(w_in_used, IN_PAGES * layer + i + 1)
                    a_.copy(proj[:, :, 256 * i:256 * i + w],
                            ps[:, 4 + i % 4, :].rearrange("p (s n) -> p s n", s=NS)[:, :, 0:w]).then_inc(proj_act, 1)
                act.wait_ge(proj_dve, IN_PAGES // 2 * (layer + 1))
                act.wait_ge(proj_act, (IN_PAGES + 1) // 2 * (layer + 1))
                for s in range(NS):
                    n = NS * layer + s
                    act.wait_ge(lr_done, n + 1)
                    link(a_.activation(g_abs, ps[:, 1, 0:256], ACT.Abs))
                    link(a_.activation(g_abs, g_abs, ACT.Exp, scale=-1.0))
                    a_.activation(g_abs, g_abs, ACT.Ln, bias=1.0).then_inc(lr_soft, 1)
                    act.wait_ge(sums_done, n + 1)
                    a_.activation(g_x.rearrange("p l t -> p (l t)"), ps[:, 2:6, :].rearrange("p b n -> p (b n)"),
                                  ACT.Exp).then_inc(decays_ready, 1)
                    for r in range(2):
                        act.wait_ge(g_turned, 2 * n + r + 1)
                        if r:
                            act.wait_ge(g_att_done, 2 * n + 1)
                        a_.copy(g_qT.rearrange("p l t -> p (l t)"), ps[:, 0, :]).then_inc(g_q_kept, 1)
                    if s == 1:
                        act.wait_ge(ext_turned, layer + 1)
                        a_.copy(g_sT.rearrange("p l t -> p (l t)"), ps[:, 0, 0:256]).then_inc(ext_kept, 1)
                    else:
                        act.wait_ge(g_out_done, n + 1)
                        a_.copy(g_st.rearrange("p l t -> p (l t)"), ps[:, 7, :]).then_inc(g_state_kept, 1)
                    o_post(2 * n, "gog", s)
                    act.wait_ge(r_turned, n + 1)
                    a_.copy(r_qT[0:64].rearrange("p l t -> p (l t)"), ps[0:64, 0, :]).then_inc(r_q_kept, 1)
                    if s == 0:
                        act.wait_ge(r_out_done, n + 1)
                        a_.copy(r_st[0:64].rearrange("p l t -> p (l t)"), ps[0:64, 3, :]).then_inc(r_state_kept, 1)
                    o_post(2 * n + 1, "rg", s)
                    act.wait_ge(o_mixed, 2 * n + 2)
                    link(a_.activation(m_q, pj(s, "mcq"), ACT.Square, accum_out=stat[:, 16:17]))
                    a_.activation(m_q[:, 0:P], pj(s, "mckv"), ACT.Square, accum_out=stat[:, 17:18]).then_inc(m_sq, 1)
                    act.wait_ge(m_up_done, n + 1)
                    a_.copy(a_q.rearrange("p h d -> p (h d)"), ps[:, 1, 0:384]).then_inc(m_q_kept, 1)
                    for kind in range(2):
                        a = 2 * n + kind
                        dk, scale = ((96, 96 ** -0.5), (64, 64 ** -0.5))[kind]
                        act.wait_ge(a_turned, a + 1)
                        a_.copy(a_qT[0:dk].rearrange("p l t -> p (l t)"), ps[0:dk, 0, :]).then_inc(a_q_kept, 1)
                        act.wait_ge(a_shift, a + 1)
                        for h in range(H):
                            o = 256 * (h % 2)
                            ins = a_.activation(a_p[:, h, 0:P * (1 + s)], ps[:, 3 + h // 2, o:o + P * (1 + s)], ACT.Exp,
                                                bias=stat[:, 24 + h:25 + h], scale=scale,
                                                accum_out=stat[:, 28 + h:29 + h])
                        if kind == 1:
                            ins = a_.activation(stat[:, 36:40], stat[:, 32:36], ACT.Exp)
                        ins.then_inc(a_probs, 1)
                        act.wait_ge(a_p_turned, a + 1)
                        a_.copy(a_pT[:, 0].rearrange("p l t -> p (l t)"), ps[:, 5, :]).then_inc(a_p0_kept, 1)
                    act.wait_ge(mix_turned, n + 1)
                    a_.copy(hT[:, 0:4, P * s:P * s + P], ps[:, 0, :].rearrange("p (k t) -> p k t", k=4)).then_inc(mix_kept_act, 1)
                act.wait_ge(stored, 16 * stores_per_layer * (layer + 1))
                norm_squares(2 * layer + 1)
                norm_spread(2 * layer + 1)
                if layer % 2 == 0:
                    for blk in range(DENSE_BLOCKS):
                        act.wait_ge(gu_done, blk + 1)
                        if blk >= 2:
                            act.wait_ge(hid_ready, blk - 1)
                        a_.activation(f_sg[:, blk % 2, :], ps[:, 4 + blk % 4, 0:256], ACT.Silu).then_inc(silu_ready, 1)
                else:
                    act.wait_ge(route_top, 1)
                    a_.activation(stat[:, 50:52], stat[:, 48:50], ACT.Exp).then_inc(route_exp, 1)
                    act.wait_ge(h_back, 1)
                    a_.copy(row[:, 0, :], ps[:, 0:2, :].rearrange("p b n -> p (b n)")).then_inc(h_rows_act, 1)

                    def keep_gathered():
                        a_.copy(e_h[:, 0:4, :], ps[:, 2, :].rearrange("p (k n) -> p k n", k=4)[:, :, 0:CAP])\
                            .then_inc(gathered_act, 1)

                    act.wait_ge(gather_done, 1)
                    keep_gathered()
                    act.wait_ge(y_kept, 1)
                    act.sem_inc(y_copied_act, 1)
                    with act.Fori(0, E) as e:
                        for u in range(UNITS):
                            for t in range(TILES):
                                i = TILES * u + t
                                act.wait_ge(gu_done, e * MOE_TILES + (DENSE_BLOCKS + i + 1))
                                act.wait_ge(hid_ready, e * MOE_TILES + (DENSE_BLOCKS + i - 2))
                                a_.activation(e_sg[:, i % 3, :], ps[:, 4 + i % 3, 0:P], ACT.Silu).then_inc(silu_ready, 1)
                                if t == 0 and u:
                                    keep_hidden_turned(act, a_, e * UNITS + u)
                        act.wait_ge(gather_done, e + 2)
                        keep_gathered()
                        keep_hidden_turned(act, a_, e * UNITS + UNITS)
                        act.wait_ge(down_done, e * UNITS + (DENSE_BLOCKS + UNITS))
                        a_.copy(e_y[0:CAP, 0:HALF], ps[0:CAP, 0, :]).then_inc(y_copied_act, 1)
                    act.wait_ge(y_added, 2 * E + 3)
                    act.sem_inc(spill_silu, 1)
                    with act.Fori(0, E) as e:
                        count = act.value_load(moe_count[0:1, bass.ds(e, 1)], min_val=0, max_val=NS * P)
                        with act.If(count > CAP):
                            for blk in range(SPILL_BLOCKS):
                                act.wait_ge(spill_gu, e * SPILL_BLOCKS + (blk + 2))
                                act.wait_ge(spill_hid, e * SPILL_BLOCKS + (blk + 1))
                                a_.activation(s_sg, ps[:, 4 + blk % 2, 0:256], ACT.Silu).then_inc(spill_silu, 1)
                        with act.Else():
                            act.wait_ge(spill_silu, e * SPILL_BLOCKS + 1)
                            act.sem_inc(spill_silu, SPILL_BLOCKS)
            norm_squares(2 * L)

        @block.vector
        def _(dve):
            v = nc.vector
            steps = [0]

            def link(ins):
                steps[0] += 1
                ins.then_inc(dve_step, 1)
                dve.wait_ge(dve_step, steps[0])

            def norm_rows(m):
                for s in range(NS):
                    dve.wait_ge(sq_ready, NS * m + s + 1)
                    v.tensor_scalar(stat[:, 2 + s:3 + s], stat[:, s:s + 1], 1.0 / D, EPS, ALU.mult, ALU.add)\
                        .then_inc(var_ready, 1)
                for s in range(NS):
                    dve.wait_ge(rstd_ready, NS * m + s + 1)
                    v.tensor_scalar(row[:, s, :], x[:, s, :], stat[:, 4 + s:5 + s], None, ALU.mult).then_inc(xn_ready, 1)

            def norm_spread(m):
                dve.wait_ge(xT_done, NS * m + 1)
                w = m % 2
                for kt in range(KT):
                    ins = v.tensor_scalar(hT[:, kt, 0:P], ps[:, kt // 4, P * (kt % 4):P * (kt % 4) + P],
                                          scale_A[:, w, kt, 0:1], mod_T[:, 2 * w, kt, 0:1], ALU.mult, ALU.add)
                ins.then_inc(h_ready, 1)

            def o_post(k, gate, s, col):
                o3, t3, sq3 = heads(o_sum, H), heads(o_tmp, H), heads(o_sq, H)
                dve.wait_ge(o_sq_ready, k + 1)
                link(v.tensor_reduce(stat[:, 8:12], sq3, AX, ALU.add))
                v.tensor_scalar(stat[:, 8:12], stat[:, 8:12], 1.0 / 64, EPS, ALU.mult, ALU.add).then_inc(o_var, 1)
                dve.wait_ge(o_gate_exp, k + 1)
                link(v.tensor_scalar(o_gate, o_gate, 1.0, None, ALU.add))
                link(v.reciprocal(o_gate, o_gate))
                link(v.tensor_tensor(o_gate, o_gate, pj(s, gate), ALU.mult))
                dve.wait_ge(o_rstd, k + 1)
                link(v.tensor_tensor(t3, o3, last(stat[:, 12:16], 64), ALU.mult))
                v.tensor_tensor(mixed[:, col:col + 256], o_tmp, o_gate, ALU.mult).then_inc(o_mixed, 1)

            dve.wait_ge(const_in, 16)
            for q in range(4):
                for s in range(NS):
                    rows = slice(32 * q, 32 * q + 2)
                    v.tensor_copy(pick[rows, s, :], ident[rows, 32 * q + s:32 * q + s + 1].to_broadcast([2, P]))\
                        .then_inc(cond_ready, 1)
            for layer in range(L):
                for third in range(3):
                    i = 3 * layer + third
                    dve.wait_ge(mod_used, KT * (i + 1))
                    if i:
                        dve.wait_ge(mod_kept, i)
                    v.tensor_copy(mod_row[64:66], ps[64:66, 2, :])
                    v.tensor_copy(mod_row[96:98], ps[96:98, 3, :]).then_inc(mod_rows_dve, 1)
                    for part in range(2):
                        dve.wait_ge(mod_turned, 2 * i + part + 1)
                        what = 2 * third + part
                        if what in (2, 5):
                            ins = v.tensor_copy(gates[:, (what - 2) // 3].rearrange("p s n -> p (s n)"),
                                                ps[:, 4:8, :].rearrange("p b n -> p (b n)"))
                        else:
                            where = {0: 0, 1: 1, 3: 2, 4: 3}[what]
                            ins = v.tensor_copy(mod_T[:, where].rearrange("p (h k) s -> p h (k s)", h=2),
                                                ps[:, 2 * part:2 * part + 2, 0:KT])
                        if part:
                            ins.then_inc(mod_kept, 1)
                        else:
                            link(ins)
                dve.wait_ge(mod_kept, 3 * (layer + 1))
                dve.wait_ge(params_in, 16 * (N_PARAMS * (layer + 1) + 1))
                for w in range(2):
                    link(v.scalar_tensor_tensor(scale_A[:, w], mod_T[:, 2 * w + 1], 1.0, last(gT[:, w, :], NS), ALU.add, ALU.mult))
                dve.wait_ge(ret_exp, layer + 1)
                v.scalar_tensor_tensor(lg[:], decay[:], 0.0, lg_abs[:], ALU.min, ALU.subtract).then_inc(ret_lg, 1)
                dve.wait_ge(ret_lg, layer + 1)
                for h in range(H):
                    link(v.tensor_scalar(ret_D[:, h, :], dist[:, 0, :], lg[:, h:h + 1], None, ALU.mult))
                for h in range(H):
                    ins = v.scalar_tensor_tensor(ret_D[:, h, :], dist[:, 1, :], lg[:, H + h:H + h + 1], ret_D[:, h, :],
                                                 ALU.mult, ALU.add)
                    if h < H - 1:
                        link(ins)
                ins.then_inc(ret_dist, 1)
                dve.wait_ge(ret_ready, 5 * (layer + 1))
                link(v.tensor_tensor(ret_D[:], ret_D[:], mid(ident, H), ALU.add))
                norm_rows(2 * layer)
                norm_spread(2 * layer)
                for i in range(1, IN_PAGES, 2):
                    w = min(256, IN_WIDTH - 256 * i)
                    dve.wait_ge(w_in_used, IN_PAGES * layer + i + 1)
                    v.tensor_copy(proj[:, :, 256 * i:256 * i + w],
                                  ps[:, 4 + i % 4, :].rearrange("p (s n) -> p s n", s=NS)[:, :, 0:w]).then_inc(proj_dve, 1)
                dve.wait_ge(proj_act, (IN_PAGES + 1) // 2 * (layer + 1))
                dve.wait_ge(proj_dve, IN_PAGES // 2 * (layer + 1))
                for s in range(NS):
                    n = NS * layer + s
                    dve.wait_ge(lr_turned, n + 1)
                    v.tensor_copy(lrT[0:32, :], ps[0:32, 0, 0:P]).then_inc(lr_kept, 1)
                    dve.wait_ge(lr_soft, n + 1)
                    v.scalar_tensor_tensor(g_la, ps[:, 1, 0:256], 0.0, g_abs, ALU.min, ALU.subtract).then_inc(la_ready, 1)
                    dve.wait_ge(decays_ready, n + 1)
                    gq, gk = pj(s, "gq"), pj(s, "gk")
                    link(v.tensor_scalar(g_d[:, 0, :], gq, 2.0, None, ALU.mult))
                    link(v.tensor_scalar(g_d[:, 1, :], gk, 32 ** -0.5, None, ALU.mult))
                    link(v.tensor_tensor(g_x[:, 0:7, :], g_x[:, 0:7, :], mid(gq, 7), ALU.mult))
                    link(v.tensor_tensor(g_x[:, 8:15, :], g_x[:, 8:15, :], mid(g_d[:, 1, :], 7), ALU.mult))
                    state_side = gq if s == 1 else g_d[:, 1, :]
                    link(v.tensor_tensor(g_x[:, 7, :], g_x[:, 7, :], state_side, ALU.mult))
                    v.tensor_tensor(g_x[:, 15, :], g_x[:, 15, :], state_side, ALU.mult).then_inc(decayed, 1)
                    for r in range(2):
                        dve.wait_ge(g_turned, 2 * n + r + 1)
                        if r:
                            dve.wait_ge(g_att_done, 2 * n + 1)
                        v.tensor_copy(g_kT.rearrange("p l t -> p (l t)"), ps[:, 1, :]).then_inc(g_k_kept, 1)
                        dve.wait_ge(g_att_done, 2 * n + r + 1)
                        for j in range(4):
                            level = 4 * r + j
                            mask = masks[:, level, :] if level < LEVELS else ident
                            ins = v.copy_predicated(g_att, mid(mask, H).bitcast(U32), ps[:, 2:6, P * j:P * j + P])
                            if j < 3:
                                link(ins)
                        ins.then_inc(g_att_kept, 1)
                        dve.wait_ge(g_att_kept, 2 * n + r + 1)
                    dve.wait_ge(g_out_done, n + 1)
                    v.tensor_copy(o_sum, ps[:, 6, 0:256]).then_inc(o_kept, 1)
                    o_post(2 * n, "gog", s, 0)
                    dve.wait_ge(r_turned, n + 1)
                    v.tensor_copy(r_kT[0:64].rearrange("p l t -> p (l t)"), ps[0:64, 1, :]).then_inc(r_k_kept, 1)
                    if s == 0:
                        for d in range(2):
                            link(v.scalar_tensor_tensor(heads(r_kd[:, d], H), heads(pj(s, "rk"), H), 0.125,
                                                        last(ret_pow[:, d, :], 64), ALU.mult, ALU.mult))
                    dve.wait_ge(r_scores, n + 1)
                    v.scalar_tensor_tensor(r_att.rearrange("p h t -> p (h t)"), ps[:, 2, :], 0.125,
                                           ret_D[:].rearrange("p h t -> p (h t)"), ALU.mult, ALU.mult)\
                        .then_inc(r_att_kept, 1)
                    dve.wait_ge(r_out_done, n + 1)
                    if s == 0:
                        v.tensor_copy(o_sum, ps[:, 6, 0:256]).then_inc(o_kept, 1)
                    else:
                        link(v.tensor_tensor(heads(o_tmp, H), heads(ps[:, 3, 0:256], H), last(ret_pow[:, 2, :], 64), ALU.mult))
                        link(v.tensor_tensor(o_sum, ps[:, 6, 0:256], o_tmp, ALU.add))
                        link(v.tensor_tensor(heads(o_tmp, H), heads(ps[:, 3, 256:512], H), last(ret_pow[:, 3, :], 64), ALU.mult))
                        v.tensor_tensor(o_sum, o_sum, o_tmp, ALU.add).then_inc(o_kept, 1)
                    o_post(2 * n + 1, "rg", s, 512)
                    dve.wait_ge(m_sq, n + 1)
                    link(v.tensor_scalar(stat[:, 18:19], stat[:, 16:17], 1.0 / 256, EPS, ALU.mult, ALU.add))
                    v.tensor_scalar(stat[:, 19:20], stat[:, 17:18], 1.0 / 128, EPS, ALU.mult, ALU.add).then_inc(m_var, 1)
                    dve.wait_ge(m_rstd, n + 1)
                    if s == 1:
                        dve.wait_ge(stored, 16 * stores_per_layer * (layer + 1))
                    link(v.tensor_scalar(m_q, pj(s, "mcq"), stat[:, 20:21], None, ALU.mult))
                    v.scalar_tensor_tensor(m_ckv, pj(s, "mckv"), stat[:, 21:22], kv_g[:], ALU.mult, ALU.mult)\
                        .then_inc(m_normed, 1)
                    dve.wait_ge(m_turned, n + 1)
                    for k in range(2):
                        link(v.tensor_scalar(m_qT[:, k, :], ps[:, 0, P * k:P * k + P], q_g[:, k:k + 1], None, ALU.mult))
                    v.tensor_copy(m_qT[:, 2:3 + s, :].rearrange("p a t -> p (a t)"), ps[:, 0, 2 * P:(3 + s) * P])\
                        .then_inc(m_kept, 1)
                    dve.wait_ge(m_up_done, n + 1)
                    if s == 1:
                        dve.wait_ge(roped, 3 * (layer + 1))
                    for t in range(1 + s):
                        kv = heads(ps[:, 2 + t, :], H)
                        link(v.tensor_copy(a_k[:, t, :, 0:64], kv[:, :, 0:64]))
                        link(v.tensor_copy(a_v[:, t], kv[:, :, 64:128]))
                        kr = pj(s, "mkr") if t == 0 else ctx_kr[:]
                        ins = v.tensor_copy(a_k[:, t, :, 64:96], mid(kr, H))
                        if s == 1:
                            link(ins)
                    if s == 1:
                        dve.wait_ge(m_q_kept, n + 1)
                        q1, q2 = a_q[:, :, 64:80], a_q[:, :, 80:96]
                        cos, sin = mid(c("cos32"), H), mid(c("sin32"), H)
                        qa, qb, qc, qd = (take(3200 + 64 * k, H, 16) for k in range(4))
                        link(v.tensor_tensor(qa, q1, cos, ALU.mult))
                        link(v.tensor_tensor(qb, q2, sin, ALU.mult))
                        link(v.tensor_tensor(qc, q1, sin, ALU.mult))
                        link(v.tensor_tensor(qd, q2, cos, ALU.mult))
                        link(v.tensor_tensor(q1, qa, qb, ALU.subtract))
                        ins = v.tensor_tensor(q2, qc, qd, ALU.add)
                    ins.then_inc(m_k_kept, 1)
                    for kind in range(2):
                        a = 2 * n + kind
                        dk, nh, scale, col = ((96, H, 96 ** -0.5, 256), (64, 2, 64 ** -0.5, 768))[kind]
                        dve.wait_ge(a_turned, a + 1)
                        for t in range(1 + s):
                            ins = v.tensor_copy(a_kT[0:dk, t, 0:nh, :].rearrange("p h t -> p (h t)"),
                                                ps[0:dk, 1 + t, 0:nh * P])
                            if t < s:
                                link(ins)
                        ins.then_inc(a_k_kept, 1)
                        dve.wait_ge(a_scores, a + 1)
                        sc = ps[:, 3:5, :].rearrange("p b (g k) -> p (b g) k", g=2)[:, :, 0:P * (1 + s)]
                        link(v.tensor_reduce(stat[:, 40:44], sc, AX, ALU.max))
                        if kind == 0:
                            v.tensor_scalar(stat[:, 24:28], stat[:, 40:44], -scale, None, ALU.mult).then_inc(a_shift, 1)
                        else:
                            link(v.scalar_tensor_tensor(stat[:, 40:44], stat[:, 40:44], scale, sink[:], ALU.mult, ALU.max))
                            link(v.tensor_scalar(stat[:, 24:28], stat[:, 40:44], -1.0, None, ALU.mult))
                            v.tensor_tensor(stat[:, 32:36], sink[:], stat[:, 40:44], ALU.subtract).then_inc(a_shift, 1)
                        if s == 1:
                            dve.wait_ge(a_p_turned, a + 1)
                            v.tensor_copy(a_pT[:, 1].rearrange("p h t -> p (h t)"), ps[:, 6, :]).then_inc(a_p1_kept, 1)
                        dve.wait_ge(a_out, a + 1)
                        if kind == 1:
                            link(v.tensor_tensor(stat[:, 28:32], stat[:, 28:32], stat[:, 36:40], ALU.add))
                        link(v.reciprocal(stat[:, 44:48], stat[:, 28:32]))
                        v.tensor_tensor(heads(mixed[:, col:col + 256], H), heads(ps[:, 7, 0:256], H), last(stat[:, 44:48], 64),
                                        ALU.mult).then_inc(a_mixed, 1)
                    dve.wait_ge(mix_turned, n + 1)
                    v.tensor_copy(hT[:, 4:8, P * s:P * s + P], ps[:, 1, :].rearrange("p (k t) -> p k t", k=4))\
                        .then_inc(mix_kept, 1)

                def add_to_x(y, gate, k):
                    flat = row[:].rearrange("p s n -> p (s n)")
                    link(v.tensor_tensor(flat, y, gates[:, gate].rearrange("p s n -> p (s n)"), ALU.mult))
                    v.tensor_tensor(x[:].rearrange("p s n -> p (s n)"), x[:].rearrange("p s n -> p (s n)"), flat, ALU.add)\
                        .then_inc(x_mixed, 1)
                    dve.wait_ge(x_mixed, k)

                dve.wait_ge(w_out_used, (KT // 2) * (layer + 1))
                dve.wait_ge(stored, 16 * stores_per_layer * (layer + 1))
                add_to_x(ps[:, 4:8, :].rearrange("p b n -> p (b n)"), 0, 2 * layer + 1)
                norm_rows(2 * layer + 1)
                norm_spread(2 * layer + 1)
                if layer % 2 == 0:
                    for blk in range(DENSE_BLOCKS):
                        dve.wait_ge(silu_ready, blk + 1)
                        if blk >= 4:
                            dve.wait_ge(down_done, blk - 3)
                        v.tensor_tensor(f_hid[:, blk % 4, :], f_sg[:, blk % 2, :], ps[:, 4 + blk % 4, 256:512], ALU.mult)\
                            .then_inc(hid_ready, 1)
                    dve.wait_ge(down_done, DENSE_BLOCKS)
                    add_to_x(ps[:, 0:4, :].rearrange("p b n -> p (b n)"), 1, 2 * layer + 2)
                else:
                    dve.wait_ge(logits_done, 1)
                    link(v.tensor_copy(t_logit.rearrange("p s e -> p (s e)"), ps[:, 4, 0:NS * E]))
                    for s in range(NS):
                        link(v.max(t_top[:, s, :], t_logit[:, s, :]))
                        link(v.max_index(route_i[:, s, :], t_top[:, s, :], t_logit[:, s, :]))
                    link(v.tensor_copy(t_idx, route_i[:]))
                    v.tensor_tensor(stat[:, 48:50], t_top[:, :, 1], t_top[:, :, 0], ALU.subtract).then_inc(route_top, 1)
                    dve.wait_ge(route_exp, 1)
                    link(v.tensor_scalar(stat[:, 52:54], stat[:, 50:52], 1.0, None, ALU.add))
                    link(v.reciprocal(stat[:, 52:54], stat[:, 52:54]))
                    link(v.tensor_tensor(stat[:, 54:56], stat[:, 50:52], stat[:, 52:54], ALU.mult))
                    link(v.memset(moe_m[:], 0.0))
                    link(v.memset(moe_w[:], 0.0))
                    iota = c("iota")
                    for s in range(NS):
                        first, second = t_idx[:, s, 0:1], t_idx[:, s, 1:2]
                        link(v.tensor_scalar(moe_m[:, s, 0:E], iota[:, 0:E], first, None, ALU.is_equal))
                        link(v.tensor_scalar(t_w[:, s, :], iota[:, 0:E], second, None, ALU.is_equal))
                        link(v.tensor_scalar(moe_w[:, s, 0:E], moe_m[:, s, 0:E], stat[:, 52 + s:53 + s], None, ALU.mult))
                        link(v.scalar_tensor_tensor(moe_w[:, s, 0:E], t_w[:, s, :], stat[:, 54 + s:55 + s], moe_w[:, s, 0:E],
                                                    ALU.mult, ALU.add))
                    v.tensor_tensor(moe_m[:, :, 0:E], moe_m[:, :, 0:E], t_w, ALU.add).then_inc(route_ready, 1)
                    dve.wait_ge(h_back, 1)
                    v.tensor_copy(row[:, 1, :], ps[:, 2:4, :].rearrange("p b n -> p (b n)")).then_inc(h_rows_dve, 1)
                    dve.wait_ge(places_done, 1)
                    link(v.memset(moe_pos[:], 0.0))
                    link(v.tensor_scalar(moe_pos[:, :, 0:E], ps[:, 5, 0:NS * E].rearrange("p (s e) -> p s e", s=NS),
                                         GLA_GATE_NORM, None, ALU.mult))
                    link(v.tensor_tensor(moe_pos[:, 1, 0:E], moe_pos[:, 1, 0:E], moe_m[:, 0, 0:E], ALU.add))
                    link(v.scalar_tensor_tensor(moe_spill[:], moe_pos[:, :, 0:E], float(CAP), moe_w[:, :, 0:E], ALU.is_ge, ALU.mult))
                    link(v.scalar_tensor_tensor(moe_pos[:], moe_pos[:], 1.0, moe_m[:], ALU.add, ALU.mult))
                    link(v.tensor_scalar(moe_pos[:], moe_pos[:], -1.0, None, ALU.add))
                    link(v.scalar_tensor_tensor(t_count, ps[:, 5, 2 * E:3 * E], GLA_GATE_NORM, moe_m[:, 0, 0:E],
                                                ALU.mult, ALU.add))
                    link(v.tensor_tensor(moe_count[:], t_count[0:1, :], moe_m[0:1, 1, 0:E], ALU.add))

                    def select(e):
                        for s in range(NS):
                            ins = v.tensor_scalar(sel[:, s, :], iota[:, 0:CAP], moe_pos[:, s, bass.ds(e, 1)], None,
                                                  ALU.is_equal)
                        ins.then_inc(sel_ready, 1)

                    def keep_gathered():
                        v.tensor_copy(e_h[:, 4:8, :], ps[:, 3, :].rearrange("p (k n) -> p k n", k=4)[:, :, 0:CAP])\
                            .then_inc(gathered_dve, 1)

                    select(0)
                    link(v.memset(sel_wT, 0.0))
                    v.memset(f_y, 0.0).then_inc(y_added, 1)
                    dve.wait_ge(gather_done, 1)
                    keep_gathered()
                    link(v.memset(e_y, 0.0))
                    v.memset(stat[:, 60:61], 0.0).then_inc(y_kept, 1)
                    dve.sem_inc(y_copied_dve, 1)
                    dve.sem_inc(sel_wT_ready, 1)
                    with dve.Fori(0, E) as e:
                        for u in range(UNITS):
                            for t in range(TILES):
                                i = TILES * u + t
                                dve.wait_ge(silu_ready, e * MOE_TILES + (DENSE_BLOCKS + i + 1))
                                v.tensor_tensor(e_hid[:, u % 2, t, :], e_sg[:, i % 3, :], ps[:, 4 + i % 3, P:2 * P], ALU.mult)\
                                    .then_inc(hid_ready, 1)
                                if u == 0 and t < NS:
                                    dve.wait_ge(scatter_done, e * 2 + (t + 1))
                                    dve.wait_ge(y_added, e * 2 + (t + 1))
                                    v.tensor_tensor(f_y[:, t, :], ps[:, 2:4, :].rearrange("p b n -> p (b n)"), f_y[:, t, :],
                                                    ALU.add).then_inc(y_added, 1)
                            if u == 1:
                                for s in range(NS):
                                    ins = v.tensor_scalar(sel_w[:, s, :], iota[:, 0:CAP], moe_pos[:, s, bass.ds(e, 1)],
                                                          moe_w[:, s, bass.ds(e, 1)], ALU.is_equal, ALU.mult)
                                ins.then_inc(sel_w_ready, 1)
                            if u == 4:
                                dve.wait_ge(sel_w_turned, e + 1)
                                v.tensor_copy(sel_wT[0:CAP], ps[0:CAP, 2, 0:NS * P].rearrange("p (s n) -> p s n", s=NS))\
                                    .then_inc(sel_wT_ready, 1)
                                select(e + 1)
                        dve.wait_ge(gather_done, e + 2)
                        keep_gathered()
                        dve.wait_ge(down_done, e * UNITS + (DENSE_BLOCKS + UNITS))
                        v.tensor_copy(e_y[0:CAP, HALF:D], ps[0:CAP, 1, :]).then_inc(y_copied_dve, 1)
                    for s in range(NS):
                        dve.wait_ge(scatter_done, 2 * E + s + 1)
                        dve.wait_ge(y_added, 2 * E + s + 1)
                        v.tensor_tensor(f_y[:, s, :], ps[:, 2:4, :].rearrange("p b n -> p (b n)"), f_y[:, s, :],
                                        ALU.add).then_inc(y_added, 1)
                    dve.wait_ge(y_added, 2 * E + 3)
                    dve.sem_inc(spill_hid, 1)
                    dve.sem_inc(spill_y, 1)
                    with dve.Fori(0, E) as e:
                        count = dve.value_load(moe_count[0:1, bass.ds(e, 1)], min_val=0, max_val=NS * P)
                        with dve.If(count > CAP):
                            for blk in range(SPILL_BLOCKS):
                                dve.wait_ge(spill_silu, e * SPILL_BLOCKS + (blk + 2))
                                dve.wait_ge(spill_down, e * SPILL_BLOCKS + (blk + 1))
                                v.tensor_tensor(s_hid, s_sg, ps[:, 4 + blk % 2, 256:512], ALU.mult).then_inc(spill_hid, 1)
                            dve.wait_ge(spill_down, e * SPILL_BLOCKS + (SPILL_BLOCKS + 1))
                            dve.wait_ge(spill_y, e * 2 + 1)
                            for s in range(NS):
                                v.scalar_tensor_tensor(f_y[:, s, :], ps[:, 2 * s:2 * s + 2, :].rearrange("p b n -> p (b n)"),
                                                       moe_spill[:, s, bass.ds(e, 1)], f_y[:, s, :], ALU.mult, ALU.add)\
                                    .then_inc(spill_y, 1)
                        with dve.Else():
                            dve.wait_ge(spill_hid, e * SPILL_BLOCKS + 1)
                            dve.wait_ge(spill_y, e * 2 + 1)
                            dve.sem_inc(spill_hid, SPILL_BLOCKS)
                            dve.sem_inc(spill_y, 2)
                    dve.wait_ge(spill_y, 2 * E + 1)
                    add_to_x(f_y.rearrange("p s n -> p (s n)"), 1, 2 * layer + 2)
            dve.wait_ge(final_g_in, 16)
            for s in range(NS):
                dve.wait_ge(sq_ready, 2 * NS * L + s + 1)
                v.tensor_scalar(stat[:, 2 + s:3 + s], stat[:, s:s + 1], 1.0 / D, EPS, ALU.mult, ALU.add).then_inc(var_ready, 1)
            for s in range(NS):
                dve.wait_ge(rstd_ready, 2 * NS * L + s + 1)
                v.scalar_tensor_tensor(row[:, s, :], x[:, s, :], stat[:, 4 + s:5 + s], final_g, ALU.mult, ALU.mult)\
                    .then_inc(final_ready, 1)


_OUTS = ["y_prompt", "y_sample", "new_state_gla", "new_state_ret", "new_cache_mla_ckv", "new_cache_mla_krope",
         "new_cache_gqa_k", "new_cache_gqa_v"]


def kernel(**inputs):
    import concourse.bacc as bacc
    from concourse.bass_utils import run_bass_kernel_spmd as run

    nc = bacc.Bacc("TRN2", target_bir_lowering=False, num_devices=1)
    arrays, io = {}, {}
    for name, a in list(inputs.items()) + [("constants", constant_table())]:
        a = np.ascontiguousarray(a)
        arrays[f"in_{name}"] = a
        io[name] = nc.dram_tensor(f"in_{name}", a.shape, mybir.dt.from_np(a.dtype), kind="ExternalInput").ap()
    b, t, d = inputs["x_prompt"].shape
    depth = inputs["w_in"].shape[0]
    shapes = dict(
        y_prompt=(b, t, d), y_sample=inputs["x_sample"].shape,
        new_state_gla=(b,) + inputs["state_gla"].shape[1:], new_state_ret=(b,) + inputs["state_ret"].shape[1:],
        new_cache_mla_ckv=(b, depth, t, inputs["cache_mla_ckv"].shape[-1]),
        new_cache_mla_krope=(b, depth, t, inputs["cache_mla_krope"].shape[-1]),
        new_cache_gqa_k=(b, depth, inputs["cache_gqa_k"].shape[2], t, inputs["cache_gqa_k"].shape[-1]),
        new_cache_gqa_v=(b, depth, inputs["cache_gqa_v"].shape[2], t, inputs["cache_gqa_v"].shape[-1]))
    for name in _OUTS:
        io[name] = nc.dram_tensor(f"out_{name}", shapes[name], F32, kind="ExternalOutput").ap()
    hybrid_step(nc, io)
    r = run(nc, [arrays], core_ids=[0])
    return tuple(r.results[0][f"out_{name}"] for name in _OUTS)
```

```python
from contextlib import ExitStack

import numpy as np

import concourse.bass as bass
from concourse import mybir

F32 = mybir.dt.float32
U32 = mybir.dt.uint32
I32 = mybir.dt.int32
ALU = mybir.AluOpType
ACT = mybir.ActivationFunctionType
AX = mybir.AxisListType.X

P = 128
NS = 2
EPS = 1e-6
GRID_W, ROPE_BASE = 64, 10000.0
GLA_GATE_NORM = 16.0
LEVELS = 7

WIDTHS = [("gq", 128), ("gk", 128), ("gv", 256), ("gog", 256), ("glr", 32), ("mcq", 256), ("mckv", 128),
          ("mkr", 32), ("rq", 256), ("rk", 256), ("rv", 256), ("rg", 256), ("aq", 256), ("ak", 128), ("av", 128)]
COL = {}
_at = 0
for _name, _w in WIDTHS:
    COL[_name] = (_at, _at + _w)
    _at += _w
IN_WIDTH = _at

CONSTS = [("ident", P), ("scan", 4 * P), ("dist", 2 * P), ("pos", 4), ("cos64", 32), ("sin64", 32), ("cos32", 16),
          ("sin32", 16), ("iota", P), ("masks", LEVELS * P), ("sum_qf", LEVELS * P), ("sum_qb", LEVELS * P),
          ("sum_kf", LEVELS * P), ("sum_kb", LEVELS * P)]
CCOL = {}
_at = 0
for _name, _w in CONSTS:
    CCOL[_name] = (_at, _at + _w)
    _at += _w
N_CONST = _at

PAGE = 2048
SLOTS = 9
FF = 2
MOE_SLOTS = 14
TILES = 3
CAP = 32 * TILES
FEW = 64


def constant_table():
    t = np.arange(P)
    out = np.zeros((P, N_CONST), np.float32)

    def put(name, a):
        lo, hi = CCOL[name]
        out[:, lo:hi] = np.asarray(a, np.float32).reshape(P, hi - lo)

    put("ident", np.eye(P))
    masks, sums = [], {"sum_qf": [], "sum_qb": [], "sum_kf": [], "sum_kb": []}
    u, i = t[:, None], t[None, :]
    for level in range(LEVELS):
        half = 64 >> level
        block = t // (2 * half)
        second = (t % (2 * half)) >= half
        masks.append((block[:, None] == block[None, :]) & (second[:, None] != second[None, :]))
        m, s2 = (block * 2 * half + half)[None, :], second[None, :]
        sums["sum_qf"].append(s2 & (u >= m) & (u <= i))
        sums["sum_qb"].append(~s2 & (u >= i) & (u < m))
        sums["sum_kf"].append(~s2 & (u > i) & (u < m))
        sums["sum_kb"].append(s2 & (u >= m) & (u < i))
    put("masks", np.stack(masks, 1))
    for name, a in sums.items():
        put(name, np.stack(a, 1) / GLA_GATE_NORM)
    put("scan", np.stack([u > i, u < i, u <= i, u >= i], 1) / GLA_GATE_NORM)
    put("dist", np.stack([np.maximum(i - u, 0), np.maximum(u - i, 0)], 1))
    put("pos", np.stack([P - 1 - t, t, t + 1, P - t], 1))
    rows, cols = (t // GRID_W).astype(np.float32), (t % GRID_W).astype(np.float32)
    for d in (64, 32):
        quarter = d // 4
        inv = np.power(np.float32(ROPE_BASE), -np.arange(quarter, dtype=np.float32) / np.float32(quarter))
        ang = np.concatenate([rows[:, None] * inv, cols[:, None] * inv], axis=1).astype(np.float32)
        put(f"cos{d}", np.cos(ang))
        put(f"sin{d}", np.sin(ang))
    put("iota", np.tile(t, (P, 1)))
    return out


def hybrid_step(nc, io):
    D = io["x_prompt"].shape[-1]
    L = io["w_in"].shape[0]
    KT = D // P
    D_FF = io["ffn_w_gate"].shape[-1]
    E, D_FFE = io["moe_w_gate"].shape[1], io["moe_w_gate"].shape[-1]
    H = 4
    HALF = D // 2
    IN_PAGES = -(-IN_WIDTH // 256)
    DENSE_UNITS = D_FF // (FF * P)
    SPILL_UNITS = D_FFE // (FF * P)
    DENSE_BLOCKS, SPILL_BLOCKS = DENSE_UNITS * FF, SPILL_UNITS * FF
    UNITS = D_FFE // 512
    MOE_PAGES = 6 * UNITS
    MOE_TILES = UNITS * TILES
    assert FEW == CAP - 32 and MOE_PAGES % MOE_SLOTS == 0 and MOE_TILES % 3 == 0

    pages = []

    def mod_pages(layer, third):
        return [("mod_bias", layer, third, 0)] + [("mod", layer, third, kt) for kt in range(KT)]

    for layer in range(L):
        if layer == 0:
            pages += mod_pages(layer, 0)
        pages += [("w_in", layer, c, 0) for c in range(IN_PAGES)]
        pages += mod_pages(layer, 1) + mod_pages(layer, 2)
        if layer + 1 < L:
            pages += mod_pages(layer + 1, 0)
        pages += [("w_out", layer, c, 0) for c in range(KT // 2)]
        if layer % 2 == 0:
            for u in range(DENSE_UNITS):
                pages += [("gate", layer, u, 0), ("up", layer, u, 0), ("down", layer, u, 0)]
    n_pages = len(pages)
    page_at = {key: n for n, key in enumerate(pages)}
    loads_before_moe = [len(range(s, n_pages, SLOTS)) if s < SLOTS else 0 for s in range(MOE_SLOTS)]
    LOADS = MOE_PAGES // MOE_SLOTS

    with ExitStack() as ctx:
        def sb(name, shape, dt=F32):
            return ctx.enter_context(nc.sbuf_tensor(name, shape, dt))

        def sem(name):
            return ctx.enter_context(nc.semaphore(name))

        arena = sb("arena", [P, SLOTS * PAGE + N_CONST + NS * IN_WIDTH + 2 * NS * D])
        at_const = SLOTS * PAGE
        at_proj = at_const + N_CONST
        at_gates = at_proj + NS * IN_WIDTH
        ring = arena[:, 0:at_const].rearrange("p (s n) -> p s n", s=SLOTS)
        const = arena[:, at_const:at_proj]
        proj = arena[:, at_proj:at_gates].rearrange("p (s n) -> p s n", s=NS)
        gates = arena[:, at_gates:].rearrange("p (g s n) -> p g s n", g=2, s=NS)
        at_tables = at_const + CCOL["masks"][0]
        moe_at = [PAGE * k for k in range(SLOTS)] + [at_tables, at_tables + PAGE, at_proj, at_proj + PAGE, at_gates]
        assert len(moe_at) == MOE_SLOTS and 2 * PAGE <= N_CONST - CCOL["masks"][0] and 2 * PAGE + D <= NS * IN_WIDTH
        final_g = arena[:, at_proj + 2 * PAGE:at_proj + 2 * PAGE + D]
        x = sb("x", [P, NS, D])
        hT = sb("hT", [P, KT, NS * P])
        row = sb("row", [P, NS, D])
        mixed = sb("mixed", [P, D])
        scratch = sb("scratch", [P, 5504])
        o_scratch = sb("o_scratch", [P, 4, 256])
        mod_row = sb("mod_row", [P, 2, 512])
        mod_T = sb("mod_T", [P, 4, KT, NS])
        scale_A = sb("scale_A", [P, 2, KT, NS])
        cond = sb("cond", [P, NS, KT])
        cond_raw = sb("cond_raw", [P, NS, KT])
        ones2 = sb("ones2", [1, 2])
        pick = sb("pick", [P, NS, P])
        stat = sb("stat", [P, 64])
        half_neg = sb("half_neg", [P, 4])
        gT = sb("gT", [P, 2, KT])
        q_g = sb("q_g", [P, 2])
        kv_g = sb("kv_g", [P, P])
        w_q_up = sb("w_q_up", [P, 2, 384])
        w_kv_up = sb("w_kv_up", [P, 512])
        w_lr = sb("w_lr", [33, 256])
        lrT = sb("lrT", [33, P])
        decay = sb("decay", [P, 2 * H])
        lg = sb("lg", [P, 2 * H])
        lg_abs = sb("lg_abs", [P, 2 * H])
        ret_pow = sb("ret_pow", [P, 4, H])
        ret_D = sb("ret_D", [P, H, P])
        sink = sb("sink", [P, H])
        ctx_ckv = sb("ctx_ckv", [P, P])
        ctx_kr = sb("ctx_kr", [P, 32])
        ctx_k = sb("ctx_k", [P, 2, 64])
        ctx_v = sb("ctx_v", [P, 2, 64])
        s0_gla = sb("s0_gla", [P, 2, 256])
        s0_ret = sb("s0_ret", [64, 2, H, 64])
        router = sb("router", [P, KT, E])
        moe_w = sb("moe_w", [P, NS, E + 1])
        moe_m = sb("moe_m", [P, NS, E + 1])
        moe_pos = sb("moe_pos", [P, NS, E + 1])
        moe_spill = sb("moe_spill", [P, NS, E])
        moe_count = sb("moe_count", [1, E], I32)
        moe_most = sb("moe_most", [1, 1], I32)
        route_i = sb("route_i", [P, NS, 8], U32)
        ps = ctx.enter_context(nc.psum_tensor("ps", [P, 8, 512], F32))

        def take(at, *shape):
            n = int(np.prod(shape))
            v = scratch[:, at:at + n]
            if len(shape) == 2:
                v = v.rearrange("p (a b) -> p a b", a=shape[0])
            if len(shape) == 3:
                v = v.rearrange("p (a b c) -> p a b c", a=shape[0], b=shape[1])
            return v

        g_x = take(0, 16, P)
        g_d = take(2048, 2, P)
        g_qT, g_kT = take(2304, 4, P), take(2816, 4, P)
        g_sT = take(3328, 2, P)
        g_att = take(3584, H, P)
        g_la = take(4608, 256)
        g_abs = take(4864, 256)
        r_qT, r_kT, r_att = take(0, H, P), take(512, H, P), take(1024, H, P)
        r_kd = take(1536, 2, 256)
        o_sum, o_tmp, o_sq, o_gate = (o_scratch[:, k, :] for k in range(4))
        rope_t = [row[:, 0, 256 * k:256 * k + 256] for k in range(4)]
        g_st = row[:, 1, 0:512].rearrange("p (d n) -> p d n", d=2)
        r_st = row[:, 1, 512:1024].rearrange("p (a n) -> p a n", a=2 * H)
        a_q, a_k, a_v = take(0, H, 96), take(384, 2, H, 96), take(1152, 2, H, 64)
        a_qT, a_kT = take(1664, H, P), take(2176, 2, H, P)
        a_p, a_pT = take(3200, H, 256), take(4224, 2, H, P)
        m_q, m_ckv = take(4224, 256), take(5376, P)
        m_qT = take(4608, 4, P)
        f_sg, f_hid = take(0, 2, 256), take(512, 4, 256)
        t_logit, t_top, t_idx = take(4096, NS, 8), take(4112, NS, 8), take(4128, NS, 8)
        t_w, t_count = take(4144, NS, 8), take(4160, 8)
        f_y = take(0, NS, D)
        e_h = take(2048, KT, CAP)
        e_sg = take(2048 + KT * CAP, 3, P)
        e_hid = take(2048 + KT * CAP + 384, 2, TILES, P)
        e_hidT = take(2048 + KT * CAP + 384 + 768, 4, CAP)
        e_y = take(2048 + KT * CAP + 384 + 768 + 384, D)
        sel = mixed[:, 0:NS * P].rearrange("p (s n) -> p s n", s=NS)[:, :, 0:CAP]
        sel_w = mixed[:, 256:256 + NS * P].rearrange("p (s n) -> p s n", s=NS)
        sel_wT = mixed[:, 512:512 + NS * P].rearrange("p (s n) -> p s n", s=NS)
        s_sg, s_hid = e_h.rearrange("p k n -> p (k n)")[:, 0:256], e_hid.rearrange("p a b c -> p (a b c)")[:, 0:256]

        def c(name):
            lo, hi = CCOL[name]
            return const[:, lo:hi]

        def pj(s, name):
            lo, hi = COL[name]
            return proj[:, s, lo:hi]

        def heads(v, n):
            return v.rearrange("p (h d) -> p h d", h=n)

        ident = c("ident")
        masks = c("masks").rearrange("p (l t) -> p l t", l=LEVELS)
        sum_qf, sum_qb, sum_kf, sum_kb = (c(f"sum_{k}").rearrange("p (l t) -> p l t", l=LEVELS)
                                          for k in ("qf", "qb", "kf", "kb"))
        scan = c("scan").rearrange("p (l t) -> p l t", l=4)
        dist = c("dist").rearrange("p (l t) -> p l t", l=2)

        def last(v, n):
            return v.unsqueeze(2).to_broadcast([v.shape[0], v.shape[1], n])

        def mid(v, n):
            return v.unsqueeze(1).to_broadcast([v.shape[0], n, v.shape[1]])

        loaded = [sem(f"page_loaded_{i}") for i in range(MOE_SLOTS)]
        const_in, x_in, params_in, final_g_in = sem("const_in"), sem("x_in"), sem("params_in"), sem("final_g_in")
        const_set = sem("const_set")
        cond_ready = sem("cond_ready")
        mod_bias_used, mod_used, w_in_used, w_out_used = (sem("mod_bias_used"), sem("mod_used"), sem("w_in_used"),
                                                          sem("w_out_used"))
        mod_rows, mod_turned, mod_kept, gate_spread, gate_kept = (sem("mod_rows"), sem("mod_turned"), sem("mod_kept"),
                                                                  sem("gate_spread"), sem("gate_kept"))
        cond_in, gains_in, scale_ready, x0_mixed = sem("cond_in"), sem("gains_in"), sem("scale_ready"), sem("x0_mixed")
        pick_ready, tables_in = sem("pick_ready"), sem("tables_in")
        ret_lg_abs, ret_exp, ret_lg, ret_dist, ret_ready = (sem("ret_lg_abs"), sem("ret_exp"), sem("ret_lg"), sem("ret_dist"),
                                                   sem("ret_ready"))
        ret_D_ready = sem("ret_D_ready")
        sq_ready, var_ready, rstd_ready, xn_ready, xT_done, h_ready, h_ready_act = (
            sem("sq_ready"), sem("var_ready"), sem("rstd_ready"), sem("xn_ready"), sem("xT_done"), sem("h_ready"),
            sem("h_ready_act"))
        proj_done, proj_act, proj_dve = sem("proj_done"), sem("proj_act"), sem("proj_dve")
        roped = sem("roped")
        lr_turned, lr_kept, lr_done, lr_abs, lr_soft, la_ready = (sem("lr_turned"), sem("lr_kept"), sem("lr_done"),
                                                                  sem("lr_abs"), sem("lr_soft"), sem("la_ready"))
        sums_done, decays_ready, decayed = sem("sums_done"), sem("decays_ready"), sem("decayed")
        g_turned, g_q_kept, g_k_kept, g_att_done, g_att_kept = (sem("g_turned"), sem("g_q_kept"), sem("g_k_kept"),
                                                                sem("g_att_done"), sem("g_att_kept"))
        ext_turned, ext_kept = sem("ext_turned"), sem("ext_kept")
        g_out_done, g_state_kept = sem("g_out_done"), sem("g_state_kept")
        o_kept, o_sq_ready, o_gate_exp, o_var, o_rstd, o_mixed = (sem("o_kept"), sem("o_sq_ready"), sem("o_gate_exp"),
                                                                  sem("o_var"), sem("o_rstd"), sem("o_mixed"))
        r_turned, r_q_kept, r_k_kept, r_scores, r_att_kept, r_out_done, r_state_kept = (
            sem("r_turned"), sem("r_q_kept"), sem("r_k_kept"), sem("r_scores"), sem("r_att_kept"), sem("r_out_done"),
            sem("r_state_kept"))
        m_sq, m_var, m_rstd, m_normed, m_turned, m_kept, m_up_done, m_q_kept, m_k_kept = (
            sem("m_sq"), sem("m_var"), sem("m_rstd"), sem("m_normed"), sem("m_turned"), sem("m_kept"),
            sem("m_up_done"), sem("m_q_kept"), sem("m_k_kept"))
        a_turned, a_q_kept, a_k_kept, a_scores, a_shift, a_probs, a_p_turned, a_p0_kept, a_p1_kept, a_out, a_mixed = (
            sem("a_turned"), sem("a_q_kept"), sem("a_k_kept"), sem("a_scores"), sem("a_shift"), sem("a_probs"),
            sem("a_p_turned"), sem("a_p0_kept"), sem("a_p1_kept"), sem("a_out"), sem("a_mixed"))
        mix_turned, mix_kept, mix_kept_act, x_mixed = sem("mix_turned"), sem("mix_kept"), sem("mix_kept_act"), sem("x_mixed")
        logits_done, route_top, route_exp, route_ready = (sem("logits_done"), sem("route_top"), sem("route_exp"),
                                                          sem("route_ready"))
        gu_done, silu_ready, hid_ready, down_done, y_kept = (sem("gu_done"), sem("silu_ready"), sem("hid_ready"),
                                                             sem("down_done"), sem("y_kept"))
        h_back, h_rows_act, h_rows_dve, places_done = (sem("h_back"), sem("h_rows_act"), sem("h_rows_dve"),
                                                       sem("places_done"))
        sel_ready, sel_w_ready, sel_w_turned, sel_wT_ready, gather_done, gathered_act, gathered_dve = (
            sem("sel_ready"), sem("sel_w_ready"), sem("sel_w_turned"), sem("sel_wT_ready"), sem("gather_done"),
            sem("gathered_act"), sem("gathered_dve"))
        hid_turned, hidT_ready, y_copied_act, y_copied_dve, scatter_done, y_added = (
            sem("hid_turned"), sem("hidT_ready"), sem("y_copied_act"), sem("y_copied_dve"), sem("scatter_done"),
            sem("y_added"))
        spill_loaded = [sem("spill_loaded_0"), sem("spill_loaded_1")]
        spill_gu, spill_silu, spill_hid, spill_down, spill_y = (sem("spill_gu"), sem("spill_silu"), sem("spill_hid"),
                                                                sem("spill_down"), sem("spill_y"))
        stored = sem("stored")
        final_ready, finished = sem("final_ready"), sem("finished")
        dve_step, act_step, pool_step = sem("dve_step"), sem("act_step"), sem("pool_step")
        stores_per_layer = 2 * H + 1 + 4
        N_PARAMS = 12 + 2 * H + 1

        def slot_of(key):
            return page_at[key] % SLOTS

        def page(key):
            return ring[:, slot_of(key), :]

        def wait_page(eng, key):
            n = page_at[key]
            eng.wait_ge(loaded[n % SLOTS], 16 * (n // SLOTS + 1))

        def spill_if_any(eng):
            return eng.If(eng.value_load(moe_most[:], min_val=0, max_val=NS * P) > CAP)

        def few_or_all(eng, e, expert):
            count = eng.value_load(moe_count[0:1, bass.ds(e, 1)], min_val=0, max_val=NS * P)
            with eng.If(count > FEW):
                expert(TILES)
            with eng.Else():
                expert(TILES - 1)

        def y_rows(tiles):
            return CAP if tiles == TILES else 2 * FEW

        def steps_of(t, tiles):
            return 1 if t < tiles - 1 else TILES - t

        block = ctx.enter_context(nc.Block())

        @block.sync
        def _(sp):
            def source(key):
                kind, layer, i, kt = key
                if kind == "mod_bias":
                    return io["b_mod"][layer:layer + 1, i * PAGE:(i + 1) * PAGE]
                if kind == "mod":
                    return io["w_mod"][layer, kt * P:(kt + 1) * P, i * PAGE:(i + 1) * PAGE]
                if kind == "w_in":
                    w = min(256, IN_WIDTH - 256 * i)
                    return io["w_in"][layer].rearrange("(k p) n -> p k n", p=P)[:, :, 256 * i:256 * i + w]
                if kind == "w_out":
                    return io["w_out"][layer].rearrange("(k p) n -> p k n", p=P)[:, 2 * i:2 * i + 2, :]
                if kind == "down":
                    return io["ffn_w_down"][layer // 2].rearrange("(b p) n -> p b n", p=P)[:, FF * i:FF * i + FF, :]
                w = io["ffn_w_gate" if kind == "gate" else "ffn_w_up"]
                return w[layer // 2].rearrange("(k p) n -> p k n", p=P)[:, :, 256 * i:256 * i + 256]

            def target(key):
                kind, _, i, _ = key
                if kind == "mod_bias":
                    return page(key)[0:1, :]
                if kind == "mod":
                    return page(key)
                if kind in ("w_out", "down"):
                    return page(key).rearrange("p (b n) -> p b n", b=2)
                w = min(256, IN_WIDTH - 256 * i) if kind == "w_in" else 256
                return page(key).rearrange("p (k n) -> p k n", k=KT)[:, :, 0:w]

            def wait_used(key):
                kind, layer, i, kt = key
                if kind == "mod_bias":
                    sp.wait_ge(mod_bias_used, 3 * layer + i + 1)
                elif kind == "mod":
                    sp.wait_ge(mod_used, KT * (3 * layer + i) + kt + 1)
                elif kind == "w_in":
                    sp.wait_ge(w_in_used, IN_PAGES * layer + i + 1)
                elif kind == "w_out":
                    sp.wait_ge(w_out_used, (KT // 2) * layer + i + 1)
                elif kind == "down":
                    sp.wait_ge(down_done, FF * (i + 1))
                else:
                    sp.wait_ge(gu_done, FF * (i + 1))

            for n, key in enumerate(pages):
                if n >= SLOTS:
                    wait_used(pages[n - SLOTS])
                sp.dma_start(target(key), source(key)).then_inc(loaded[n % SLOTS], 16)

            gate_v = io["moe_w_gate"][0].rearrange("e (k p) n -> e p k n", p=P)
            up_v = io["moe_w_up"][0].rearrange("e (k p) n -> e p k n", p=P)
            down_v = io["moe_w_down"][0].rearrange("e (b p) n -> e p b n", p=P)

            def expert_source(e, kind, i):
                if kind == "down":
                    return down_v[bass.ds(e, 1), :, FF * i:FF * i + FF, :].rearrange("e p b n -> p (e b) n")
                w = gate_v if kind == "gate" else up_v
                return w[bass.ds(e, 1), :, :, 256 * i:256 * i + 256].rearrange("e p k n -> p (e k) n")

            def load_expert_page(e, j):
                u, k = j // 6, j % 6
                at = moe_at[j % MOE_SLOTS]
                if k >= 4:
                    dst, src = 2, expert_source(e, "down", 2 * u + k - 4)
                else:
                    w, half = (gate_v, up_v)[k % 2], slice(KT // 2 * (k // 2), KT // 2 * (k // 2 + 1))
                    dst, src = KT // 2, w[bass.ds(e, 1), :, half, 512 * u:512 * u + 512].rearrange("e p k n -> p (e k) n")
                sp.dma_start(arena[:, at:at + PAGE].rearrange("p (b n) -> p b n", b=dst), src)\
                    .then_inc(loaded[j % MOE_SLOTS], 16)

            def wait_expert_page_used(e, j):
                u = j // 6
                if j % 6 >= 4:
                    sp.wait_ge(down_done, e * UNITS + (DENSE_BLOCKS + u + 1))
                else:
                    sp.wait_ge(gu_done, e * MOE_TILES + (DENSE_BLOCKS + TILES * (u + 1)))

            for j in range(MOE_SLOTS):
                if j < SLOTS:
                    wait_used([pages[n] for n in range(j, n_pages, SLOTS)][-1])
                elif j == SLOTS:
                    sp.wait_ge(x_mixed, 2 * L - 1)
                load_expert_page(0, j)
            with sp.Fori(0, E - 1) as e:
                for j in range(MOE_SLOTS, MOE_PAGES):
                    wait_expert_page_used(e, j - MOE_SLOTS)
                    load_expert_page(e, j)
                for j in range(MOE_SLOTS):
                    wait_expert_page_used(e, MOE_PAGES - MOE_SLOTS + j)
                    load_expert_page(e + 1, j)
            for j in range(MOE_SLOTS, MOE_PAGES):
                wait_expert_page_used(E - 1, j - MOE_SLOTS)
                load_expert_page(E - 1, j)
            sp.wait_ge(gu_done, DENSE_BLOCKS + E * MOE_TILES)
            sp.wait_ge(down_done, DENSE_BLOCKS + E * UNITS)
            sp.wait_ge(y_added, 2 * E + 3)
            with spill_if_any(sp):
                with sp.Fori(0, E) as e:
                    count = sp.value_load(moe_count[0:1, bass.ds(e, 1)], min_val=0, max_val=NS * P)
                    with sp.If(count > CAP):
                        for u in range(SPILL_UNITS):
                            sp.wait_ge(spill_down, e * SPILL_BLOCKS + max(1, 1 + FF * (u - 1)))
                            for k, kind in enumerate(("gate", "up", "down")):
                                at = PAGE * (3 * (u % 2) + k)
                                dst = arena[:, at:at + PAGE].rearrange("p (b n) -> p b n", b=2 if kind == "down" else KT)
                                sp.dma_start(dst, expert_source(e, kind, u)).then_inc(spill_loaded[u % 2], 16)
                    with sp.Else():
                        sp.wait_ge(spill_down, e * SPILL_BLOCKS + 1)
                        for half in range(2):
                            sp.sem_inc(spill_loaded[half], 16 * 3 * SPILL_UNITS // 2)
            for s, name in enumerate(("y_prompt", "y_sample")):
                sp.wait_ge(final_ready, s + 1)
                sp.dma_start(io[name][0], row[:, s, :]).then_inc(finished, 16)
            sp.wait_ge(finished, 32)

        @block.gpsimd
        def _(pool):
            g = nc.gpsimd
            steps = [0]

            def link(ins):
                steps[0] += 1
                ins.then_inc(pool_step, 1)
                pool.wait_ge(pool_step, steps[0])

            with nc.allow_non_contiguous_dma(reason="vectors of one number per partition"):
                pool.dma_start(cond_raw[:, 0, :], io["c_ctx"].rearrange("(k p) -> p k", p=P)).then_inc(cond_in, 16)
                pool.dma_start(cond_raw[:, 1, :], io["c"][0].rearrange("(k p) -> p k", p=P)).then_inc(cond_in, 16)
            table = CCOL["scan"][0]
            pool.dma_start(x[:, 0, :], io["x_prompt"][0]).then_inc(x_in, 16)
            pool.dma_start(x[:, 1, :], io["x_sample"][0]).then_inc(x_in, 16)
            pool.dma_start(const[:, 0:table], io["constants"][:, 0:table]).then_inc(const_in, 16)
            for k, (dst, value) in enumerate([(mod_row[:], 0.0), (s0_gla[:], 0.0), (w_lr[:], 0.0), (lrT[32:33, :], 1.0),
                                              (half_neg[:], -0.5), (ones2[:], 1.0)]):
                g.memset(dst, value).then_inc(const_set, 1)
                pool.wait_ge(const_set, k + 1)

            def load_gains(layer):
                with nc.allow_non_contiguous_dma(reason="vectors of one number per partition"):
                    for k, name in enumerate(("norm1_g", "norm2_g")):
                        pool.dma_start(gT[:, k, :], io[name][layer].rearrange("(k p) -> p k", p=P)).then_inc(gains_in, 16)
                pool.dma_start(decay[:], io["ret_decay"][layer:layer + 1].rearrange("l d h -> l (d h)").to_broadcast([P, 2 * H]))\
                    .then_inc(gains_in, 16)

            def rstd(m):
                for s in range(NS):
                    pool.wait_ge(var_ready, NS * m + s + 1)
                    g.tensor_tensor(stat[:, 4 + s:5 + s], stat[:, 2 + s:3 + s], half_neg[:, 0:1],
                                    ALU.pow).then_inc(rstd_ready, 1)

            def load_params(layer):
                def ld(dst, src):
                    pool.dma_start(dst, src).then_inc(params_in, 16)
                with nc.allow_non_contiguous_dma(reason="vectors of one number per partition"):
                    ld(q_g[:], io["mla_q_norm_g"][layer].rearrange("(k p) -> p k", p=P))
                ld(kv_g[:], io["mla_kv_norm_g"][layer:layer + 1, :].to_broadcast([P, P]))
                ld(w_q_up[:], io["mla_w_q_up"][layer].rearrange("(k p) n -> p k n", p=P))
                ld(w_kv_up[:], io["mla_w_kv_up"][layer])
                ld(w_lr[0:16, 0:128], io["gla_gate_w"][layer, 0])
                ld(w_lr[16:32, 128:256], io["gla_gate_w"][layer, 1])
                ld(w_lr[32:33, :], io["gla_gate_b"][layer:layer + 1].rearrange("l d n -> l (d n)"))
                ld(sink[:], io["gqa_sink"][layer:layer + 1, :].to_broadcast([P, H]))
                ld(ctx_ckv[:], io["cache_mla_ckv"][0, layer])
                ld(ctx_kr[:], io["cache_mla_krope"][0, layer])
                ld(ctx_k[:], io["cache_gqa_k"][0, layer].rearrange("h t d -> t h d"))
                ld(ctx_v[:], io["cache_gqa_v"][0, layer].rearrange("h t d -> t h d"))
                for d in range(2):
                    for h in range(H):
                        ld(s0_gla[32 * h:32 * h + 32, d, 64 * h:64 * h + 64], io["state_gla"][0, layer, d, h])
                ld(s0_ret[:].rearrange("k d h v -> k (d h) v"), io["state_ret"][0, layer].rearrange("d h k v -> k (d h) v"))

            def rope(v, n, d):
                x1, x2 = v[:, :, 0:d // 2], v[:, :, d // 2:d]
                cos, sin = mid(c(f"cos{d}"), n), mid(c(f"sin{d}"), n)
                ta, tb, tc, td = (r[:, 0:n * d // 2].rearrange("p (h d) -> p h d", h=n) for r in rope_t)
                link(g.tensor_tensor(ta, x1, cos, ALU.mult))
                link(g.tensor_tensor(tb, x2, sin, ALU.mult))
                link(g.tensor_tensor(tc, x1, sin, ALU.mult))
                link(g.tensor_tensor(td, x2, cos, ALU.mult))
                link(g.tensor_tensor(x1, ta, tb, ALU.subtract))
                return g.tensor_tensor(x2, tc, td, ALU.add)

            load_gains(0)
            pool.dma_start(const[:, table:], io["constants"][:, table:]).then_inc(tables_in, 16)
            rstd(0)
            load_params(0)
            pool.dma_start(router[:], io["moe_router"][0].rearrange("(k p) e -> p k e", p=P)).then_inc(params_in, 16)

            for layer in range(L):
                if layer:
                    pool.wait_ge(x_mixed, 2 * layer - 1)
                    pool.wait_ge(stored, 16 * stores_per_layer * layer)
                    load_gains(layer)
                    load_params(layer)
                    rstd(2 * layer)
                pool.wait_ge(proj_act, (IN_PAGES + 1) // 2 * (layer + 1))
                pool.wait_ge(proj_dve, IN_PAGES // 2 * (layer + 1))

                def store(dst, src):
                    pool.dma_start(dst, src).then_inc(stored, 16)
                store(io["new_cache_mla_krope"][0, layer], pj(0, "mkr"))
                store(io["new_cache_gqa_k"][0, layer].rearrange("h t d -> t h d"), heads(pj(0, "ak"), 2))
                store(io["new_cache_gqa_v"][0, layer].rearrange("h t d -> t h d"), heads(pj(0, "av"), 2))

                def latent_rstd(n):
                    pool.wait_ge(m_var, n + 1)
                    g.tensor_tensor(stat[:, 20:22], stat[:, 18:20], half_neg[:, 0:2], ALU.pow).then_inc(m_rstd, 1)
                latent_rstd(NS * layer)
                pool.wait_ge(m_normed, NS * layer + 1)
                store(io["new_cache_mla_ckv"][0, layer], m_ckv)
                pool.wait_ge(tables_in, 16)
                rope(proj[:, 1, COL["rq"][0]:COL["rk"][1]].rearrange("p (h d) -> p h d", h=8), 8, 64).then_inc(roped, 1)
                pool.wait_ge(roped, 3 * layer + 1)
                rope(proj[:, 1, COL["aq"][0]:COL["ak"][1]].rearrange("p (h d) -> p h d", h=6), 6, 64).then_inc(roped, 1)
                pool.wait_ge(roped, 3 * layer + 2)
                rope(heads(pj(1, "mkr"), 1), 1, 32).then_inc(roped, 1)
                for s in range(NS):
                    n = NS * layer + s

                    def o_power(k):
                        pool.wait_ge(o_var, k + 1)
                        g.tensor_tensor(stat[:, 12:16], stat[:, 8:12], half_neg[:], ALU.pow).then_inc(o_rstd, 1)
                    if s == 1:
                        latent_rstd(n)
                    if s == 0:
                        pool.wait_ge(g_state_kept, layer + 1)
                        for d in range(2):
                            for h in range(H):
                                store(io["new_state_gla"][0, layer, d, h],
                                      g_st[32 * h:32 * h + 32, d, 64 * h:64 * h + 64])
                    o_power(2 * n)
                    if s == 0:
                        pool.wait_ge(r_state_kept, layer + 1)
                        store(io["new_state_ret"][0, layer].rearrange("d h k v -> k (d h) v"), r_st[0:64, :, :])
                    o_power(2 * n + 1)
                rstd(2 * layer + 1)
            pool.wait_ge(x_mixed, 2 * L - 1)
            pool.dma_start(final_g, io["final_norm_g"].rearrange("(a d) -> a d", a=1).to_broadcast([P, D]))\
                .then_inc(final_g_in, 16)
            rstd(2 * L)
            pool.wait_ge(stored, 16 * stores_per_layer * L)

        @block.tensor
        def _(pe):
            mm, turn = nc.tensor.matmul, nc.tensor.transpose

            def mod_steps(i, lo, hi):
                layer, third = i // 3, i % 3
                for step in range(lo, hi):
                    if step == 0:
                        if i:
                            pe.wait_ge(mod_kept, i)
                        key, left = ("mod_bias", layer, third, 0), ones2[:]
                    else:
                        key, left = ("mod", layer, third, step - 1), cond[:, :, step - 1]
                    wait_page(pe, key)
                    for q in range(4):
                        right = page(key)[0:1, 512 * q:512 * q + 512] if step == 0 else page(key)[:, 512 * q:512 * q + 512]
                        ins = mm(ps[32 * q:32 * q + 2, 7, :], left, right, start=(step == 0), stop=(step == KT))
                    ins.then_inc(mod_used if step else mod_bias_used, 1)

            def mod_turn(i):
                pe.wait_ge(mod_rows, i + 1)
                for j in range(4):
                    ins = turn(ps[:, 7, P * j:P * j + P], mod_row[:, 0, P * j:P * j + P], ident)
                ins.then_inc(mod_turned, 1)

            def spread_gate(layer, g):
                if g:
                    pe.wait_ge(gate_kept, 2 * layer + 1)
                for half in range(2):
                    q = 2 * g + half
                    for s in range(NS):
                        ins = mm(ps[:, 2 * s + half, :], pick[32 * q:32 * q + 2, s, :], mod_row[32 * q:32 * q + 2, 1, :],
                                 start=True, stop=True)
                ins.then_inc(gate_spread, 1)

            def mixer_mod_steps(layer, s, lo, hi):
                if s == 0:
                    mod_steps(3 * layer + 1, lo, hi)
                elif layer + 1 < L:
                    mod_steps(3 * layer + 3, lo, hi)

            def norm_turn(m):
                for s in range(NS):
                    pe.wait_ge(xn_ready, NS * m + s + 1)
                    if m % 2:
                        pe.wait_ge(gate_kept, m + 1)
                    for kt in range(KT):
                        ins = turn(ps[:, 2 * s + kt // 4, P * (kt % 4):P * (kt % 4) + P], row[:, s, P * kt:P * kt + P], ident)
                    ins.then_inc(xT_done, 1)

            def project(layer):
                pe.wait_ge(h_ready, 2 * layer + 1)
                pe.wait_ge(h_ready_act, 2 * layer + 1)
                for i in range(IN_PAGES):
                    key = ("w_in", layer, i, 0)
                    wait_page(pe, key)
                    w = min(256, IN_WIDTH - 256 * i)
                    b = page(key).rearrange("p (k n) -> p k n", k=KT)
                    if i >= 4:
                        if i % 2 == 0:
                            pe.wait_ge(proj_act, (IN_PAGES + 1) // 2 * layer + (i - 4) // 2 + 1)
                        else:
                            pe.wait_ge(proj_dve, IN_PAGES // 2 * layer + (i - 4) // 2 + 1)
                    for s in range(NS):
                        for kt in range(KT):
                            ins = mm(ps[:, 4 + i % 4, 256 * s:256 * s + w], hT[:, kt, P * s:P * s + P], b[:, kt, 0:w],
                                     start=(kt == 0), stop=(kt == KT - 1))
                    ins.then_inc(w_in_used, 1)

            def gla(layer, s):
                n = NS * layer + s
                turn(ps[0:32, 0, 0:P], pj(s, "glr"), ident).then_inc(lr_turned, 1)
                if s == 1:
                    mod_steps(3 * layer + 2, 2, 4)
                pe.wait_ge(lr_kept, n + 1)
                mm(ps[:, 1, 0:256], lrT[:], w_lr[:], start=True, stop=True).then_inc(lr_done, 1)
                if s == 1:
                    mod_steps(3 * layer + 2, 4, KT + 1)
                else:
                    mixer_mod_steps(layer, s, 0, 3)
                pe.wait_ge(la_ready, n + 1)
                la_f, la_b = g_la[:, 0:P], g_la[:, P:2 * P]
                for level in range(LEVELS):
                    b, o = 2 + level // 4, P * (level % 4)
                    for to, fwd, bwd in ((b, sum_qf, sum_qb), (b + 2, sum_kf, sum_kb)):
                        mm(ps[:, to, o:o + P], fwd[:, level, :], la_f, start=True, stop=False)
                        mm(ps[:, to, o:o + P], bwd[:, level, :], la_b, start=False, stop=True)
                mm(ps[:, 3, 3 * P:], scan[:, 2 * s, :], la_f, start=True, stop=True)
                mm(ps[:, 5, 3 * P:], scan[:, 2 * s + 1, :], la_b, start=True, stop=True).then_inc(sums_done, 1)
                if s == 0:
                    mixer_mod_steps(layer, s, 3, 6)
                else:
                    mod_turn(3 * layer + 2)
                pe.wait_ge(decayed, n + 1)
                for r in range(2):
                    for j in range(4):
                        level = 4 * r + j
                        q_l = g_x[:, level, :] if level < LEVELS else g_d[:, 0, :]
                        k_l = g_x[:, 8 + level, :] if level < LEVELS else g_d[:, 1, :]
                        turn(ps[:, 0, P * j:P * j + P], q_l, ident)
                        ins = turn(ps[:, 1, P * j:P * j + P], k_l, ident)
                    ins.then_inc(g_turned, 1)
                    pe.wait_ge(g_q_kept, 2 * n + r + 1)
                    pe.wait_ge(g_k_kept, 2 * n + r + 1)
                    if r == 1:
                        pe.wait_ge(g_att_kept, 2 * n + 1)
                    for h in range(H):
                        for j in range(4):
                            ins = mm(ps[:, 2 + h, P * j:P * j + P], g_kT[32 * h:32 * h + 32, j, :],
                                     g_qT[32 * h:32 * h + 32, j, :], start=True, stop=True, tile_position=(32 * h, 0))
                    ins.then_inc(g_att_done, 1)
                gv = pj(s, "gv")
                if s == 1:
                    for d in range(2):
                        ins = turn(ps[:, 0, P * d:P * d + P], g_x[:, 7 + 8 * d, :], ident)
                    ins.then_inc(ext_turned, 1)
                mixer_mod_steps(layer, s, *((6, 8) if s == 0 else (0, 3)))
                pe.wait_ge(g_att_kept, 2 * n + 2)
                if s == 0:
                    for d in range(2):
                        mm(ps[:, 5, 256 * d:256 * d + 256], g_x[:, 7 + 8 * d, :], gv, start=True, stop=True)
                for h in range(H):
                    ins = mm(ps[:, 6, 64 * h:64 * h + 64], g_att[:, h, :], gv[:, 64 * h:64 * h + 64],
                             start=(s == 0 or h == 0), stop=(s == 0), skip_group_check=True)
                if s == 1:
                    pe.wait_ge(ext_kept, layer + 1)
                    for d in range(2):
                        ins = mm(ps[:, 6, 0:256], g_sT[:, d, :], s0_gla[:, d, :], start=False, stop=(d == 1),
                                 skip_group_check=True)
                ins.then_inc(g_out_done, 1)

            def retention_scores(layer, s):
                n = NS * layer + s
                if s == 1:
                    pe.wait_ge(roped, 3 * layer + 1)
                for h in range(H):
                    turn(ps[0:64, 0, P * h:P * h + P], pj(s, "rq")[:, 64 * h:64 * h + 64], ident)
                    ins = turn(ps[0:64, 1, P * h:P * h + P], pj(s, "rk")[:, 64 * h:64 * h + 64], ident)
                ins.then_inc(r_turned, 1)
                pe.wait_ge(r_q_kept, n + 1)
                pe.wait_ge(r_k_kept, n + 1)
                for h in range(H):
                    ins = mm(ps[:, 2, P * h:P * h + P], r_kT[0:64, h, :], r_qT[0:64, h, :], start=True, stop=True)
                ins.then_inc(r_scores, 1)

            def mla_turn(layer, s):
                n = NS * layer + s
                pe.wait_ge(m_normed, n + 1)
                turn(ps[:, 0, 0:P], m_q[:, 0:P], ident)
                turn(ps[:, 0, P:2 * P], m_q[:, P:2 * P], ident)
                ins = turn(ps[:, 0, 2 * P:3 * P], m_ckv, ident)
                if s == 1:
                    ins = turn(ps[:, 0, 3 * P:], ctx_ckv[:], ident)
                ins.then_inc(m_turned, 1)

            def retention_out(layer, s):
                n = NS * layer + s
                rv = pj(s, "rv")
                if s == 1:
                    mixer_mod_steps(layer, s, 3, 4)
                pe.wait_ge(r_att_kept, n + 1)
                for h in range(H):
                    mm(ps[:, 6, 64 * h:64 * h + 64], r_att[:, h, :], rv[:, 64 * h:64 * h + 64], start=True, stop=True)
                for d in range(2):
                    for h in range(H):
                        o = 256 * d + 64 * h
                        if s == 1:
                            ins = mm(ps[:, 3, o:o + 64], r_qT[0:64, h, :], s0_ret[:, d, h, :], start=True, stop=True)
                        else:
                            ins = mm(ps[0:64, 3, o:o + 64], r_kd[:, d, 64 * h:64 * h + 64], rv[:, 64 * h:64 * h + 64],
                                     start=True, stop=True)
                ins.then_inc(r_out_done, 1)

            def mla_up(layer, s):
                n = NS * layer + s
                pe.wait_ge(m_kept, n + 1)
                for k in range(2):
                    mm(ps[:, 1, 0:384], m_qT[:, k, :], w_q_up[:, k, :], start=(k == 0), stop=(k == 1))
                ins = mm(ps[:, 2, :], m_qT[:, 2, :], w_kv_up[:], start=True, stop=True)
                if s == 1:
                    ins = mm(ps[:, 4, :], m_qT[:, 3, :], w_kv_up[:], start=True, stop=True)
                ins.then_inc(m_up_done, 1)

            def attention(layer, s, kind):
                n = NS * layer + s
                a = 2 * n + kind
                nk = 1 + s
                if kind == 0:
                    if s == 1:
                        mixer_mod_steps(layer, s, 4, 7)
                    pe.wait_ge(m_q_kept, n + 1)
                    pe.wait_ge(m_k_kept, n + 1)
                    dk, q = 96, a_q
                    k, nh = [a_k[:, t] for t in range(nk)], H
                    v = [a_v[:, t] for t in range(nk)]
                else:
                    pe.wait_ge(a_mixed, 2 * n + 1)
                    if s == 1:
                        pe.wait_ge(roped, 3 * layer + 2)
                    dk, q = 64, heads(pj(s, "aq"), H)
                    k, nh = [heads(pj(s, "ak"), 2), ctx_k[:]][:nk], 2
                    v = [heads(pj(s, "av"), 2), ctx_v[:]][:nk]
                for h in range(H):
                    ins = turn(ps[0:dk, 0, P * h:P * h + P], q[:, h, :], ident)
                for t in range(nk):
                    for h in range(nh):
                        ins = turn(ps[0:dk, 1 + t, P * h:P * h + P], k[t][:, h, :], ident)
                ins.then_inc(a_turned, 1)
                pe.wait_ge(a_q_kept, a + 1)
                pe.wait_ge(a_k_kept, a + 1)
                for h in range(H):
                    for t in range(nk):
                        o = 256 * (h % 2) + P * t
                        ins = mm(ps[:, 3 + h // 2, o:o + P], a_qT[0:dk, h, :], a_kT[0:dk, t, h * nh // H, :],
                                 start=True, stop=True)
                ins.then_inc(a_scores, 1)
                if kind == 0:
                    mixer_mod_steps(layer, s, 8 if s == 0 else 7, KT + 1)
                elif s == 0:
                    mod_turn(3 * layer + 1)
                elif layer + 1 < L:
                    mod_turn(3 * layer + 3)
                pe.wait_ge(a_probs, a + 1)
                for t in range(nk):
                    for h in range(H):
                        ins = turn(ps[:, 5 + t, P * h:P * h + P], a_p[:, h, P * t:P * t + P], ident)
                ins.then_inc(a_p_turned, 1)
                pe.wait_ge(a_p0_kept, a + 1)
                if s == 1:
                    pe.wait_ge(a_p1_kept, 2 * layer + kind + 1)
                for h in range(H):
                    for t in range(nk):
                        ins = mm(ps[:, 2, 64 * h:64 * h + 64], a_pT[:, t, h, :], v[t][:, h * nh // H, :],
                                 start=(t == 0), stop=(t == nk - 1))
                ins.then_inc(a_out, 1)

            def out_project(layer):
                spread_gate(layer, 0)
                for i in range(KT // 2):
                    key = ("w_out", layer, i, 0)
                    wait_page(pe, key)
                    b = page(key).rearrange("p (k n) -> p k n", k=2)
                    for s in range(NS):
                        for half in range(2):
                            for k in range(2):
                                kt = 2 * i + k
                                ins = mm(ps[:, 4 + 2 * s + half, :], hT[:, kt, P * s:P * s + P],
                                         b[:, k, HALF * half:HALF * half + HALF], start=(kt == 0), stop=(kt == KT - 1))
                    ins.then_inc(w_out_used, 1)
                spread_gate(layer, 1)

            def gate_up(gp, up, k, bank, done):
                for w, o in ((gp, 0), (up, 256)):
                    wv = w.rearrange("p (k n) -> p k n", k=KT)
                    for kt in range(KT):
                        ins = mm(ps[:, bank, o:o + 256], wv[:, kt, P * k:P * k + P], hT[:, kt, :],
                                 start=(kt == 0), stop=(kt == KT - 1))
                ins.then_inc(done, 1)

            def down(dp, k, hid, blk, n_blocks, done):
                dv = dp.rearrange("p (b n) -> p b n", b=2)
                for s in range(NS):
                    for half in range(2):
                        ins = mm(ps[:, 2 * s + half, :], hid[:, P * s:P * s + P],
                                 dv[:, k, HALF * half:HALF * half + HALF], start=(blk == 0), stop=(blk == n_blocks - 1))
                ins.then_inc(done, 1)

            def dense(layer):
                pe.wait_ge(h_ready, 2 * layer + 2)
                pe.wait_ge(h_ready_act, 2 * layer + 2)
                for blk in range(DENSE_BLOCKS + 1):
                    if blk < DENSE_BLOCKS:
                        u, k = blk // FF, blk % FF
                        if k == 0:
                            wait_page(pe, ("gate", layer, u, 0))
                            wait_page(pe, ("up", layer, u, 0))
                        if blk >= 4:
                            pe.wait_ge(hid_ready, blk - 3)
                        gate_up(page(("gate", layer, u, 0)), page(("up", layer, u, 0)), k, 4 + blk % 4, gu_done)
                    if blk:
                        u, k = (blk - 1) // FF, (blk - 1) % FF
                        if k == 0:
                            wait_page(pe, ("down", layer, u, 0))
                        pe.wait_ge(hid_ready, blk)
                        down(page(("down", layer, u, 0)), k, f_hid[:, (blk - 1) % 4], blk - 1, DENSE_BLOCKS, down_done)

            def route():
                pe.wait_ge(params_in, 16 * (N_PARAMS * L + 1))
                pe.wait_ge(h_ready, 2 * L)
                pe.wait_ge(h_ready_act, 2 * L)
                for s in range(NS):
                    for kt in range(KT):
                        ins = mm(ps[:, 4, E * s:E * s + E], hT[:, kt, P * s:P * s + P], router[:, kt, :],
                                 start=(kt == 0), stop=(kt == KT - 1))
                ins.then_inc(logits_done, 1)
                for s in range(NS):
                    for kt in range(KT):
                        ins = turn(ps[:, 2 * s + kt // 4, P * (kt % 4):P * (kt % 4) + P], hT[:, kt, P * s:P * s + P], ident)
                ins.then_inc(h_back, 1)
                pe.wait_ge(route_ready, 1)
                after, before = scan[:, 0, :], scan[:, 1, :]
                m0, m1 = moe_m[:, 0, 0:E], moe_m[:, 1, 0:E]
                for o, terms in ((0, [(before, m0)]), (E, [(before, m1), (after, m0), (before, m0)]),
                                 (2 * E, [(after, m0), (before, m0), (after, m1), (before, m1)])):
                    for k, (tri, m) in enumerate(terms):
                        ins = mm(ps[:, 5, o:o + E], tri, m, start=(k == 0), stop=(k == len(terms) - 1))
                ins.then_inc(places_done, 1)
                pe.wait_ge(h_rows_act, 1)
                pe.wait_ge(h_rows_dve, 1)
                pe.wait_ge(sel_ready, 1)
                gather()

            def gather():
                for kt in range(KT):
                    for s in range(NS):
                        ins = mm(ps[:, 2 + kt // 4, P * (kt % 4):P * (kt % 4) + CAP], row[:, s, P * kt:P * kt + P],
                                 sel[:, s, :], start=(s == 0), stop=(s == NS - 1))
                ins.then_inc(gather_done, 1)

            def scatter(s):
                for half in range(2):
                    ins = mm(ps[:, 2 + half, :], sel_wT[:, s, :], e_y[:, HALF * half:HALF * half + HALF],
                             start=True, stop=True)
                ins.then_inc(scatter_done, 1)

            def experts():
                def wait_expert_page(e, j):
                    pe.wait_ge(loaded[j % MOE_SLOTS],
                               e * (16 * LOADS) + 16 * (loads_before_moe[j % MOE_SLOTS] + j // MOE_SLOTS + 1))

                def gate_up_pair(u, kt, g):
                    j, k = 6 * u + 2 * (kt // (KT // 2)), kt % (KT // 2)
                    a, b = moe_at[j % MOE_SLOTS], moe_at[(j + 1) % MOE_SLOTS]
                    off = 512 * k + P * g
                    return arena[:, a:a + 2 * (b - a)].rearrange("p (two n) -> p two n", two=2)[:, :, off:off + P]

                def tile_gate_up(e, u, t, tiles):
                    i = TILES * u + t
                    pe.wait_ge(hid_ready, e * MOE_TILES + (DENSE_BLOCKS + i - 2))
                    for kt in range(KT):
                        for g in range(4):
                            ins = mm(ps[32 * g:32 * g + 32, 4 + i % 3, 0:256], e_h[:, kt, 32 * t:32 * t + 32],
                                     gate_up_pair(u, kt, g), start=(kt == 0), stop=(kt == KT - 1))
                    ins.then_inc(gu_done, steps_of(t, tiles))

                def turn_hidden(e, u, tiles):
                    pe.wait_ge(hid_ready, e * MOE_TILES + (DENSE_BLOCKS + TILES * (u + 1)))
                    for t in range(tiles):
                        ins = turn(ps[:, 7, P * t:P * t + P], e_hid[:, u % 2, t, :], ident)
                    ins.then_inc(hid_turned, 1)

                def unit_down(e, u, tiles):
                    pe.wait_ge(hidT_ready, e * UNITS + (u + 1))
                    wait_expert_page(e, 6 * u + 4)
                    wait_expert_page(e, 6 * u + 5)
                    pairs = 2 if tiles < TILES else 1
                    n = 32 * tiles
                    for g0 in range(0, 4, pairs):
                        for half in range(2):
                            for g in range(g0, g0 + pairs):
                                at = moe_at[(6 * u + 4 + g // 2) % MOE_SLOTS] + D * (g % 2) + HALF * half
                                row0 = FEW * (g - g0)
                                ins = mm(ps[row0:row0 + n, half, :], e_hidT[:, g, 0:n], arena[:, at:at + HALF],
                                         start=(u == 0 and g0 == 0), stop=(u == UNITS - 1 and g0 + pairs == 4))
                    ins.then_inc(down_done, 1)

                def expert(e, tiles):
                    for u in range(UNITS):
                        for j in range(4):
                            wait_expert_page(e, 6 * u + j)
                        tile_gate_up(e, u, 0, tiles)
                        if u:
                            turn_hidden(e, u - 1, tiles)
                        else:
                            pe.wait_ge(y_copied_act, e + 1)
                            pe.wait_ge(y_copied_dve, e + 1)
                            scatter(0)
                        tile_gate_up(e, u, 1, tiles)
                        if u:
                            unit_down(e, u - 1, tiles)
                        else:
                            pe.wait_ge(y_added, e * 2 + 2)
                            scatter(1)
                        for t in range(2, tiles):
                            tile_gate_up(e, u, t, tiles)
                        if u == 3:
                            pe.wait_ge(sel_w_ready, e + 1)
                            pe.wait_ge(y_added, e * 2 + 3)
                            for s in range(NS):
                                ins = turn(ps[:, 2, P * s:P * s + P], sel_w[:, s, :], ident)
                            ins.then_inc(sel_w_turned, 1)
                    pe.wait_ge(sel_ready, e + 2)
                    pe.wait_ge(sel_wT_ready, e + 2)
                    gather()
                    turn_hidden(e, UNITS - 1, tiles)
                    unit_down(e, UNITS - 1, tiles)

                with pe.Fori(0, E) as e:
                    pe.wait_ge(gathered_act, e + 1)
                    pe.wait_ge(gathered_dve, e + 1)
                    few_or_all(pe, e, lambda tiles: expert(e, tiles))
                pe.wait_ge(y_copied_act, E + 1)
                pe.wait_ge(y_copied_dve, E + 1)
                pe.wait_ge(gathered_act, E + 1)
                pe.wait_ge(gathered_dve, E + 1)
                scatter(0)
                pe.wait_ge(y_added, 2 * E + 2)
                scatter(1)

            def spill():
                pe.wait_ge(y_added, 2 * E + 3)
                with spill_if_any(pe):
                    pe.sem_inc(spill_down, 1)
                    pe.sem_inc(spill_gu, 1)
                    with pe.Fori(0, E) as e:
                        count = pe.value_load(moe_count[0:1, bass.ds(e, 1)], min_val=0, max_val=NS * P)
                        with pe.If(count > CAP):
                            for blk in range(SPILL_BLOCKS):
                                u, k = blk // FF, blk % FF
                                at = PAGE * 3 * (u % 2)
                                if k == 0:
                                    pe.wait_ge(spill_loaded[u % 2], e * (24 * SPILL_UNITS) + 48 * (u // 2 + 1))
                                if blk == 0:
                                    pe.wait_ge(spill_y, e * 2 + 1)
                                gate_up(arena[:, at:at + PAGE], arena[:, at + PAGE:at + 2 * PAGE], k, 4 + blk % 2, spill_gu)
                                pe.wait_ge(spill_hid, e * SPILL_BLOCKS + (blk + 2))
                                down(arena[:, at + 2 * PAGE:at + 3 * PAGE], k, s_hid, blk, SPILL_BLOCKS, spill_down)
                        with pe.Else():
                            pe.wait_ge(spill_down, e * SPILL_BLOCKS + 1)
                            pe.sem_inc(spill_gu, SPILL_BLOCKS)
                            pe.sem_inc(spill_down, SPILL_BLOCKS)

            pe.wait_ge(const_set, 6)
            pe.wait_ge(cond_ready, 1)
            for layer in range(L):
                if layer == 0:
                    mod_steps(0, 0, KT + 1)
                    pe.wait_ge(const_in, 16)
                    mod_turn(0)
                norm_turn(2 * layer)
                project(layer)
                pe.wait_ge(params_in, 16 * (N_PARAMS * (layer + 1) + 1))
                pe.wait_ge(proj_act, (IN_PAGES + 1) // 2 * (layer + 1))
                pe.wait_ge(proj_dve, IN_PAGES // 2 * (layer + 1))
                pe.wait_ge(tables_in, 16)
                pe.wait_ge(pick_ready, 2 * 4)
                for s in range(NS):
                    n = NS * layer + s
                    gla(layer, s)
                    retention_scores(layer, s)
                    mla_turn(layer, s)
                    retention_out(layer, s)
                    mla_up(layer, s)
                    attention(layer, s, 0)
                    attention(layer, s, 1)
                    if s == 0:
                        mod_steps(3 * layer + 2, 0, 2)
                    pe.wait_ge(a_mixed, 2 * n + 2)
                    for kt in range(KT):
                        ins = turn(ps[:, kt // 4, P * (kt % 4):P * (kt % 4) + P], mixed[:, P * kt:P * kt + P], ident)
                    ins.then_inc(mix_turned, 1)
                    pe.wait_ge(mix_kept, n + 1)
                    pe.wait_ge(mix_kept_act, n + 1)
                out_project(layer)
                norm_turn(2 * layer + 1)
                if layer % 2 == 0:
                    dense(layer)
                else:
                    route()
                    experts()
                    spill()

        @block.scalar
        def _(act):
            a_ = nc.scalar
            steps = [0]

            def link(ins):
                steps[0] += 1
                ins.then_inc(act_step, 1)
                act.wait_ge(act_step, steps[0])

            def keep_hidden_turned(n, tiles):
                act.wait_ge(hid_turned, n)
                a_.copy(e_hidT[:, :, 0:32 * tiles].rearrange("p g (t n) -> p t g n", t=tiles),
                        ps[:, 7, 0:tiles * P].rearrange("p (t g n) -> p t g n", t=tiles, g=4)).then_inc(hidT_ready, 1)

            def keep_mod_rows(i):
                act.wait_ge(mod_used, KT * (i + 1))
                act.wait_ge(mod_bias_used, i + 1)
                for q in range(4):
                    gate = 2 * (i % 3) + q // 2 in (2, 5)
                    ins = a_.copy(mod_row[32 * q:32 * q + 2, int(gate), :], ps[32 * q:32 * q + 2, 7, :])
                ins.then_inc(mod_rows, 1)

            def keep_mod(i):
                act.wait_ge(mod_turned, i + 1)
                turned = ps[:, 7, :].rearrange("p (j q n) -> p q j n", j=4, q=4)
                for part, w in {0: ((0, 0), (1, 1)), 1: ((1, 2),), 2: ((0, 3),)}[i % 3]:
                    ins = a_.copy(mod_T[:, w].rearrange("p (h j) s -> p h j s", h=2),
                                  turned[:, 2 * part:2 * part + 2, :, 0:NS])
                ins.then_inc(mod_kept, 1)

            def keep_gate(layer, g):
                act.wait_ge(gate_spread, 2 * layer + g + 1)
                a_.copy(gates[:, g].rearrange("p s n -> p (s n)"), ps[:, 0:4, :].rearrange("p b n -> p (b n)"))\
                    .then_inc(gate_kept, 1)

            def norm_squares(m, between=None):
                for s in range(NS):
                    if s and between:
                        between()
                    if m:
                        act.wait_ge((x0_mixed, x_mixed)[s], m)
                    else:
                        act.wait_ge(x_in, 32)
                    a_.activation(row[:, s, :], x[:, s, :], ACT.Square, accum_out=stat[:, s:s + 1]).then_inc(sq_ready, 1)

            def norm_spread(m):
                act.wait_ge(xT_done, NS * m + 2)
                act.wait_ge(scale_ready, m + 1)
                w = m % 2
                for kt in range(KT):
                    ins = a_.activation(hT[:, kt, P:2 * P], ps[:, 2 + kt // 4, P * (kt % 4):P * (kt % 4) + P], ACT.Identity,
                                        bias=mod_T[:, 2 * w, kt, 1:2], scale=scale_A[:, w, kt, 1:2])
                ins.then_inc(h_ready_act, 1)

            def o_post(k, gate, s):
                act.wait_ge(o_kept, k + 1)
                a_.activation(o_sq, o_sum, ACT.Square).then_inc(o_sq_ready, 1)
                a_.activation(o_gate, pj(s, gate), ACT.Exp, scale=-1.0).then_inc(o_gate_exp, 1)

            act.wait_ge(cond_in, 32)
            a_.activation(cond[:], cond_raw[:], ACT.Silu).then_inc(cond_ready, 1)
            for layer in range(L):
                norm_squares(2 * layer)
                if layer == 0:
                    act.wait_ge(const_set, 1)
                    keep_mod_rows(0)
                    keep_mod(0)
                act.wait_ge(mod_kept, 3 * layer + 1)
                norm_spread(2 * layer)
                act.wait_ge(gains_in, 48 * (layer + 1))
                link(a_.activation(lg_abs[:], decay[:], ACT.Abs))
                link(a_.activation(lg_abs[:], lg_abs[:], ACT.Exp, scale=-1.0))
                a_.activation(lg_abs[:], lg_abs[:], ACT.Ln, bias=1.0).then_inc(ret_exp, 1)
                act.wait_ge(ret_lg, layer + 1)
                act.wait_ge(tables_in, 16)
                for k in range(4):
                    a_.activation(ret_pow[:, k, :], lg[:, H * (k % 2):H * (k % 2) + H], ACT.Exp,
                                  scale=c("pos")[:, k:k + 1]).then_inc(ret_ready, 1)
                act.wait_ge(ret_dist, layer + 1)
                a_.activation(ret_D[:], ret_D[:], ACT.Exp).then_inc(ret_ready, 1)
                for i in range(0, IN_PAGES, 2):
                    w = min(256, IN_WIDTH - 256 * i)
                    act.wait_ge(w_in_used, IN_PAGES * layer + i + 1)
                    a_.copy(proj[:, :, 256 * i:256 * i + w],
                            ps[:, 4 + i % 4, :].rearrange("p (s n) -> p s n", s=NS)[:, :, 0:w]).then_inc(proj_act, 1)
                act.wait_ge(proj_dve, IN_PAGES // 2 * (layer + 1))
                act.wait_ge(proj_act, (IN_PAGES + 1) // 2 * (layer + 1))
                for s in range(NS):
                    n = NS * layer + s
                    link(a_.activation(m_q, pj(s, "mcq"), ACT.Square, accum_out=stat[:, 16:17]))
                    a_.activation(m_q[:, 0:P], pj(s, "mckv"), ACT.Square, accum_out=stat[:, 17:18]).then_inc(m_sq, 1)
                    act.wait_ge(lr_done, n + 1)
                    link(a_.activation(g_abs, ps[:, 1, 0:256], ACT.Abs))
                    link(a_.activation(g_abs, g_abs, ACT.Exp, scale=-1.0))
                    a_.activation(g_abs, g_abs, ACT.Ln, bias=1.0).then_inc(lr_soft, 1)
                    if s == 1:
                        keep_mod_rows(3 * layer + 2)
                    act.wait_ge(sums_done, n + 1)
                    a_.activation(g_x.rearrange("p l t -> p (l t)"), ps[:, 2:6, :].rearrange("p b n -> p (b n)"),
                                  ACT.Exp).then_inc(decays_ready, 1)
                    if s == 1:
                        keep_mod(3 * layer + 2)
                    for r in range(2):
                        act.wait_ge(g_turned, 2 * n + r + 1)
                        if r:
                            act.wait_ge(g_att_done, 2 * n + 1)
                        a_.copy(g_qT.rearrange("p l t -> p (l t)"), ps[:, 0, :]).then_inc(g_q_kept, 1)
                    if s == 1:
                        act.wait_ge(ext_turned, layer + 1)
                        a_.copy(g_sT.rearrange("p l t -> p (l t)"), ps[:, 0, 0:256]).then_inc(ext_kept, 1)
                    act.wait_ge(r_turned, n + 1)
                    a_.copy(r_qT[0:64].rearrange("p l t -> p (l t)"), ps[0:64, 0, :]).then_inc(r_q_kept, 1)
                    if s == 0:
                        act.wait_ge(g_out_done, n + 1)
                        a_.copy(g_st.rearrange("p l t -> p (l t)"), ps[:, 5, :]).then_inc(g_state_kept, 1)
                    o_post(2 * n, "gog", s)
                    if s == 0:
                        act.wait_ge(r_out_done, n + 1)
                        a_.copy(r_st[0:64].rearrange("p l t -> p (l t)"), ps[0:64, 3, :]).then_inc(r_state_kept, 1)
                    act.wait_ge(m_up_done, n + 1)
                    a_.copy(a_q.rearrange("p h d -> p (h d)"), ps[:, 1, 0:384]).then_inc(m_q_kept, 1)
                    o_post(2 * n + 1, "rg", s)
                    for kind in range(2):
                        a = 2 * n + kind
                        dk, scale = ((96, 96 ** -0.5), (64, 64 ** -0.5))[kind]
                        act.wait_ge(a_turned, a + 1)
                        a_.copy(a_qT[0:dk].rearrange("p l t -> p (l t)"), ps[0:dk, 0, :]).then_inc(a_q_kept, 1)
                        act.wait_ge(a_shift, a + 1)
                        for h in range(H):
                            o = 256 * (h % 2)
                            ins = a_.activation(a_p[:, h, 0:P * (1 + s)], ps[:, 3 + h // 2, o:o + P * (1 + s)], ACT.Exp,
                                                bias=stat[:, 24 + h:25 + h], scale=scale,
                                                accum_out=stat[:, 28 + h:29 + h])
                        if kind == 1:
                            ins = a_.activation(stat[:, 36:40], stat[:, 32:36], ACT.Exp)
                        ins.then_inc(a_probs, 1)
                        third = 3 * layer + (1, 3)[s]
                        if kind == 1 and third < 3 * L:
                            keep_mod(third)
                        act.wait_ge(a_p_turned, a + 1)
                        a_.copy(a_pT[:, 0].rearrange("p l t -> p (l t)"), ps[:, 5, :]).then_inc(a_p0_kept, 1)
                        if kind == 0 and third < 3 * L:
                            keep_mod_rows(third)
                    act.wait_ge(mix_turned, n + 1)
                    a_.copy(hT[:, 0:4, P * s:P * s + P], ps[:, 0, :].rearrange("p (k t) -> p k t", k=4)).then_inc(mix_kept_act, 1)
                keep_gate(layer, 0)
                act.wait_ge(stored, 16 * stores_per_layer * (layer + 1))
                norm_squares(2 * layer + 1, lambda: keep_gate(layer, 1))
                norm_spread(2 * layer + 1)
                if layer % 2 == 0:
                    for blk in range(DENSE_BLOCKS):
                        act.wait_ge(gu_done, blk + 1)
                        if blk >= 2:
                            act.wait_ge(hid_ready, blk - 1)
                        a_.activation(f_sg[:, blk % 2, :], ps[:, 4 + blk % 4, 0:256], ACT.Silu).then_inc(silu_ready, 1)
                else:
                    act.wait_ge(route_top, 1)
                    a_.activation(stat[:, 50:52], stat[:, 48:50], ACT.Exp).then_inc(route_exp, 1)
                    act.wait_ge(h_back, 1)
                    a_.copy(row[:, 0, :], ps[:, 0:2, :].rearrange("p b n -> p (b n)")).then_inc(h_rows_act, 1)

                    def keep_gathered():
                        a_.copy(e_h[:, 0:4, :], ps[:, 2, :].rearrange("p (k n) -> p k n", k=4)[:, :, 0:CAP])\
                            .then_inc(gathered_act, 1)

                    def expert(e, tiles):
                        for u in range(UNITS):
                            for t in range(tiles):
                                i = TILES * u + t
                                act.wait_ge(gu_done, e * MOE_TILES + (DENSE_BLOCKS + i + 1))
                                act.wait_ge(hid_ready, e * MOE_TILES + (DENSE_BLOCKS + i - 2))
                                a_.activation(e_sg[:, i % 3, :], ps[:, 4 + i % 3, 0:P], ACT.Silu)\
                                    .then_inc(silu_ready, steps_of(t, tiles))
                                if t == 0 and u:
                                    keep_hidden_turned(e * UNITS + u, tiles)
                        act.wait_ge(gather_done, e + 2)
                        keep_gathered()
                        keep_hidden_turned(e * UNITS + UNITS, tiles)
                        act.wait_ge(down_done, e * UNITS + (DENSE_BLOCKS + UNITS))
                        a_.copy(e_y[0:y_rows(tiles), 0:HALF], ps[0:y_rows(tiles), 0, :]).then_inc(y_copied_act, 1)

                    act.wait_ge(gather_done, 1)
                    keep_gathered()
                    act.wait_ge(y_kept, 1)
                    act.sem_inc(y_copied_act, 1)
                    with act.Fori(0, E) as e:
                        few_or_all(act, e, lambda tiles: expert(e, tiles))
                    act.wait_ge(y_added, 2 * E + 3)
                    with spill_if_any(act):
                        act.sem_inc(spill_silu, 1)
                        with act.Fori(0, E) as e:
                            count = act.value_load(moe_count[0:1, bass.ds(e, 1)], min_val=0, max_val=NS * P)
                            with act.If(count > CAP):
                                for blk in range(SPILL_BLOCKS):
                                    act.wait_ge(spill_gu, e * SPILL_BLOCKS + (blk + 2))
                                    act.wait_ge(spill_hid, e * SPILL_BLOCKS + (blk + 1))
                                    a_.activation(s_sg, ps[:, 4 + blk % 2, 0:256], ACT.Silu).then_inc(spill_silu, 1)
                            with act.Else():
                                act.wait_ge(spill_silu, e * SPILL_BLOCKS + 1)
                                act.sem_inc(spill_silu, SPILL_BLOCKS)
            norm_squares(2 * L)

        @block.vector
        def _(dve):
            v = nc.vector
            steps = [0]

            def link(ins):
                steps[0] += 1
                ins.then_inc(dve_step, 1)
                dve.wait_ge(dve_step, steps[0])

            def norm_rows(m):
                for s in range(NS):
                    dve.wait_ge(sq_ready, NS * m + s + 1)
                    v.tensor_scalar(stat[:, 2 + s:3 + s], stat[:, s:s + 1], 1.0 / D, EPS, ALU.mult, ALU.add)\
                        .then_inc(var_ready, 1)
                for s in range(NS):
                    dve.wait_ge(rstd_ready, NS * m + s + 1)
                    v.tensor_scalar(row[:, s, :], x[:, s, :], stat[:, 4 + s:5 + s], None, ALU.mult).then_inc(xn_ready, 1)

            def norm_spread(m):
                dve.wait_ge(xT_done, NS * m + 1)
                w = m % 2
                for kt in range(KT):
                    ins = v.tensor_scalar(hT[:, kt, 0:P], ps[:, kt // 4, P * (kt % 4):P * (kt % 4) + P],
                                          scale_A[:, w, kt, 0:1], mod_T[:, 2 * w, kt, 0:1], ALU.mult, ALU.add)
                ins.then_inc(h_ready, 1)

            def o_post(k, gate, s, col):
                o3, t3, sq3 = heads(o_sum, H), heads(o_tmp, H), heads(o_sq, H)
                dve.wait_ge(o_sq_ready, k + 1)
                link(v.tensor_reduce(stat[:, 8:12], sq3, AX, ALU.add))
                v.tensor_scalar(stat[:, 8:12], stat[:, 8:12], 1.0 / 64, EPS, ALU.mult, ALU.add).then_inc(o_var, 1)
                dve.wait_ge(o_gate_exp, k + 1)
                link(v.tensor_scalar(o_gate, o_gate, 1.0, None, ALU.add))
                link(v.reciprocal(o_gate, o_gate))
                link(v.tensor_tensor(o_gate, o_gate, pj(s, gate), ALU.mult))
                dve.wait_ge(o_rstd, k + 1)
                link(v.tensor_tensor(t3, o3, last(stat[:, 12:16], 64), ALU.mult))
                v.tensor_tensor(mixed[:, col:col + 256], o_tmp, o_gate, ALU.mult).then_inc(o_mixed, 1)

            for layer in range(L):
                norm_rows(2 * layer)
                dve.wait_ge(mod_kept, 3 * layer + 1)
                dve.wait_ge(gains_in, 48 * (layer + 1))
                v.scalar_tensor_tensor(scale_A[:, 0], mod_T[:, 1], 1.0, last(gT[:, 0, :], NS), ALU.add, ALU.mult)\
                    .then_inc(scale_ready, 1)
                dve.wait_ge(scale_ready, 2 * layer + 1)
                norm_spread(2 * layer)
                if layer == 0:
                    dve.wait_ge(const_in, 16)
                    for q in range(4):
                        for s in range(NS):
                            rows = slice(32 * q, 32 * q + 2)
                            v.tensor_copy(pick[rows, s, :], ident[rows, 32 * q + s:32 * q + s + 1].to_broadcast([2, P]))\
                                .then_inc(pick_ready, 1)
                dve.wait_ge(ret_exp, layer + 1)
                v.scalar_tensor_tensor(lg[:], decay[:], 0.0, lg_abs[:], ALU.min, ALU.subtract).then_inc(ret_lg, 1)
                dve.wait_ge(ret_lg, layer + 1)
                dve.wait_ge(tables_in, 16)
                for h in range(H):
                    link(v.tensor_scalar(ret_D[:, h, :], dist[:, 0, :], lg[:, h:h + 1], None, ALU.mult))
                for h in range(H):
                    ins = v.scalar_tensor_tensor(ret_D[:, h, :], dist[:, 1, :], lg[:, H + h:H + h + 1], ret_D[:, h, :],
                                                 ALU.mult, ALU.add)
                    if h < H - 1:
                        link(ins)
                ins.then_inc(ret_dist, 1)
                dve.wait_ge(ret_ready, 5 * (layer + 1))
                link(v.tensor_tensor(ret_D[:], ret_D[:], mid(ident, H), ALU.add))
                for i in range(1, IN_PAGES, 2):
                    w = min(256, IN_WIDTH - 256 * i)
                    dve.wait_ge(w_in_used, IN_PAGES * layer + i + 1)
                    v.tensor_copy(proj[:, :, 256 * i:256 * i + w],
                                  ps[:, 4 + i % 4, :].rearrange("p (s n) -> p s n", s=NS)[:, :, 0:w]).then_inc(proj_dve, 1)
                dve.wait_ge(proj_act, (IN_PAGES + 1) // 2 * (layer + 1))
                dve.wait_ge(proj_dve, IN_PAGES // 2 * (layer + 1))
                dve.wait_ge(params_in, 16 * (N_PARAMS * (layer + 1) + 1))
                for s in range(NS):
                    n = NS * layer + s
                    dve.wait_ge(lr_turned, n + 1)
                    v.tensor_copy(lrT[0:32, :], ps[0:32, 0, 0:P]).then_inc(lr_kept, 1)
                    dve.wait_ge(m_sq, n + 1)
                    link(v.tensor_scalar(stat[:, 18:19], stat[:, 16:17], 1.0 / 256, EPS, ALU.mult, ALU.add))
                    v.tensor_scalar(stat[:, 19:20], stat[:, 17:18], 1.0 / 128, EPS, ALU.mult, ALU.add).then_inc(m_var, 1)
                    dve.wait_ge(lr_soft, n + 1)
                    v.scalar_tensor_tensor(g_la, ps[:, 1, 0:256], 0.0, g_abs, ALU.min, ALU.subtract).then_inc(la_ready, 1)
                    dve.wait_ge(m_rstd, n + 1)
                    if s == 1:
                        dve.wait_ge(stored, 16 * stores_per_layer * (layer + 1))
                    link(v.tensor_scalar(m_q, pj(s, "mcq"), stat[:, 20:21], None, ALU.mult))
                    v.scalar_tensor_tensor(m_ckv, pj(s, "mckv"), stat[:, 21:22], kv_g[:], ALU.mult, ALU.mult)\
                        .then_inc(m_normed, 1)
                    dve.wait_ge(decays_ready, n + 1)
                    gq, gk = pj(s, "gq"), pj(s, "gk")
                    link(v.tensor_scalar(g_d[:, 0, :], gq, 2.0, None, ALU.mult))
                    link(v.tensor_scalar(g_d[:, 1, :], gk, 32 ** -0.5, None, ALU.mult))
                    link(v.tensor_tensor(g_x[:, 0:7, :], g_x[:, 0:7, :], mid(gq, 7), ALU.mult))
                    link(v.tensor_tensor(g_x[:, 8:15, :], g_x[:, 8:15, :], mid(g_d[:, 1, :], 7), ALU.mult))
                    state_side = gq if s == 1 else g_d[:, 1, :]
                    link(v.tensor_tensor(g_x[:, 7, :], g_x[:, 7, :], state_side, ALU.mult))
                    v.tensor_tensor(g_x[:, 15, :], g_x[:, 15, :], state_side, ALU.mult).then_inc(decayed, 1)
                    for r in range(2):
                        dve.wait_ge(g_turned, 2 * n + r + 1)
                        if r:
                            dve.wait_ge(g_att_done, 2 * n + 1)
                        v.tensor_copy(g_kT.rearrange("p l t -> p (l t)"), ps[:, 1, :]).then_inc(g_k_kept, 1)
                        dve.wait_ge(g_att_done, 2 * n + r + 1)
                        for j in range(4):
                            level = 4 * r + j
                            mask = masks[:, level, :] if level < LEVELS else ident
                            ins = v.copy_predicated(g_att, mid(mask, H).bitcast(U32), ps[:, 2:6, P * j:P * j + P])
                            if j < 3:
                                link(ins)
                        ins.then_inc(g_att_kept, 1)
                        dve.wait_ge(g_att_kept, 2 * n + r + 1)
                    dve.wait_ge(g_out_done, n + 1)
                    v.tensor_copy(o_sum, ps[:, 6, 0:256]).then_inc(o_kept, 1)
                    dve.wait_ge(r_turned, n + 1)
                    v.tensor_copy(r_kT[0:64].rearrange("p l t -> p (l t)"), ps[0:64, 1, :]).then_inc(r_k_kept, 1)
                    if s == 0:
                        for d in range(2):
                            link(v.scalar_tensor_tensor(heads(r_kd[:, d], H), heads(pj(s, "rk"), H), 0.125,
                                                        last(ret_pow[:, d, :], 64), ALU.mult, ALU.mult))
                    dve.wait_ge(r_scores, n + 1)
                    v.scalar_tensor_tensor(r_att.rearrange("p h t -> p (h t)"), ps[:, 2, :], 0.125,
                                           ret_D[:].rearrange("p h t -> p (h t)"), ALU.mult, ALU.mult)\
                        .then_inc(r_att_kept, 1)
                    dve.wait_ge(m_turned, n + 1)
                    for k in range(2):
                        link(v.tensor_scalar(m_qT[:, k, :], ps[:, 0, P * k:P * k + P], q_g[:, k:k + 1], None, ALU.mult))
                    v.tensor_copy(m_qT[:, 2:3 + s, :].rearrange("p a t -> p (a t)"), ps[:, 0, 2 * P:(3 + s) * P])\
                        .then_inc(m_kept, 1)
                    o_post(2 * n, "gog", s, 0)
                    dve.wait_ge(o_mixed, 2 * n + 1)
                    dve.wait_ge(r_out_done, n + 1)
                    if s == 0:
                        v.tensor_copy(o_sum, ps[:, 6, 0:256]).then_inc(o_kept, 1)
                    else:
                        link(v.tensor_tensor(heads(o_tmp, H), heads(ps[:, 3, 0:256], H), last(ret_pow[:, 2, :], 64), ALU.mult))
                        link(v.tensor_tensor(o_sum, ps[:, 6, 0:256], o_tmp, ALU.add))
                        link(v.tensor_tensor(heads(o_tmp, H), heads(ps[:, 3, 256:512], H), last(ret_pow[:, 3, :], 64), ALU.mult))
                        v.tensor_tensor(o_sum, o_sum, o_tmp, ALU.add).then_inc(o_kept, 1)
                    dve.wait_ge(m_up_done, n + 1)
                    if s == 1:
                        dve.wait_ge(roped, 3 * (layer + 1))
                    for t in range(1 + s):
                        kv = heads(ps[:, 2 + 2 * t, :], H)
                        link(v.tensor_copy(a_k[:, t, :, 0:64], kv[:, :, 0:64]))
                        link(v.tensor_copy(a_v[:, t], kv[:, :, 64:128]))
                        kr = pj(s, "mkr") if t == 0 else ctx_kr[:]
                        ins = v.tensor_copy(a_k[:, t, :, 64:96], mid(kr, H))
                        if s == 1:
                            link(ins)
                    if s == 1:
                        dve.wait_ge(m_q_kept, n + 1)
                        q1, q2 = a_q[:, :, 64:80], a_q[:, :, 80:96]
                        cos, sin = mid(c("cos32"), H), mid(c("sin32"), H)
                        qa, qb, qc, qd = (take(1664 + 64 * k, H, 16) for k in range(4))
                        link(v.tensor_tensor(qa, q1, cos, ALU.mult))
                        link(v.tensor_tensor(qb, q2, sin, ALU.mult))
                        link(v.tensor_tensor(qc, q1, sin, ALU.mult))
                        link(v.tensor_tensor(qd, q2, cos, ALU.mult))
                        link(v.tensor_tensor(q1, qa, qb, ALU.subtract))
                        ins = v.tensor_tensor(q2, qc, qd, ALU.add)
                    ins.then_inc(m_k_kept, 1)
                    for kind in range(2):
                        a = 2 * n + kind
                        dk, nh, scale, col = ((96, H, 96 ** -0.5, 256), (64, 2, 64 ** -0.5, 768))[kind]
                        dve.wait_ge(a_turned, a + 1)
                        for t in range(1 + s):
                            ins = v.tensor_copy(a_kT[0:dk, t, 0:nh, :].rearrange("p h t -> p (h t)"),
                                                ps[0:dk, 1 + t, 0:nh * P])
                            if t < s:
                                link(ins)
                        ins.then_inc(a_k_kept, 1)
                        dve.wait_ge(a_scores, a + 1)
                        sc = ps[:, 3:5, :].rearrange("p b (g k) -> p (b g) k", g=2)[:, :, 0:P * (1 + s)]
                        link(v.tensor_reduce(stat[:, 40:44], sc, AX, ALU.max))
                        if kind == 0:
                            v.tensor_scalar(stat[:, 24:28], stat[:, 40:44], -scale, None, ALU.mult).then_inc(a_shift, 1)
                        else:
                            link(v.scalar_tensor_tensor(stat[:, 40:44], stat[:, 40:44], scale, sink[:], ALU.mult, ALU.max))
                            link(v.tensor_scalar(stat[:, 24:28], stat[:, 40:44], -1.0, None, ALU.mult))
                            v.tensor_tensor(stat[:, 32:36], sink[:], stat[:, 40:44], ALU.subtract).then_inc(a_shift, 1)
                        if kind == 0:
                            o_post(2 * n + 1, "rg", s, 512)
                        if s == 1:
                            dve.wait_ge(a_p_turned, a + 1)
                            v.tensor_copy(a_pT[:, 1].rearrange("p h t -> p (h t)"), ps[:, 6, :]).then_inc(a_p1_kept, 1)
                        dve.wait_ge(a_out, a + 1)
                        if kind == 1:
                            link(v.tensor_tensor(stat[:, 28:32], stat[:, 28:32], stat[:, 36:40], ALU.add))
                        link(v.reciprocal(stat[:, 44:48], stat[:, 28:32]))
                        v.tensor_tensor(heads(mixed[:, col:col + 256], H), heads(ps[:, 2, 0:256], H), last(stat[:, 44:48], 64),
                                        ALU.mult).then_inc(a_mixed, 1)
                    dve.wait_ge(mix_turned, n + 1)
                    v.tensor_copy(hT[:, 4:8, P * s:P * s + P], ps[:, 1, :].rearrange("p (k t) -> p k t", k=4))\
                        .then_inc(mix_kept, 1)

                def add_to_x(y, gate, k):
                    for s in range(NS):
                        link(v.tensor_tensor(row[:, s, :], y[:, D * s:D * s + D], gates[:, gate, s, :], ALU.mult))
                        v.tensor_tensor(x[:, s, :], x[:, s, :], row[:, s, :], ALU.add)\
                            .then_inc((x0_mixed, x_mixed)[s], 1)
                    dve.wait_ge(x0_mixed, k)
                    dve.wait_ge(x_mixed, k)

                dve.wait_ge(mod_kept, 3 * layer + 3)
                v.scalar_tensor_tensor(scale_A[:, 1], mod_T[:, 3], 1.0, last(gT[:, 1, :], NS), ALU.add, ALU.mult)\
                    .then_inc(scale_ready, 1)
                dve.wait_ge(scale_ready, 2 * layer + 2)
                dve.wait_ge(gate_kept, 2 * layer + 1)
                dve.wait_ge(w_out_used, (KT // 2) * (layer + 1))
                dve.wait_ge(stored, 16 * stores_per_layer * (layer + 1))
                add_to_x(ps[:, 4:8, :].rearrange("p b n -> p (b n)"), 0, 2 * layer + 1)
                norm_rows(2 * layer + 1)
                norm_spread(2 * layer + 1)
                if layer % 2 == 0:
                    for blk in range(DENSE_BLOCKS):
                        dve.wait_ge(silu_ready, blk + 1)
                        if blk >= 4:
                            dve.wait_ge(down_done, blk - 3)
                        v.tensor_tensor(f_hid[:, blk % 4, :], f_sg[:, blk % 2, :], ps[:, 4 + blk % 4, 256:512], ALU.mult)\
                            .then_inc(hid_ready, 1)
                    dve.wait_ge(down_done, DENSE_BLOCKS)
                    dve.wait_ge(gate_kept, 2 * layer + 2)
                    add_to_x(ps[:, 0:4, :].rearrange("p b n -> p (b n)"), 1, 2 * layer + 2)
                else:
                    dve.wait_ge(logits_done, 1)
                    link(v.tensor_copy(t_logit.rearrange("p s e -> p (s e)"), ps[:, 4, 0:NS * E]))
                    for s in range(NS):
                        link(v.max(t_top[:, s, :], t_logit[:, s, :]))
                        link(v.max_index(route_i[:, s, :], t_top[:, s, :], t_logit[:, s, :]))
                    link(v.tensor_copy(t_idx, route_i[:]))
                    v.tensor_tensor(stat[:, 48:50], t_top[:, :, 1], t_top[:, :, 0], ALU.subtract).then_inc(route_top, 1)
                    dve.wait_ge(route_exp, 1)
                    link(v.tensor_scalar(stat[:, 52:54], stat[:, 50:52], 1.0, None, ALU.add))
                    link(v.reciprocal(stat[:, 52:54], stat[:, 52:54]))
                    link(v.tensor_tensor(stat[:, 54:56], stat[:, 50:52], stat[:, 52:54], ALU.mult))
                    link(v.memset(moe_m[:], 0.0))
                    link(v.memset(moe_w[:], 0.0))
                    iota = c("iota")
                    for s in range(NS):
                        first, second = t_idx[:, s, 0:1], t_idx[:, s, 1:2]
                        link(v.tensor_scalar(moe_m[:, s, 0:E], iota[:, 0:E], first, None, ALU.is_equal))
                        link(v.tensor_scalar(t_w[:, s, :], iota[:, 0:E], second, None, ALU.is_equal))
                        link(v.tensor_scalar(moe_w[:, s, 0:E], moe_m[:, s, 0:E], stat[:, 52 + s:53 + s], None, ALU.mult))
                        link(v.scalar_tensor_tensor(moe_w[:, s, 0:E], t_w[:, s, :], stat[:, 54 + s:55 + s], moe_w[:, s, 0:E],
                                                    ALU.mult, ALU.add))
                    v.tensor_tensor(moe_m[:, :, 0:E], moe_m[:, :, 0:E], t_w, ALU.add).then_inc(route_ready, 1)
                    dve.wait_ge(h_back, 1)
                    v.tensor_copy(row[:, 1, :], ps[:, 2:4, :].rearrange("p b n -> p (b n)")).then_inc(h_rows_dve, 1)
                    dve.wait_ge(places_done, 1)
                    link(v.memset(moe_pos[:], 0.0))
                    link(v.tensor_scalar(moe_pos[:, :, 0:E], ps[:, 5, 0:NS * E].rearrange("p (s e) -> p s e", s=NS),
                                         GLA_GATE_NORM, None, ALU.mult))
                    link(v.tensor_tensor(moe_pos[:, 1, 0:E], moe_pos[:, 1, 0:E], moe_m[:, 0, 0:E], ALU.add))
                    link(v.scalar_tensor_tensor(moe_spill[:], moe_pos[:, :, 0:E], float(CAP), moe_w[:, :, 0:E], ALU.is_ge, ALU.mult))
                    link(v.scalar_tensor_tensor(moe_pos[:], moe_pos[:], 1.0, moe_m[:], ALU.add, ALU.mult))
                    link(v.tensor_scalar(moe_pos[:], moe_pos[:], -1.0, None, ALU.add))
                    link(v.scalar_tensor_tensor(t_count, ps[:, 5, 2 * E:3 * E], GLA_GATE_NORM, moe_m[:, 0, 0:E],
                                                ALU.mult, ALU.add))
                    link(v.tensor_tensor(moe_count[:], t_count[0:1, :], moe_m[0:1, 1, 0:E], ALU.add))
                    link(v.tensor_tensor(t_count[0:1, :], t_count[0:1, :], moe_m[0:1, 1, 0:E], ALU.add))
                    link(v.tensor_reduce(stat[0:1, 61:62], t_count[0:1, :], AX, ALU.max))
                    link(v.tensor_tensor(moe_most[:], stat[0:1, 61:62], moe_m[0:1, 0, E:E + 1], ALU.add))

                    def select(e):
                        for s in range(NS):
                            ins = v.tensor_scalar(sel[:, s, :], iota[:, 0:CAP], moe_pos[:, s, bass.ds(e, 1)], None,
                                                  ALU.is_equal)
                        ins.then_inc(sel_ready, 1)

                    def keep_gathered():
                        v.tensor_copy(e_h[:, 4:8, :], ps[:, 3, :].rearrange("p (k n) -> p k n", k=4)[:, :, 0:CAP])\
                            .then_inc(gathered_dve, 1)

                    def expert(e, tiles):
                        for u in range(UNITS):
                            for t in range(tiles):
                                i = TILES * u + t
                                dve.wait_ge(silu_ready, e * MOE_TILES + (DENSE_BLOCKS + i + 1))
                                v.tensor_tensor(e_hid[:, u % 2, t, :], e_sg[:, i % 3, :], ps[:, 4 + i % 3, P:2 * P], ALU.mult)\
                                    .then_inc(hid_ready, steps_of(t, tiles))
                                if u == 0 and t < NS:
                                    dve.wait_ge(scatter_done, e * 2 + (t + 1))
                                    dve.wait_ge(y_added, e * 2 + (t + 1))
                                    v.tensor_tensor(f_y[:, t, :], ps[:, 2:4, :].rearrange("p b n -> p (b n)"), f_y[:, t, :],
                                                    ALU.add).then_inc(y_added, 1)
                            if u == 1:
                                for s in range(NS):
                                    for lo in range(0, y_rows(tiles), 32 * tiles):
                                        ins = v.tensor_scalar(sel_w[:, s, lo:lo + 32 * tiles], iota[:, 0:32 * tiles],
                                                              moe_pos[:, s, bass.ds(e, 1)], moe_w[:, s, bass.ds(e, 1)],
                                                              ALU.is_equal, ALU.mult)
                                if tiles == TILES:
                                    ins = v.memset(sel_w[:, :, CAP:P], 0.0)
                                ins.then_inc(sel_w_ready, 1)
                            if u == 4:
                                dve.wait_ge(sel_w_turned, e + 1)
                                v.tensor_copy(sel_wT, ps[:, 2, 0:NS * P].rearrange("p (s n) -> p s n", s=NS))\
                                    .then_inc(sel_wT_ready, 1)
                                select(e + 1)
                        dve.wait_ge(gather_done, e + 2)
                        keep_gathered()
                        dve.wait_ge(down_done, e * UNITS + (DENSE_BLOCKS + UNITS))
                        v.tensor_copy(e_y[0:y_rows(tiles), HALF:D], ps[0:y_rows(tiles), 1, :]).then_inc(y_copied_dve, 1)

                    select(0)
                    link(v.memset(sel_wT, 0.0))
                    v.memset(f_y, 0.0).then_inc(y_added, 1)
                    dve.wait_ge(gather_done, 1)
                    keep_gathered()
                    link(v.memset(e_y, 0.0))
                    v.memset(stat[:, 60:61], 0.0).then_inc(y_kept, 1)
                    dve.sem_inc(y_copied_dve, 1)
                    dve.sem_inc(sel_wT_ready, 1)
                    with dve.Fori(0, E) as e:
                        few_or_all(dve, e, lambda tiles: expert(e, tiles))
                    for s in range(NS):
                        dve.wait_ge(scatter_done, 2 * E + s + 1)
                        dve.wait_ge(y_added, 2 * E + s + 1)
                        v.tensor_tensor(f_y[:, s, :], ps[:, 2:4, :].rearrange("p b n -> p (b n)"), f_y[:, s, :],
                                        ALU.add).then_inc(y_added, 1)
                    dve.wait_ge(y_added, 2 * E + 3)
                    with spill_if_any(dve):
                        dve.sem_inc(spill_hid, 1)
                        dve.sem_inc(spill_y, 1)
                        with dve.Fori(0, E) as e:
                            count = dve.value_load(moe_count[0:1, bass.ds(e, 1)], min_val=0, max_val=NS * P)
                            with dve.If(count > CAP):
                                for blk in range(SPILL_BLOCKS):
                                    dve.wait_ge(spill_silu, e * SPILL_BLOCKS + (blk + 2))
                                    dve.wait_ge(spill_down, e * SPILL_BLOCKS + (blk + 1))
                                    v.tensor_tensor(s_hid, s_sg, ps[:, 4 + blk % 2, 256:512], ALU.mult).then_inc(spill_hid, 1)
                                dve.wait_ge(spill_down, e * SPILL_BLOCKS + (SPILL_BLOCKS + 1))
                                dve.wait_ge(spill_y, e * 2 + 1)
                                for s in range(NS):
                                    v.scalar_tensor_tensor(f_y[:, s, :], ps[:, 2 * s:2 * s + 2, :].rearrange("p b n -> p (b n)"),
                                                           moe_spill[:, s, bass.ds(e, 1)], f_y[:, s, :], ALU.mult, ALU.add)\
                                        .then_inc(spill_y, 1)
                            with dve.Else():
                                dve.wait_ge(spill_hid, e * SPILL_BLOCKS + 1)
                                dve.wait_ge(spill_y, e * 2 + 1)
                                dve.sem_inc(spill_hid, SPILL_BLOCKS)
                                dve.sem_inc(spill_y, 2)
                        dve.wait_ge(spill_y, 2 * E + 1)
                    dve.wait_ge(gate_kept, 2 * layer + 2)
                    add_to_x(f_y.rearrange("p s n -> p (s n)"), 1, 2 * layer + 2)
            dve.wait_ge(final_g_in, 16)
            for s in range(NS):
                dve.wait_ge(sq_ready, 2 * NS * L + s + 1)
                v.tensor_scalar(stat[:, 2 + s:3 + s], stat[:, s:s + 1], 1.0 / D, EPS, ALU.mult, ALU.add).then_inc(var_ready, 1)
            for s in range(NS):
                dve.wait_ge(rstd_ready, 2 * NS * L + s + 1)
                v.scalar_tensor_tensor(row[:, s, :], x[:, s, :], stat[:, 4 + s:5 + s], final_g, ALU.mult, ALU.mult)\
                    .then_inc(final_ready, 1)


_OUTS = ["y_prompt", "y_sample", "new_state_gla", "new_state_ret", "new_cache_mla_ckv", "new_cache_mla_krope",
         "new_cache_gqa_k", "new_cache_gqa_v"]


def kernel(**inputs):
    import concourse.bacc as bacc
    from concourse.bass_utils import run_bass_kernel_spmd as run

    nc = bacc.Bacc("TRN2", target_bir_lowering=False, num_devices=1)
    arrays, io = {}, {}
    for name, a in list(inputs.items()) + [("constants", constant_table())]:
        a = np.ascontiguousarray(a)
        arrays[f"in_{name}"] = a
        io[name] = nc.dram_tensor(f"in_{name}", a.shape, mybir.dt.from_np(a.dtype), kind="ExternalInput").ap()
    b, t, d = inputs["x_prompt"].shape
    depth = inputs["w_in"].shape[0]
    shapes = dict(
        y_prompt=(b, t, d), y_sample=inputs["x_sample"].shape,
        new_state_gla=(b,) + inputs["state_gla"].shape[1:], new_state_ret=(b,) + inputs["state_ret"].shape[1:],
        new_cache_mla_ckv=(b, depth, t, inputs["cache_mla_ckv"].shape[-1]),
        new_cache_mla_krope=(b, depth, t, inputs["cache_mla_krope"].shape[-1]),
        new_cache_gqa_k=(b, depth, inputs["cache_gqa_k"].shape[2], t, inputs["cache_gqa_k"].shape[-1]),
        new_cache_gqa_v=(b, depth, inputs["cache_gqa_v"].shape[2], t, inputs["cache_gqa_v"].shape[-1]))
    for name in _OUTS:
        io[name] = nc.dram_tensor(f"out_{name}", shapes[name], F32, kind="ExternalOutput").ap()
    hybrid_step(nc, io)
    r = run(nc, [arrays], core_ids=[0])
    return tuple(r.results[0][f"out_{name}"] for name in _OUTS)
```
